# Optimizing a Trainium2 kernel written in Bass

```python
import math
import jax, jax.numpy as jnp
from jax import lax
import numpy as np

D_MODEL = 1024
BATCH = 1
SEQ = 256
DEPTH = 1

N_MEM = 256
EPS = 1e-6
NEG = -1e30

A_HEADS = 16
A_HEAD_DIM = 64
A_WIDTH = A_HEADS * A_HEAD_DIM
MOBA_BLOCK = 256
MOBA_TOPK = 3
MOBA_Q_CHUNK = 32
ROPE_THETA = 10000.0

B_HEADS = 8
B_KEY_DIM = 128
B_VAL_DIM = D_MODEL // B_HEADS
B_KEY_WIDTH = B_HEADS * B_KEY_DIM
B_VAL_WIDTH = B_HEADS * B_VAL_DIM
HGRN_CHUNK = 64

X_HEADS = 4
X_HEAD_DIM = D_MODEL // X_HEADS

FFN_HIDDEN = ((8 * D_MODEL + 3 * 256 - 1) // (3 * 256)) * 256

IN_WIDTHS = (A_WIDTH, A_WIDTH, A_WIDTH, B_KEY_WIDTH, B_KEY_WIDTH, B_VAL_WIDTH, B_VAL_WIDTH, D_MODEL, D_MODEL)
IN_WIDTH = A_WIDTH * 3 + B_KEY_WIDTH * 2 + B_VAL_WIDTH * 2 + D_MODEL * 2


def rmsnorm(x, g):
    xf = x.astype(jnp.float32)
    y = xf * lax.rsqrt(jnp.mean(xf * xf, axis=-1, keepdims=True) + EPS)
    return (y * g.astype(jnp.float32)).astype(x.dtype)

def rope(t, pos):
    hd = t.shape[-1]
    inv_freq = jnp.power(ROPE_THETA, -jnp.arange(0, hd, 2, dtype=jnp.float32) / hd)
    ang = pos.astype(jnp.float32)[:, None, :, None] * inv_freq
    cos, sin = jnp.cos(ang), jnp.sin(ang)
    tf = t.astype(jnp.float32)
    t1, t2 = tf[..., : hd // 2], tf[..., hd // 2:]
    return jnp.concatenate([t1 * cos - t2 * sin, t2 * cos + t1 * sin], axis=-1).astype(t.dtype)

def split_cols(z):
    outs, off = [], 0
    for w in IN_WIDTHS:
        outs.append(z[..., off:off + w])
        off += w
    return outs

def moba_attention(q, k, v, pos):
    B, S, _ = q.shape
    H, hd, BLK, QC = A_HEADS, A_HEAD_DIM, MOBA_BLOCK, MOBA_Q_CHUNK
    scale = hd ** -0.5

    def heads(t):
        return t.reshape(B, S, H, hd).transpose(0, 2, 1, 3)

    q = rope(heads(q), pos)
    k = rope(heads(k), pos)
    v = heads(v)
    nb = -(-S // BLK)
    s_pad = nb * BLK
    padw = [(0, 0), (0, 0), (0, s_pad - S), (0, 0)]
    q, k, v = jnp.pad(q, padw), jnp.pad(k, padw), jnp.pad(v, padw)
    kb = k.reshape(B, H, nb, BLK, hd)
    vb = v.reshape(B, H, nb, BLK, hd)

    k_mean = jnp.mean(kb.astype(jnp.float32), axis=3)
    gate = jnp.einsum('bhsd,bhnd->bhsn', q.astype(jnp.float32), k_mean)
    q_blk = jnp.arange(s_pad) // BLK
    past = jnp.arange(nb)[None, :] < q_blk[:, None]
    gate = jnp.where(past, gate, NEG)
    n_sel = min(MOBA_TOPK, nb)
    _, idx = lax.top_k(gate, n_sel)
    valid = idx < q_blk[:, None]

    n_chunks = s_pad // QC

    def to_chunks(t):
        return jnp.moveaxis(t.reshape(B, H, n_chunks, QC, t.shape[-1]), 2, 0)

    starts = jnp.arange(n_chunks, dtype=jnp.int32) * QC
    bi = jnp.arange(B)[:, None, None, None]
    hi = jnp.arange(H)[None, :, None, None]

    def attend(args):
        qc, ic, vmask, start = args
        blk = start // BLK
        k_own = lax.dynamic_index_in_dim(kb, blk, axis=2, keepdims=False)
        v_own = lax.dynamic_index_in_dim(vb, blk, axis=2, keepdims=False)
        q_pos = start + jnp.arange(QC)
        k_pos = blk * BLK + jnp.arange(BLK)
        s_own = jnp.einsum('bhqd,bhkd->bhqk', qc, k_own).astype(jnp.float32) * scale
        s_own = jnp.where(k_pos[None, :] <= q_pos[:, None], s_own, NEG)
        k_sel = kb[bi, hi, ic]
        v_sel = vb[bi, hi, ic]
        s_sel = jnp.einsum('bhqd,bhqjkd->bhqjk', qc, k_sel).astype(jnp.float32) * scale
        s_sel = jnp.where(vmask[..., None], s_sel, NEG).reshape(B, H, QC, n_sel * BLK)
        p = jax.nn.softmax(jnp.concatenate([s_sel, s_own], axis=-1), axis=-1).astype(v.dtype)
        p_sel = p[..., : n_sel * BLK].reshape(B, H, QC, n_sel, BLK)
        p_own = p[..., n_sel * BLK:]
        return (jnp.einsum('bhqjk,bhqjkd->bhqd', p_sel, v_sel)
                + jnp.einsum('bhqk,bhkd->bhqd', p_own, v_own))

    o = lax.map(attend, (to_chunks(q), to_chunks(idx), to_chunks(valid), starts))
    o = jnp.moveaxis(o, 0, 2).reshape(B, H, s_pad, hd)[:, :, :S]
    return o.transpose(0, 2, 1, 3).reshape(B, S, H * hd)

def hgrn2(q, f, i, og, lb, norm_g):
    B, S, _ = q.shape
    H, dk, dv, C = B_HEADS, B_KEY_DIM, B_VAL_DIM, HGRN_CHUNK
    nc = S // C

    def heads(t, d):
        return t.reshape(B, S, H, d).transpose(0, 2, 1, 3).astype(jnp.float32)

    qh = jax.nn.silu(heads(q, dk)) * (dk ** -0.5)
    lbh = lb.astype(jnp.float32).reshape(1, H, 1, dk)
    fg = lbh + (1.0 - lbh) * jax.nn.sigmoid(heads(f, dk))
    logf = jnp.log(fg)
    kh = 1.0 - fg
    vh = heads(i, dv)

    def to_chunks(t):
        return jnp.moveaxis(t.reshape(B, H, nc, C, t.shape[-1]), 2, 0)

    causal = jnp.tril(jnp.ones((C, C), dtype=bool))[:, :, None]

    def step(state, xs):
        qc, kc, vc, gc = xs
        b = jnp.cumsum(gc, axis=2)
        o_inter = jnp.einsum('bhtd,bhdv->bhtv', qc * jnp.exp(b), state)
        diff = b[:, :, :, None, :] - b[:, :, None, :, :]
        decay = jnp.where(causal, jnp.exp(jnp.where(causal, diff, 0.0)), 0.0)
        a = jnp.einsum('bhtd,bhsd,bhtsd->bhts', qc, kc, decay)
        o = o_inter + jnp.einsum('bhts,bhsv->bhtv', a, vc)
        b_last = b[:, :, -1:, :]
        new_state = (jnp.exp(b_last[:, :, 0, :])[..., None] * state
                     + jnp.einsum('bhsd,bhsv->bhdv', kc * jnp.exp(b_last - b), vc))
        return new_state, o

    s0 = jnp.zeros((B, H, dk, dv), jnp.float32)
    _, o = lax.scan(step, s0, (to_chunks(qh), to_chunks(kh), to_chunks(vh), to_chunks(logf)))
    o = jnp.moveaxis(o, 0, 2).reshape(B, H, S, dv).transpose(0, 2, 1, 3)
    o = o * lax.rsqrt(jnp.mean(o * o, axis=-1, keepdims=True) + EPS)
    o = o.reshape(B, S, H * dv) * norm_g.astype(jnp.float32)
    o = o * jax.nn.silu(og.astype(jnp.float32))
    return o.astype(q.dtype)

def memory_cross_attention(h, mem, wq, wkv, wo):
    B, S, _ = h.shape
    M = mem.shape[1]
    q = (h @ wq).reshape(B, S, X_HEADS, X_HEAD_DIM)
    kv = mem @ wkv
    k = kv[..., :D_MODEL].reshape(B, M, X_HEADS, X_HEAD_DIM)
    v = kv[..., D_MODEL:].reshape(B, M, X_HEADS, X_HEAD_DIM)
    s = jnp.einsum('bshd,bmhd->bhsm', q, k).astype(jnp.float32) * (X_HEAD_DIM ** -0.5)
    p = jax.nn.softmax(s, axis=-1).astype(v.dtype)
    o = jnp.einsum('bhsm,bmhd->bshd', p, v).reshape(B, S, D_MODEL)
    return o @ wo

def first_inputs(seed: int = 0) -> dict:
    key = jax.random.key(seed)
    ks = jax.random.split(key, 24)
    f32 = jnp.float32

    def w(k, shape, fan_in):
        return jax.random.normal(k, shape, f32) * (fan_in ** -0.5)

    def gain(k, shape):
        return 1.0 + 0.02 * jax.random.normal(k, shape, f32)

    x = jax.random.normal(ks[0], (BATCH, SEQ, D_MODEL), f32)
    mem = jax.random.normal(ks[1], (BATCH, N_MEM, D_MODEL), f32)
    offs = jax.random.randint(ks[2], (BATCH, 1), 0, 1024, dtype=jnp.int32)
    positions = offs + jnp.arange(SEQ, dtype=jnp.int32)[None, :]
    return {
        "x": x,
        "mem": mem,
        "positions": positions,
        "norm_mix_g": gain(ks[3], (DEPTH, D_MODEL)),
        "w_in": w(ks[4], (DEPTH, D_MODEL, IN_WIDTH), D_MODEL),
        "hgrn_lb_logits": 0.5 * jax.random.normal(ks[5], (DEPTH + 1, B_KEY_WIDTH), f32),
        "hgrn_norm_g": gain(ks[6], (DEPTH, B_VAL_WIDTH)),
        "w_br_attn": w(ks[7], (DEPTH, A_WIDTH, D_MODEL), A_WIDTH),
        "w_br_hgrn": w(ks[8], (DEPTH, B_VAL_WIDTH, D_MODEL), B_VAL_WIDTH),
        "w_out": w(ks[9], (DEPTH, D_MODEL, D_MODEL), D_MODEL),
        "norm_x_g": gain(ks[10], (DEPTH, D_MODEL)),
        "norm_mem_g": gain(ks[11], (DEPTH, D_MODEL)),
        "wq_x": w(ks[12], (DEPTH, D_MODEL, D_MODEL), D_MODEL),
        "wkv_x": w(ks[13], (DEPTH, D_MODEL, 2 * D_MODEL), D_MODEL),
        "wo_x": w(ks[14], (DEPTH, D_MODEL, D_MODEL), D_MODEL),
        "norm_ffn_g": gain(ks[15], (DEPTH, D_MODEL)),
        "w_ffn_in": w(ks[16], (DEPTH, D_MODEL, 2 * FFN_HIDDEN), D_MODEL),
        "w_ffn_out": w(ks[17], (DEPTH, FFN_HIDDEN, D_MODEL), FFN_HIDDEN),
        "final_norm_g": gain(ks[18], (D_MODEL,)),
    }

def first_block(x, mem, positions, norm_mix_g, w_in, hgrn_lb_logits, hgrn_norm_g, w_br_attn,
              w_br_hgrn, w_out, norm_x_g, norm_mem_g, wq_x, wkv_x, wo_x, norm_ffn_g,
              w_ffn_in, w_ffn_out, final_norm_g):
    lb_all = jnp.cumsum(jax.nn.softmax(hgrn_lb_logits.astype(jnp.float32), axis=0), axis=0)
    h = x
    for l in range(DEPTH):
        xn = rmsnorm(h, norm_mix_g[l])
        q_a, k_a, v_a, q_b, f_b, i_b, og_b, g_a, g_b = split_cols(xn @ w_in[l])
        y_a = moba_attention(q_a, k_a, v_a, positions) @ w_br_attn[l]
        y_b = hgrn2(q_b, f_b, i_b, og_b, lb_all[l], hgrn_norm_g[l]) @ w_br_hgrn[l]
        merged = jax.nn.sigmoid(g_a) * y_a + jax.nn.sigmoid(g_b) * y_b
        h = h + merged @ w_out[l]
        h = h + memory_cross_attention(rmsnorm(h, norm_x_g[l]), rmsnorm(mem, norm_mem_g[l]),
                                       wq_x[l], wkv_x[l], wo_x[l])
        hn = rmsnorm(h, norm_ffn_g[l])
        gu = hn @ w_ffn_in[l]
        h = h + (jax.nn.silu(gu[..., :FFN_HIDDEN]) * gu[..., FFN_HIDDEN:]) @ w_ffn_out[l]
    return rmsnorm(h, final_norm_g)


DEPTH_2 = 2

CTX_LEN = 256
GRID_W = 64
N_MIXERS = 2
N_LAYERS_A = (DEPTH_2 + 1) // 2
N_LAYERS_B = DEPTH_2 // 2
BRANCH_WIDTH = D_MODEL
DA_HEAD_DIM = 64
DA_HEADS = BRANCH_WIDTH // (2 * DA_HEAD_DIM)
DA_QK_WIDTH = DA_HEADS * 2 * DA_HEAD_DIM
DA_IN_WIDTH = 2 * DA_QK_WIDTH + 2 * BRANCH_WIDTH
GQ_HEAD_DIM = 128
GQ_HEADS = BRANCH_WIDTH // GQ_HEAD_DIM
GQ_KV_HEADS = 2
GQ_Q_WIDTH = GQ_HEADS * GQ_HEAD_DIM
GQ_KV_WIDTH = GQ_KV_HEADS * GQ_HEAD_DIM
GQ_IN_WIDTH = GQ_Q_WIDTH + 2 * GQ_KV_WIDTH + BRANCH_WIDTH
Q_BLOCK = 128
NORM_EPS = 1e-6


def rms_norm(x, g):
    xf = x.astype(jnp.float32)
    y = xf * lax.rsqrt(jnp.mean(xf * xf, axis=-1, keepdims=True) + NORM_EPS)
    return (y * g.astype(jnp.float32)).astype(x.dtype)

def adaln(cvec, w, b):
    m = jax.nn.silu(cvec) @ w + b
    return jnp.split(m, 3, axis=-1)

def axial_rope_tables(rows, cols, head_dim):
    axis_dim = head_dim // 2
    freqs = ROPE_THETA ** (-jnp.arange(0, axis_dim, 2, dtype=jnp.float32) / axis_dim)
    ang = jnp.concatenate([rows.astype(jnp.float32)[:, None] * freqs,
                           cols.astype(jnp.float32)[:, None] * freqs], axis=-1)
    return jnp.cos(ang), jnp.sin(ang)

def apply_rope(x, cos, sin):
    S, half = cos.shape
    shp = (1, S) + (1,) * (x.ndim - 3) + (half,)
    cs = cos.reshape(shp).astype(x.dtype)
    sn = sin.reshape(shp).astype(x.dtype)
    x1, x2 = jnp.split(x, 2, axis=-1)
    return jnp.concatenate([x1 * cs - x2 * sn, x2 * cs + x1 * sn], axis=-1)

def sweep_attention(q, k, v):
    B, Sq, Hq, Dh = q.shape
    Hkv = k.shape[2]
    G = Hq // Hkv
    Dv = v.shape[-1]
    scale = Dh ** -0.5
    k32 = k.astype(jnp.float32)
    qb = q.reshape(B, Sq // Q_BLOCK, Q_BLOCK, Hkv, G, Dh).transpose(1, 0, 2, 3, 4, 5)

    def one_block(qblk):
        s = jnp.einsum('bqhgd,bkhd->bhgqk', qblk.astype(jnp.float32), k32) * scale
        p = jax.nn.softmax(s, axis=-1)
        return jnp.einsum('bhgqk,bkhd->bqhgd', p.astype(v.dtype), v)

    out = lax.map(one_block, qb)
    return out.transpose(1, 0, 2, 3, 4, 5).reshape(B, Sq, Hq, Dv)

def lambda_init_fn(layer_idx):
    return 0.8 - 0.6 * math.exp(-0.3 * layer_idx)

def diff_attention_mixer(h, hc, w_in, w_out, lam_p, subln_g, lam_init, cos, sin, with_ctx_out):
    B, S, _ = h.shape

    def project(t):
        L = t.shape[1]
        p = t @ w_in
        q, k, v, z = jnp.split(p, [DA_QK_WIDTH, 2 * DA_QK_WIDTH, 2 * DA_QK_WIDTH + BRANCH_WIDTH], axis=-1)
        q = q.reshape(B, L, DA_HEADS, 2, DA_HEAD_DIM)
        k = k.reshape(B, L, DA_HEADS, 2, DA_HEAD_DIM)
        v = v.reshape(B, L, DA_HEADS, 2 * DA_HEAD_DIM)
        return q, k, v, z

    q, k, v, z = project(h)
    qc, kc, vc, zc = project(hc)
    q = apply_rope(q, cos, sin)
    k = apply_rope(k, cos, sin)
    k_all = jnp.concatenate([k, kc], axis=1)
    v_all = jnp.concatenate([v, vc], axis=1)

    lp = lam_p.astype(jnp.float32)
    lam = jnp.exp(jnp.sum(lp[0] * lp[1])) - jnp.exp(jnp.sum(lp[2] * lp[3])) + lam_init

    def diff(qq, kk, vv, gate):
        o1 = sweep_attention(qq[..., 0, :], kk[..., 0, :], vv)
        o2 = sweep_attention(qq[..., 1, :], kk[..., 1, :], vv)
        o = o1 - lam.astype(o1.dtype) * o2
        o = rms_norm(o, subln_g) * (1.0 - lam_init)
        o = o.reshape(o.shape[0], o.shape[1], BRANCH_WIDTH)
        return (o * jax.nn.silu(gate)) @ w_out

    y = diff(q, k_all, v_all, z)
    yc = diff(qc, kc, vc, zc) if with_ctx_out else None
    return y, yc

def gqa_mixer(h, hc, w_in, w_out, qk_g, cos, sin, with_ctx_out):
    B, S, _ = h.shape

    def project(t):
        L = t.shape[1]
        p = t @ w_in
        q, k, v, z = jnp.split(p, [GQ_Q_WIDTH, GQ_Q_WIDTH + GQ_KV_WIDTH, GQ_Q_WIDTH + 2 * GQ_KV_WIDTH], axis=-1)
        q = rms_norm(q.reshape(B, L, GQ_HEADS, GQ_HEAD_DIM), qk_g[0])
        k = rms_norm(k.reshape(B, L, GQ_KV_HEADS, GQ_HEAD_DIM), qk_g[1])
        v = v.reshape(B, L, GQ_KV_HEADS, GQ_HEAD_DIM)
        return q, k, v, z

    q, k, v, z = project(h)
    qc, kc, vc, zc = project(hc)
    q = apply_rope(q, cos, sin)
    k = apply_rope(k, cos, sin)
    k_all = jnp.concatenate([k, kc], axis=1)
    v_all = jnp.concatenate([v, vc], axis=1)

    def attend(qq, kk, vv, gate):
        o = sweep_attention(qq, kk, vv)
        o = o.reshape(o.shape[0], o.shape[1], BRANCH_WIDTH)
        return (o * jax.nn.silu(gate)) @ w_out

    y = attend(q, k_all, v_all, z)
    yc = attend(qc, kc, vc, zc) if with_ctx_out else None
    return y, yc

def second_inputs(seed: int = 0) -> dict:
    key = jax.random.key(seed)
    ks = jax.random.split(key, 16)
    f32 = jnp.float32
    D = D_MODEL
    s_in = D ** -0.5
    return {
        "x": jax.random.normal(ks[0], (BATCH, SEQ, D), f32),
        "c": jax.random.normal(ks[1], (BATCH, D), f32),
        "ctx": jax.random.normal(ks[2], (BATCH, CTX_LEN, D), f32),
        "c_ctx": jax.random.normal(ks[3], (D,), f32),
        "ada_w": jax.random.normal(ks[4], (DEPTH_2, D, 3 * D), f32) * (0.5 * s_in),
        "ada_b": jax.random.normal(ks[5], (DEPTH_2, 3 * D), f32) * 0.01,
        "pre_g": 1.0 + 0.05 * jax.random.normal(ks[6], (DEPTH_2, D), f32),
        "post_g": 1.0 + 0.05 * jax.random.normal(ks[7], (DEPTH_2, D), f32),
        "w_out": jax.random.normal(ks[8], (DEPTH_2, BRANCH_WIDTH, D), f32) * (BRANCH_WIDTH ** -0.5),
        "a_w_in": jax.random.normal(ks[9], (N_LAYERS_A, D, DA_IN_WIDTH), f32) * s_in,
        "a_lambda": jax.random.normal(ks[10], (N_LAYERS_A, 4, DA_HEAD_DIM), f32) * 0.1,
        "a_subln_g": 1.0 + 0.05 * jax.random.normal(ks[11], (N_LAYERS_A, 2 * DA_HEAD_DIM), f32),
        "b_w_in": jax.random.normal(ks[12], (N_LAYERS_B, D, GQ_IN_WIDTH), f32) * s_in,
        "b_qk_g": 1.0 + 0.05 * jax.random.normal(ks[13], (N_LAYERS_B, 2, GQ_HEAD_DIM), f32),
    }

def second_block(x, c, ctx, c_ctx, ada_w, ada_b, pre_g, post_g, w_out, a_w_in, a_lambda, a_subln_g, b_w_in, b_qk_g):
    n_tokens = x.shape[1]
    n_rows = n_tokens // GRID_W
    rows = jnp.repeat(jnp.arange(n_rows, dtype=jnp.int32), GRID_W)
    cols = jnp.tile(jnp.arange(GRID_W, dtype=jnp.int32), n_rows)
    cos_a, sin_a = axial_rope_tables(rows, cols, DA_HEAD_DIM)
    cos_b, sin_b = axial_rope_tables(rows, cols, GQ_HEAD_DIM)

    xc = ctx
    for i in range(DEPTH_2):
        last = i == DEPTH_2 - 1
        shift, scale, gate = adaln(c, ada_w[i], ada_b[i])
        shift, scale, gate = shift[:, None, :], scale[:, None, :], gate[:, None, :]
        cshift, cscale, cgate = adaln(c_ctx, ada_w[i], ada_b[i])
        h = rms_norm(x, pre_g[i]) * (1.0 + scale) + shift
        hc = rms_norm(xc, pre_g[i]) * (1.0 + cscale) + cshift
        j = i // N_MIXERS
        if i % N_MIXERS == 0:
            y, yc = diff_attention_mixer(h, hc, a_w_in[j], w_out[i], a_lambda[j], a_subln_g[j],
                                         lambda_init_fn(i), cos_a, sin_a, not last)
        else:
            y, yc = gqa_mixer(h, hc, b_w_in[j], w_out[i], b_qk_g[j], cos_b, sin_b, not last)
        x = x + gate * rms_norm(y, post_g[i])
        if not last:
            xc = xc + cgate * rms_norm(yc, post_g[i])
    return x


def setup_inputs(seed=0):
    out = dict(first_inputs(seed))
    for name, value in second_inputs(seed + 1).items():
        if name != "x":
            out[name + "_2"] = value
    return out


def reference(
    x, mem, positions, norm_mix_g, w_in, hgrn_lb_logits, hgrn_norm_g, w_br_attn, w_br_hgrn,
    w_out, norm_x_g, norm_mem_g, wq_x, wkv_x, wo_x, norm_ffn_g, w_ffn_in, w_ffn_out,
    final_norm_g, c_2, ctx_2, c_ctx_2, ada_w_2, ada_b_2, pre_g_2, post_g_2, w_out_2, a_w_in_2,
    a_lambda_2, a_subln_g_2, b_w_in_2, b_qk_g_2,
):
    x = first_block(
        x, mem, positions, norm_mix_g, w_in, hgrn_lb_logits, hgrn_norm_g, w_br_attn, w_br_hgrn,
        w_out, norm_x_g, norm_mem_g, wq_x, wkv_x, wo_x, norm_ffn_g, w_ffn_in, w_ffn_out,
        final_norm_g,
    )
    return second_block(
        x, c_2, ctx_2, c_ctx_2, ada_w_2, ada_b_2, pre_g_2, post_g_2, w_out_2, a_w_in_2,
        a_lambda_2, a_subln_g_2, b_w_in_2, b_qk_g_2,
    )


_drawn_inputs = setup_inputs


def setup_inputs(seed=0):
    import zlib

    import numpy as np

    out = dict(_drawn_inputs(seed))
    spreads = {}
    factors = {'norm_mix_g': 5.298,
     'hgrn_lb_logits': 2.695,
     'hgrn_norm_g': 7.691,
     'norm_x_g': 8.0,
     'norm_mem_g': 8.0,
     'norm_ffn_g': 3.948,
     'final_norm_g': 2.808,
     'ada_b_2': 2.678,
     'post_g_2': 2.721,
     'a_subln_g_2': 3.35,
     'b_qk_g_2': 8.0}
    for name, (base, spread) in spreads.items():
        noise = np.random.default_rng([zlib.crc32(name.encode()), seed]).standard_normal(out[name].shape)
        drawn = base * np.exp(spread * noise) if base else spread * noise
        out[name] = __import__('jax').numpy.asarray(drawn.astype(out[name].dtype))
    for name, factor in factors.items():
        out[name] = (out[name] * factor).astype(out[name].dtype)
    return out
```

```python
import math
from contextlib import ExitStack

import numpy as np

import concourse.bass as bass
from concourse import mybir

F32 = mybir.dt.float32
F32R = mybir.dt.float32r
I32 = mybir.dt.int32
U32 = mybir.dt.uint32
ALU = mybir.AluOpType
ACT = mybir.ActivationFunctionType
AX_X = mybir.AxisListType.X

P = 128
T = 256
D = 1024
DT = D // P
EPS = 1e-6
NEG = -1e30
FFN = 2816
FT = FFN // P
A_HEADS, A_HD = 16, 64
B_HEADS = 8
X_HEADS, X_HD = 4, 256
DA_HEADS, DA_HD = 8, 64
GQ_HEADS, GQ_KV, GQ_HD = 8, 2, 128
LAM_INIT = 0.8 - 0.6 * math.exp(-0.3 * 0)
LEVELS = 7
TWO_PI = 2 * math.pi
PI_A = 6.28125
PI_B = float(np.float32(int((TWO_PI - PI_A) * 2 ** 20) / 2 ** 20))
PI_C = TWO_PI - PI_A - PI_B
ROUND = 1.5 * 2 ** 23
PI_F = 3.1415925

COLS = {}
_at = 0
for _name, _n in [("norm_mix", 8), ("hgrn", 8), ("norm_x", 8), ("norm_mem", 8), ("norm_ffn", 8),
                  ("final", 8), ("pre0", 8), ("pre1", 8), ("post0", 8), ("post1", 8), ("c", 8), ("c_ctx", 8),
                  ("ada_b", 48), ("subln", 1), ("qk_g", 2), ("lb", 16), ("lam", 4), ("invfreq", 1)]:
    COLS[_name] = (_at, _n)
    _at += _n
NCOLS = _at

RAW, HL, LOOK = 8, 4, 3
NLIN = 3


def program(nc, dram, out_dram):
    ctx = ExitStack()
    with ctx:
        base = 16512
        SLAB = DT * T * 4
        at = [base]

        def place(name, shape, dt=F32, offset=None):
            n = int(np.prod(shape[1:])) * 4
            if offset is None:
                offset = at[0]
                at[0] += (n + 31) // 32 * 32
            return nc.alloc_sbuf_tensor_at(name, shape, dt, offset=offset)

        raw = place("w_raw", [P, RAW, DT * P])
        w_hi = place("w_hi", [P, HL, DT * P], F32R)
        w_lo = place("w_lo", [P, HL, DT * P], F32R)
        slab0 = at[0]
        at[0] += 14 * SLAB

        def slab(name, i, shape, dt=F32, extra=0):
            return place(name, [P] + shape, dt, slab0 + i * SLAB + extra)

        probs = place("probs", [P, 4, 512])
        probsT = place("probsT", [P, 2, 512])
        rot = place("rot", [P, 2, 512])
        rstd = place("rstd", [P, 2, 512])
        head_sq = place("head_sq", [P, 512])
        ident = place("ident", [P, P])
        ones = place("ones", [P, P])
        causal = place("causal", [P, 2 * P])
        hmask = place("hmask", [P, 8, P], U32)
        hmask_at = at[0] - 8 * P * 4
        tab2 = place("tab2", [P, 4, T], F32, hmask_at)
        cs1 = place("cs1", [P, 2, T])
        cols = place("cols", [P, NCOLS])
        ada = place("ada", [P, 48, 2])
        silu_c = place("silu_c", [P, DT, 2])
        stat = place("stat", [P, 3, 4, 2])
        lbt = place("lbt", [P, 4, 8])
        lamt = place("lamt", [P, 6])
        coef = place("coef", [P, 4, 8])
        assert at[0] <= 229368, at[0]

        xT = slab("xT", 0, [DT, T])
        XH, XL = slab("XH", 1, [DT, T], F32R), slab("XL", 2, [DT, T], F32R)
        Q, K = slab("Q", 3, [DT, T]), slab("K", 4, [DT, T])
        V = slab("V", 5, [2, D])
        qb, fb, og = slab("qb", 6, [DT, T]), slab("fb", 7, [DT, T]), slab("og", 9, [DT, T])
        ib = slab("ib", 8, [2, D])
        ga, gb = slab("ga", 10, [DT, T]), slab("gb", 11, [DT, T])
        AH, AL = slab("AH", 12, [DT, T], F32R), slab("AL", 13, [DT, T], F32R)
        tmp3 = slab("tmp3", 3, [DT, T])
        memT = slab("memT", 0, [DT, T])
        MH, ML = slab("MH", 1, [DT, T], F32R), slab("ML", 2, [DT, T], F32R)
        kh = slab("kh", 3, [DT, T])
        decF, decB = slab("decF", 4, [4, T]), slab("decB", 4, [4, T], F32, SLAB // 2)
        qk = [slab("qk0", 5, [2, 4, T]), slab("qk1", 12, [2, 4, T])]
        KX, VX = slab("KX", 13, [DT, T]), slab("VX", 0, [2, D])
        HH, HLo = slab("HH", 7, [DT, T], F32R), slab("HLo", 8, [DT, T], F32R)
        GH, GL = slab("GH", 1, [DT, T], F32R), slab("GL", 2, [DT, T], F32R)
        hres = slab("hres", 3, [DT, T])
        tmp4 = slab("tmp4", 4, [DT, T])
        NH, NL = slab("NH", 5, [DT, T], F32R), slab("NL", 6, [DT, T], F32R)
        QX = slab("QX", 7, [DT, T])
        CH, CL = slab("CH", 8, [DT, T], F32R), slab("CL", 9, [DT, T], F32R)
        FH, FL = slab("FH", 7, [FT, T], F32R), slab("FL", 10, [FT, T], F32R)
        X2, XC = slab("X2", 0, [DT, T]), slab("XC", 1, [DT, T])
        tmp5 = slab("tmp5", 5, [DT, T])
        WH, WL = slab("WH", 6, [DT, 2 * T], F32R), slab("WL", 8, [DT, 2 * T], F32R)
        Q2, K2 = slab("Q2", 10, [DT, 2 * T]), slab("K2", 12, [DT, 2 * T])
        V2 = slab("V2", 2, [4, D])
        ZH, ZL = slab("ZH", 12, [DT, 2 * T], F32R), slab("ZL", 2, [DT, 2 * T], F32R)
        Y2 = slab("Y2", 6, [DT, 2 * T])
        tmp8 = slab("tmp8", 8, [DT, 2 * T])
        QB = slab("QB", 10, [DT, T])
        KB = slab("KB", 11, [GQ_KV, 2 * T])
        VB = slab("VB", 11, [4, GQ_KV * GQ_HD], F32, SLAB // 2)
        BH, BL = slab("BH", 12, [DT, T], F32R), slab("BL", 13, [DT, T], F32R)
        YB = slab("YB", 2, [DT, T])

        def psum(name):
            return ctx.enter_context(nc.psum_tensor(name, [P, 512], F32))

        lin = [psum(f"lin{i}") for i in range(NLIN)]
        sc_bank = [psum("score0"), psum("score1")]
        pt_bank, o_bank, sum_bank = psum("pt_bank"), psum("o_bank"), psum("sum_bank")
        hg_banks = [(sc_bank[0], sc_bank[1]), (pt_bank, o_bank)]

        def sem(name):
            return ctx.enter_context(nc.semaphore(name))

        w_landed = [sem(f"w_landed{i}") for i in range(RAW)]
        w_hi_ready, w_lo_ready = sem("w_hi_ready"), sem("w_lo_ready")
        w_used = sem("w_used")
        ada_used = sem("ada_used")
        lin_out = [sem(f"lin_out{i}") for i in range(NLIN)]
        const_in, x_in, mem_in, x_again, ctx_in, tab_in = (sem(n) for n in
                                                            ("const_in", "x_in", "mem_in", "x_again", "ctx_in", "tab_in"))
        tables = sem("tables")
        tables_act = sem("tables_act")
        tables_pe = sem("tables_pe")
        sq_ready, sum_ready, rstd_ready, norm_out = (sem(n) for n in ("sq_ready", "sum_ready", "rstd_ready", "norm_out"))
        rot_ready, roped = sem("rot_ready"), sem("roped")
        scored, maxed, exped, probs_ready = (sem(n) for n in ("scored", "maxed", "exped", "probs_ready"))
        transposed, pt_ready, pv_done, heads_out = (sem(n) for n in ("transposed", "pt_ready", "pv_done", "heads_out"))
        gates_ready = sem("gates_ready")
        hg_qk, hg_scored, hg_taken, hg_att, hg_pv, hg_out = (sem(n) for n in
                                                             ("hg_qk", "hg_scored", "hg_taken", "hg_att", "hg_pv", "hg_out"))
        gate_used = sem("gate_used")
        dve_chain, act_chain = sem("dve_chain"), sem("act_chain")
        stored = sem("stored")

        def col(name, i=0):
            return cols[:, COLS[name][0] + i:COLS[name][0] + i + 1]

        def colr(name):
            a, n = COLS[name]
            return cols[:, a:a + n]

        steps = []
        tiles = []
        n_lin = [0]
        n_split = [0]
        n_ada = [0]
        n_z = [0]
        rot_uses = []
        stage_last = {}

        def lin_step(stage, t, kts, feat, H, L, width, evac, kind="split"):
            pieces = []
            k = 0
            while k < kts:
                n = min(DT, kts - k)
                tile = {"stage": stage, "t": t, "k": k, "n": n, "kind": kind, "i": len(tiles)}
                if kind == "split":
                    tile["s"] = n_split[0]
                    n_split[0] += 1
                else:
                    tile["a"] = n_ada[0]
                    n_ada[0] += 1
                tiles.append(tile)
                pieces.append(tile)
                k += n
            g = n_lin[0]
            n_lin[0] += 1
            stage_last[stage] = g
            slot = len(rot_uses)
            if evac[0] == "silu":
                rot_uses.append(("lin", g + 1))
            elif evac[0] == "zgate":
                n_z[0] += 1
                rot_uses.append(("z", n_z[0]))
            steps.append(("lin", {"g": g, "pieces": pieces, "feat": feat, "H": H, "L": L, "w": width, "evac": evac,
                                  "t": t, "stage": stage, "pos": n_split[0], "kind": kind, "kts": kts,
                                  "slot": slot, "z": n_z[0]}))

        n_norm = [0]

        def norm_step(src, sq, n_in, width, gate, apply, after_g=None, after=()):
            steps.append(("norm", {"n": n_norm[0], "src": src, "sq": sq, "inv": 1.0 / n_in, "w": width, "apply": apply,
                                   "after_g": after_g, "after": after, "gate": gate, "pos": n_split[0]}))
            n_norm[0] += 1
            return n_norm[0]

        units = []
        combos = []
        groups = []
        n_rope = [0]

        def rope_step(dst, halves, cos, sin, after_g=None, after_n=None):
            steps.append(("rope", {"r": n_rope[0], "dst": dst, "half": halves, "cos": cos, "sin": sin,
                                   "after_g": after_g, "after_n": after_n, "slot": len(rot_uses)}))
            n_rope[0] += 1
            rot_uses.append(("rope", n_rope[0]))

        def ada_some(k):
            for _ in range(k):
                if n_ada[0] < 48:
                    lin_step("ada", n_ada[0], DT, True, silu_c, None, 2, "ada", "ada")

        def attention(new_units, fill):
            todo = []
            for cb in new_units:
                c = len(combos)
                combos.append(cb)
                for j, u in enumerate(cb["units"]):
                    u["u"] = len(units)
                    u["c"] = c
                    units.append(u)
                cb["c"] = c
                cb["o"] = len(groups)
                if cb["last"]:
                    groups.append(cb)
                todo.append(cb)
            flat = [u for cb in todo for u in cb["units"]]
            fed = 0

            def feed(upto):
                nonlocal fed
                while fed < min(upto, len(flat)):
                    steps.append(("score", flat[fed]))
                    fed += 1

            seen = 0
            prev = None
            for cb in todo:
                feed(seen + len(cb["units"]) + (2 if len(cb["units"]) > 1 else 1))
                fill()
                seen += len(cb["units"])
                steps.append(("probs", cb))
                if prev is not None:
                    steps.append(("values", prev))
                    if prev["last"] and prev.get("post"):
                        prev["post"]()
                prev = cb
            steps.append(("values", prev))
            if prev.get("post"):
                prev["post"]()

        def apply_simple(g, tmp, H, L):
            return {"kind": "affine", "a": g, "b": None, "tmp": tmp, "H": H, "L": L}

        steps.append(("setup", {}))
        norm_step(xT[:, :, :], tmp3, D, T, None, apply_simple("norm_mix", tmp3, XH, XL))
        XW = (XH, XL)
        for t in range(8):
            lin_step("q_a", t, DT, True, *XW, T, ("act", Q))
            if t:
                rope_step(Q[:, t - 1, :], 32, cs1[:, 0, :], cs1[:, 1, :], n_lin[0] - 2)
        for t in range(8):
            lin_step("k_a", t, DT, True, *XW, T, ("act", K))
            rope_step(K[:, t - 1, :] if t else Q[:, 7, :], 32, cs1[:, 0, :], cs1[:, 1, :], n_lin[0] - 2)
        for t in range(8):
            lin_step("v_a", t, DT, False, *XW, T, ("tok", V, t))
            if t == 0:
                rope_step(K[:, 7, :], 32, cs1[:, 0, :], cs1[:, 1, :], n_lin[0] - 2)
        roped_a = n_rope[0]

        def head_a(h):
            j, r = h // 2, 64 * (h % 2)
            qh, kk_ = Q[r:r + 64, j, :], K[r:r + 64, j, :]
            u = {"segs": [(0, 128, causal[:, 128:256]), (128, 256, causal[:, :])], "scale": A_HD ** -0.5,
                 "mm": [(0, 128, qh[:, 0:128], kk_[:, 0:128], True, True),
                        (128, 256, qh[:, 128:256], kk_, True, True)],
                 "need_g": stage_last["v_a"], "need_rope": roped_a}
            vh = [V[:, i, h * 64:h * 64 + 64] for i in range(2)]
            return {"units": [u], "blocks": [0, 128, 256], "out": (r, 64),
                    "pv": [(0, 128, vh[0], 0, True, True), (128, 128, vh[0], 1, True, False),
                           (128, 128, vh[1], 2, False, True)],
                    "first": h % 2 == 0, "last": h % 2 == 1,
                    "evac": ("split", [(AH[:, j, :], AL[:, j, :], slice(0, T))])}

        todo = [("q_b", qb, True), ("f_b", fb, True), ("i_b", ib, False), ("og_b", og, True),
                ("g_a", ga, True), ("g_b", gb, True)]
        todo = [(n, t, d, f) for n, d, f in todo for t in range(8)]

        def fill_w():
            for _ in range(3):
                if todo:
                    n, t, dst, feat = todo.pop(0)
                    lin_step(n, t, DT, feat, *XW, T, ("act", dst) if feat else ("tok", dst, t))

        attention([head_a(h) for h in range(A_HEADS)], fill_w)
        while todo:
            fill_w()
        att_a_groups = len(groups)
        steps.append(("gates", {"g": stage_last["g_b"]}))

        norm_step(memT[:, :, :], tmp3, D, T, "mem", apply_simple("norm_mem", tmp3, MH, ML))
        for t in range(8):
            lin_step("br_attn", t, DT, True, AH, AL, T, ("gate_a", None))
        g_br_attn = stage_last["br_attn"]
        steps.append(("hprep", {"g": g_br_attn}))
        kv = [("k_x", t, ("act", KX), True) for t in range(8)] + [("v_x", t, ("tok", VX, t), False) for t in range(8)]
        for grp in range(2):
            for r in range(LEVELS + 2):
                steps.append(("hround", {"grp": grp, "r": r, "i": grp * (LEVELS + 2) + r}))
                if kv:
                    n, t, ev, feat = kv.pop(0)
                    lin_step(n, t, DT, feat, MH, ML, T, ev)
                else:
                    ada_some(3)
            steps.append(("hvalues", {"grp": grp}))
            ada_some(3)
        for pr in range(4):
            norm_step(qb[:, 2 * pr:2 * pr + 2, :], head_sq, P, 512, "hg",
                      {"kind": "hgrn", "pr": pr})
            ada_some(4)
        g_before = n_lin[0] - 1
        for t in range(8):
            lin_step("br_hgrn", t, DT, True, HH, HLo, T, ("gate_b", None))
        for t in range(8):
            lin_step("w_out", t, DT, True, GH, GL, T, ("add", hres))

        norm_step(hres[:, :, :], tmp4, D, T, None, apply_simple("norm_x", tmp4, NH, NL), stage_last["w_out"])
        for t in range(8):
            lin_step("q_x", t, DT, True, NH, NL, T, ("act", QX))

        def head_x(h):
            u = {"segs": [(0, 256, None), (256, 256, None)], "scale": X_HD ** -0.5, "need_g": stage_last["q_x"],
                 "mm": [(s * 256, 256, QX[:, 2 * h + k, s * 128:s * 128 + 128], KX[:, 2 * h + k, :], k == 0, k == 1)
                        for s in range(2) for k in range(2)]}
            pv = []
            for dv in range(2):
                for qt in range(2):
                    for kt in range(2):
                        pv.append((dv * 256 + qt * 128, 128, VX[:, kt, h * 256 + dv * 128:h * 256 + dv * 128 + 128],
                                   qt * 2 + kt, kt == 0, kt == 1))
            return {"units": [u], "blocks": [0, 128, 256, 384], "out": (0, 128), "pv": pv, "first": True, "last": True,
                    "evac": ("split", [(CH[:, 2 * h + dv, :], CL[:, 2 * h + dv, :], slice(dv * 256, dv * 256 + 256))
                                       for dv in range(2)])}

        attention([head_x(h) for h in range(X_HEADS)], lambda: ada_some(3))
        for t in range(8):
            lin_step("wo_x", t, DT, True, CH, CL, T, ("add", hres))

        norm_step(hres[:, :, :], tmp4, D, T, None, apply_simple("norm_ffn", tmp4, NH, NL), stage_last["wo_x"])
        for t in range(FT):
            lin_step("gate", t, DT, True, NH, NL, T, ("silu", None))
            lin_step("up", t, DT, True, NH, NL, T, ("up", None))
        for t in range(8):
            lin_step("ffn_out", t, FT, True, FH, FL, T, ("add", hres))
        norm_step(hres[:, :, :], tmp4, D, T, None, {"kind": "plain", "a": "final", "tmp": tmp4, "dst": X2},
                  stage_last["ffn_out"])

        ada_some(48)
        g_ada = stage_last["ada"]

        def pre_norms(layer):
            for s, src, tm in ((0, X2, tmp4), (1, XC, tmp5)):
                norm_step(src[:, :, :], tm, D, T, "ctx" if s and layer == 0 else None,
                          {"kind": "ada", "layer": layer, "s": s, "tmp": tm, "g_ada": g_ada})

        pre_norms(0)
        for t in range(8):
            lin_step("q_2", t, DT, True, WH, WL, 2 * T, ("act", Q2))
            if t:
                rope_step(Q2[:, t - 1, 0:T], 32, tab2[:, 0, :], tab2[:, 1, :], n_lin[0] - 2)
        for t in range(8):
            lin_step("k_2", t, DT, True, WH, WL, 2 * T, ("act", K2))
            rope_step(K2[:, t - 1, 0:T] if t else Q2[:, 7, 0:T], 32, tab2[:, 0, :], tab2[:, 1, :], n_lin[0] - 2)
        for t in range(8):
            lin_step("v_2", t, DT, False, WH, WL, 2 * T, ("tok", V2, t))
            if t == 0:
                rope_step(K2[:, 7, 0:T], 32, tab2[:, 0, :], tab2[:, 1, :], n_lin[0] - 2)
        roped_2 = n_rope[0]

        def head_da(h):
            made = []
            vh = [V2[:, i, h * 128:h * 128 + 128] for i in range(4)]
            for part in range(3):
                us = []
                for s in range(2):
                    qq = Q2[64 * s:64 * s + 64, h, :]
                    kk_ = K2[64 * s:64 * s + 64, h, :]
                    if part < 2:
                        segs = [(0, 512, None)]
                        mm = [(0, 512, qq[:, part * 128:part * 128 + 128], kk_, True, True)]
                    else:
                        segs = [(0, 256, None), (256, 256, None)]
                        mm = [(i * 256, 256, qq[:, 256 + i * 128:384 + i * 128], kk_[:, 256:512], True, True)
                              for i in range(2)]
                    us.append({"segs": segs, "scale": DA_HD ** -0.5, "mm": mm, "need_g": stage_last["v_2"],
                               "need_rope": roped_2})
                if part < 2:
                    pv = [(part * 128, 128, vh[kt], kt, kt == 0, kt == 3) for kt in range(4)]
                else:
                    pv = [(256 + i * 128, 128, vh[2 + kt], i * 2 + kt, kt == 0, kt == 1)
                          for i in range(2) for kt in range(2)]
                made.append({"units": us, "blocks": [0, 128, 256, 384], "out": (0, 128), "pv": pv,
                             "first": part == 0, "last": part == 2, "evac": ("copy", Q2[:, h, :], 512)})
            made[2]["post"] = lambda: norm_step(Q2[:, h, :], head_sq, P, 512, ("group", made[2]),
                                                {"kind": "head", "dst": Q2[:, h, :], "g": "subln"})
            return made

        attention([c for h in range(DA_HEADS) for c in head_da(h)], lambda: None)
        att_2_groups = len(groups)
        for t in range(8):
            lin_step("z_2", t, DT, True, WH, WL, 2 * T, ("zgate", Q2, ZH, ZL))
        for t in range(8):
            lin_step("w_out0", t, DT, True, ZH, ZL, 2 * T, ("act", Y2))
        for s in range(2):
            norm_step(Y2[:, :, s * T:(s + 1) * T], tmp8[:, :, s * T:(s + 1) * T], D, T, None,
                      {"kind": "post", "layer": 0, "s": s, "tmp": tmp8[:, :, s * T:(s + 1) * T],
                       "y": Y2[:, :, s * T:(s + 1) * T], "res": XC if s else X2}, stage_last["w_out0"])

        n_post0 = n_norm[0]
        pre_norms(1)

        def qk_post(dst, w, gi, g):
            n = norm_step(dst, head_sq, P, w, None, {"kind": "head", "dst": dst, "g": "qk_g", "gi": gi}, g)
            rope_step(dst[:, 0:T], 64, tab2[:, 2, :], tab2[:, 3, :], None, n)

        for t in range(GQ_HEADS):
            lin_step("q_3", t, DT, True, WH[:, :, 0:T], WL[:, :, 0:T], T, ("act", QB))
            if t:
                qk_post(QB[:, t - 1, :], T, 0, n_lin[0] - 2)
        for t in range(GQ_KV):
            lin_step("k_3", t, DT, True, WH, WL, 2 * T, ("act", KB))
            qk_post(KB[:, t - 1, :] if t else QB[:, 7, :], 2 * T if t else T, 1 if t else 0, n_lin[0] - 2)
        for t in range(GQ_KV):
            lin_step("v_3", t, DT, False, WH, WL, 2 * T, ("tok", VB, t))
            if t == 0:
                qk_post(KB[:, 1, :], 2 * T, 1, n_lin[0] - 2)
        roped_3 = n_rope[0]

        def head_gq(h):
            kv_ = h // (GQ_HEADS // GQ_KV)
            made = []
            for part in range(2):
                u = {"segs": [(0, 512, None)], "scale": GQ_HD ** -0.5, "need_g": stage_last["v_3"], "need_rope": roped_3,
                     "mm": [(0, 512, QB[:, h, part * 128:part * 128 + 128], KB[:, kv_, :], True, True)]}
                pv = [(part * 128, 128, VB[:, kt, kv_ * 128:kv_ * 128 + 128], kt, kt == 0, kt == 3) for kt in range(4)]
                made.append({"units": [u], "blocks": [0, 128, 256, 384], "out": (0, 128), "pv": pv,
                             "first": part == 0, "last": part == 1, "evac": ("copy", QB[:, h, :], T)})
            return made

        attention([c for h in range(GQ_HEADS) for c in head_gq(h)], lambda: None)
        for t in range(8):
            lin_step("z_3", t, DT, True, WH[:, :, 0:T], WL[:, :, 0:T], T, ("zgate", QB, BH, BL))
        for t in range(8):
            lin_step("w_out1", t, DT, True, BH, BL, T, ("act", YB))
        norm_step(YB[:, :, :], tmp4, D, T, None, {"kind": "post", "layer": 1, "s": 0, "tmp": tmp4[:, :, :],
                                                 "y": YB[:, :, :], "res": X2}, stage_last["w_out1"])
        total_norms = n_norm[0]
        splits = [t for t in tiles if t["kind"] == "split"]

        done_norms = done_groups = 0
        for kind, s in steps:
            s["norms"], s["groups"] = done_norms, done_groups
            if kind == "norm":
                done_norms += 1
            if kind == "values" and s["last"]:
                done_groups += 1
        w_out_pos = max(s["pos"] for k, s in steps if k == "lin" and s["stage"] == "w_out")

        def after_lin(eng, g):
            for b in range(NLIN):
                uses = len(range(b, g + 1, NLIN))
                if uses:
                    eng.wait_ge(lin_out[b], uses)

        def landed(eng, tile):
            eng.wait_ge(w_landed[tile["i"] % RAW], 16 * (tile["i"] // RAW + 1))

        def rot_free(eng, slot):
            if slot >= 2:
                kind, n = rot_uses[slot - 2]
                if kind == "rope":
                    eng.wait_ge(roped, n)
                elif kind == "z":
                    eng.wait_ge(gate_used, n)
                else:
                    eng.wait_ge(lin_out[n % NLIN], n // NLIN + 1)

        block = ctx.enter_context(nc.Block())

        @block.sync
        def _(sp):
            for name, dst in (("cols", cols[:, :]), ("positions", rot[:, 0, 0:T].bitcast(I32)), ("ident", ident[:, :]),
                              ("ones", ones[:, :]), ("causal", causal[:, :]), ("hmask", hmask[:, :, :])):
                sp.dma_start(dst, dram[name]).then_inc(const_in, 16)
            sp.dma_start(xT[:, :, :], dram["xT"]).then_inc(x_in, 16)

            def load(tile):
                i = tile["i"]
                if i >= RAW:
                    old = tiles[i - RAW]
                    if old["kind"] == "split":
                        sp.wait_ge(w_hi_ready, old["s"] + 1)
                        sp.wait_ge(w_lo_ready, old["s"] + 1)
                    else:
                        sp.wait_ge(ada_used, old["a"] + 1)
                n = tile["n"] * P
                sp.dma_start(raw[:, i % RAW, 0:n], dram[tile["stage"]][tile["t"], :, tile["k"] * P:tile["k"] * P + n])\
                    .then_inc(w_landed[i % RAW], 16)

            for tile in tiles:
                load(tile)
                if tile["stage"] == "q_a" and tile["t"] == 7:
                    sp.wait_ge(norm_out, 1)
                    sp.dma_start(memT[:, :, :], dram["memT"]).then_inc(mem_in, 16)
                if tile["stage"] == "br_hgrn" and tile["t"] == 0:
                    sp.wait_ge(hg_out, 4)
                    sp.dma_start(hres[:, :, :], dram["xT"]).then_inc(x_again, 16)
                    sp.dma_start(tab2[:, :, :], dram["tab2"]).then_inc(tab_in, 16)
                if tile["stage"] == "gate" and tile["t"] == 0:
                    sp.wait_ge(w_used, w_out_pos)
                    sp.dma_start(XC[:, :, :], dram["ctxT"]).then_inc(ctx_in, 16)
            sp.wait_ge(norm_out, total_norms)
            sp.dma_start(out_dram, X2[:, :, :]).then_inc(stored, 16)
            sp.wait_ge(stored, 16)

        @block.tensor
        def _(pe):
            def setup(s):
                pe.wait_ge(const_in, 96)
                pe.wait_ge(tables, 2)
                nc.tensor.matmul(sum_bank[:, 0:2], ones[0:64, :], lamt[0:64, 0:2], start=True, stop=True)\
                    .then_inc(tables_pe, 1)

            def linear(s):
                g = s["g"]
                bank = lin[g % NLIN]
                if g >= NLIN:
                    pe.wait_ge(lin_out[g % NLIN], g // NLIN)
                if s["kind"] == "ada":
                    tile = s["pieces"][0]
                    landed(pe, tile)
                    pe.wait_ge(tables, 5)
                    for k in range(DT):
                        last = nc.tensor.matmul(bank[:, 0:2], raw[:, tile["i"] % RAW, k * P:(k + 1) * P],
                                                silu_c[:, k, :], start=(k == 0), stop=(k == DT - 1))
                    last.then_inc(ada_used, 1)
                    return
                if s["norms"]:
                    pe.wait_ge(norm_out, s["norms"])
                if s["groups"] and s["stage"] in ("br_attn", "wo_x"):
                    pe.wait_ge(heads_out, s["groups"])
                if s["stage"] == "w_out":
                    after_lin(pe, stage_last["br_hgrn"])
                if s["stage"] == "ffn_out":
                    after_lin(pe, stage_last["up"])
                if s["stage"] in ("w_out0", "w_out1"):
                    pe.wait_ge(gate_used, s["z"])
                H, L, W = s["H"], s["L"], s["w"]
                for tile in s["pieces"]:
                    pe.wait_ge(w_hi_ready, tile["s"] + 1)
                    pe.wait_ge(w_lo_ready, tile["s"] + 1)
                    slot = tile["s"] % HL
                    if s["feat"]:
                        for k in range(tile["n"]):
                            wh = w_hi[:, slot, k * P:(k + 1) * P]
                            wl = w_lo[:, slot, k * P:(k + 1) * P]
                            kk = tile["k"] + k
                            first, final = kk == 0, kk == s["kts"] - 1
                            nc.tensor.matmul(bank[:, 0:W], wh, H[:, kk, :], start=first, stop=False)
                            nc.tensor.matmul(bank[:, 0:W], wh, L[:, kk, :], start=False, stop=False)
                            last = nc.tensor.matmul(bank[:, 0:W], wl, H[:, kk, :], start=False, stop=final)
                    else:
                        for tt in range(W // P):
                            o = bank[:, tt * P:(tt + 1) * P]
                            for k in range(DT):
                                wh = w_hi[:, slot, k * P:(k + 1) * P]
                                wl = w_lo[:, slot, k * P:(k + 1) * P]
                                xh, xl = H[:, k, tt * P:(tt + 1) * P], L[:, k, tt * P:(tt + 1) * P]
                                nc.tensor.matmul(o, xh, wh, start=(k == 0), stop=False)
                                nc.tensor.matmul(o, xh, wl, start=False, stop=False)
                                last = nc.tensor.matmul(o, xl, wh, start=False, stop=(k == DT - 1))
                    last.then_inc(w_used, 1)

            def norm(s):
                n = s["n"]
                pe.wait_ge(sq_ready, n + 1)
                if n:
                    pe.wait_ge(rstd_ready, n)
                else:
                    pe.wait_ge(tables_act, 3)
                sq, W = s["sq"], s["w"]
                if len(sq.shape) == 2:
                    last = nc.tensor.matmul(sum_bank[:, 0:W], ones[:, :], sq[:, 0:W], start=True, stop=True)
                else:
                    for k in range(DT):
                        last = nc.tensor.matmul(sum_bank[:, 0:W], ones[:, :], sq[:, k, :], start=(k == 0), stop=(k == DT - 1))
                last.then_inc(sum_ready, 1)

            def score(u):
                i = u["u"]
                if i >= 2:
                    pe.wait_ge(exped, i - 1)
                if i == A_HEADS:
                    pe.wait_ge(hg_out, 4)
                if "need_rope" in u:
                    pe.wait_ge(roped, u["need_rope"])
                after_lin(pe, u["need_g"])
                for c0, w, q_, k_, st, sp_ in u["mm"]:
                    last = nc.tensor.matmul(sc_bank[i % 2][:, c0:c0 + w], q_, k_, start=st, stop=sp_)
                last.then_inc(scored, 1)

            def prob(cb):
                c = cb["c"]
                pe.wait_ge(probs_ready, c + 1)
                if c:
                    pe.wait_ge(pt_ready, c)
                src = probs[:, cb["units"][-1]["u"] % 4, :]
                for b, c0 in enumerate(cb["blocks"]):
                    last = nc.tensor.transpose(pt_bank[:, b * P:(b + 1) * P], src[:, c0:c0 + P], ident[:, :])
                last.then_inc(transposed, 1)

            def values(cb):
                c = cb["c"]
                pe.wait_ge(pt_ready, c + 1)
                if cb["first"] and cb["o"]:
                    pe.wait_ge(heads_out, cb["o"])
                r0, m = cb["out"]
                for c0, w, v_, b, st, sp_ in cb["pv"]:
                    last = nc.tensor.matmul(o_bank[r0:r0 + m, c0:c0 + w], v_, probsT[:, c % 2, b * P:(b + 1) * P],
                                            start=st, stop=sp_)
                last.then_inc(pv_done, 1)

            def hround(s):
                i, r = s["i"], s["r"]
                pe.wait_ge(hg_qk, i + 1)
                if i >= 2:
                    pe.wait_ge(hg_taken, i - 1)
                else:
                    pe.wait_ge(heads_out, att_a_groups)
                if s["grp"] == 1 and r < 2:
                    pe.wait_ge(hg_out, 2)
                banks = hg_banks[i % 2]
                for h in range(4):
                    hh = 4 * s["grp"] + h
                    qv = qk[i % 2][:, 0, h, :]
                    kv_ = kh[:, hh, :] if r < 2 else qk[i % 2][:, 1, h, :]
                    b = banks[h // 2]
                    o = (h % 2) * 256
                    if r <= LEVELS:
                        for tt in range(2):
                            last = nc.tensor.matmul(b[:, o + tt * P:o + (tt + 1) * P], kv_[:, tt * P:(tt + 1) * P],
                                                    qv[:, tt * P:(tt + 1) * P], start=True, stop=True)
                    else:
                        last = nc.tensor.matmul(b[:, o:o + P], kv_[:, 0:P], qv[:, P:2 * P], start=True, stop=True)
                last.then_inc(hg_scored, 1)

            def hvalues(s):
                grp = s["grp"]
                after_lin(pe, stage_last["g_b"])
                pe.wait_ge(hg_taken, (grp + 1) * (LEVELS + 2))
                for h in range(4):
                    hh = 4 * grp + h
                    b = sc_bank[h // 2]
                    o = (h % 2) * 256
                    v_ = [ib[:, i, hh * P:(hh + 1) * P] for i in range(2)]
                    nc.tensor.matmul(b[:, o:o + P], v_[0], probs[:, h // 2, o:o + P], start=True, stop=True)
                    nc.tensor.matmul(b[:, o + P:o + 2 * P], v_[0], probs[:, 2, h * P:(h + 1) * P], start=True, stop=False)
                    last = nc.tensor.matmul(b[:, o + P:o + 2 * P], v_[1], probs[:, h // 2, o + P:o + 2 * P],
                                            start=False, stop=True)
                    if h % 2:
                        last.then_inc(hg_pv, 1)

            do = {"setup": setup, "lin": linear, "norm": norm, "score": score, "probs": prob, "values": values,
                  "hround": hround, "hvalues": hvalues}
            for kind, s in steps:
                if kind in do:
                    do[kind](s)

        @block.scalar
        def _(act):
            chained = [0]
            split_done = [0]
            scal = nc.scalar

            def chain(ins):
                chained[0] += 1
                ins.then_inc(act_chain, 1)
                act.wait_ge(act_chain, chained[0])

            def split(upto, stream):
                for i in range(split_done[0], min(upto, len(splits))):
                    tile = splits[i]
                    if tile["i"] >= stream + RAW - 1:
                        return
                    landed(act, tile)
                    if i >= HL:
                        act.wait_ge(w_used, i - HL + 1)
                    n = tile["n"] * P
                    scal.copy(w_hi[:, i % HL, 0:n], raw[:, tile["i"] % RAW, 0:n]).then_inc(w_hi_ready, 1)
                    split_done[0] = i + 1

            def setup(s):
                act.wait_ge(tables, 1)
                scal.activation(cs1[:, :, :], cs1[:, :, :], ACT.Sin).then_inc(tables_act, 1)
                act.wait_ge(const_in, 96)
                for j, name in enumerate(("c", "c_ctx")):
                    ins = scal.activation(silu_c[:, :, j], colr(name), ACT.Silu)
                ins.then_inc(tables_act, 1)
                act.wait_ge(tables_pe, 1)
                scal.activation(lamt[:, 2:4], sum_bank[:, 0:2], ACT.Exp).then_inc(tables_act, 1)
                act.wait_ge(tables, 4)
                scal.activation(lbt[:, 1:3, :], lbt[:, 1:3, :], ACT.Exp).then_inc(tables_act, 1)

            def linear(s):
                g, ev, t = s["g"], s["evac"], s["t"]
                W = s["w"]
                bank = lin[g % NLIN]
                pos = s["pos"]
                if ev[0] == "act":
                    act.wait_ge(w_used, pos)
                    scal.copy(ev[1][:, t, 0:W], bank[:, 0:W]).then_inc(lin_out[g % NLIN], 1)
                elif ev[0] == "tok":
                    act.wait_ge(w_used, pos)
                    scal.copy(ev[1][:, 0:W // P, ev[2] * P:(ev[2] + 1) * P],
                              bank[:, 0:W].rearrange("p (t n) -> p t n", n=P)).then_inc(lin_out[g % NLIN], 1)
                elif ev[0] in ("silu", "zgate"):
                    act.wait_ge(w_used, pos)
                    rot_free(act, s["slot"])
                    scal.activation(rot[:, s["slot"] % 2, 0:W], bank[:, 0:W], ACT.Silu).then_inc(lin_out[g % NLIN], 1)

            def gates_(s):
                after_lin(act, s["g"])
                scal.activation(qb[:, :, :], qb[:, :, :], ACT.Silu)
                scal.activation(og[:, :, :], og[:, :, :], ACT.Silu).then_inc(gates_ready, 1)
                scal.activation(fb[:, :, :], fb[:, :, :], ACT.Sigmoid)
                scal.activation(ga[:, :, :], ga[:, :, :], ACT.Sigmoid)
                scal.activation(gb[:, :, :], gb[:, :, :], ACT.Sigmoid).then_inc(gates_ready, 1)

            def norm(s):
                n, W = s["n"], s["w"]
                if n:
                    act.wait_ge(sum_ready, n)
                gate = s["gate"]
                if n == 0:
                    act.wait_ge(x_in, 16)
                if gate == "mem":
                    act.wait_ge(mem_in, 16)
                    act.wait_ge(heads_out, s["groups"])
                if gate == "hg":
                    act.wait_ge(hg_out, 4)
                if gate == "ctx":
                    act.wait_ge(ctx_in, 16)
                if gate and gate[0] == "group":
                    act.wait_ge(heads_out, gate[1]["o"] + 1)
                if s["after_g"] is not None:
                    after_lin(act, s["after_g"])
                if s["apply"]["kind"] not in ("head", "hgrn"):
                    if n:
                        act.wait_ge(norm_out, n)
                    if s["pos"]:
                        act.wait_ge(w_used, s["pos"])
                elif n >= 2:
                    act.wait_ge(norm_out, n - 1)
                src, sq = s["src"], s["sq"]
                if len(sq.shape) == 2:
                    dst = sq[:, 0:W]
                    if len(src.shape) == 3:
                        dst = dst.rearrange("p (h t) -> p h t", h=src.shape[1])
                    scal.activation(dst, src, ACT.Square).then_inc(sq_ready, 1)
                else:
                    scal.activation(sq[:, :, :], src, ACT.Square).then_inc(sq_ready, 1)
                act.wait_ge(sum_ready, n + 1)
                r = rstd[:, n % 2, 0:W]
                chain(scal.activation(r, sum_bank[:, 0:W], ACT.Ln, bias=lamt[:, 5:6], scale=s["inv"]))
                scal.activation(r, r, ACT.Exp, scale=-0.5).then_inc(rstd_ready, 1)

            def rope(s):
                if s["after_g"] is not None:
                    after_lin(act, s["after_g"])
                if s["after_n"]:
                    act.wait_ge(norm_out, s["after_n"])
                r, hf = s["slot"], s["half"]
                rot_free(act, r)
                for p0 in range(0, P, 2 * hf):
                    scal.mul(rot[p0:p0 + hf, r % 2, 0:T], s["dst"][p0 + hf:p0 + 2 * hf, :], -1.0)
                    ins = scal.copy(rot[p0 + hf:p0 + 2 * hf, r % 2, 0:T], s["dst"][p0:p0 + hf, :])
                ins.then_inc(rot_ready, 1)

            def score(u):
                i = u["u"]
                act.wait_ge(maxed, i + 1)
                if i >= 4:
                    act.wait_ge(transposed, units[i - 4]["c"] + 1)
                for j, (c0, w, mask) in enumerate(u["segs"]):
                    dst = probs[:, i % 4, c0:c0 + w]
                    ins = scal.activation(dst, dst if mask is not None else sc_bank[i % 2][:, c0:c0 + w], ACT.Exp,
                                          bias=stat[:, 0, i % 4, j:j + 1], scale=u["scale"],
                                          accum_out=stat[:, 1, i % 4, j:j + 1])
                ins.then_inc(exped, 1)

            def prob(cb):
                c = cb["c"]
                act.wait_ge(transposed, c + 1)
                if c >= 2:
                    act.wait_ge(pv_done, c - 1)
                w = len(cb["blocks"]) * P
                scal.copy(probsT[:, c % 2, 0:w], pt_bank[:, 0:w]).then_inc(pt_ready, 1)

            def hvalues(s):
                for j in range(2):
                    act.wait_ge(hg_pv, 2 * s["grp"] + j + 1)
                    a = 4 * s["grp"] + 2 * j
                    scal.copy(qb[:, a:a + 2, :], sc_bank[j][:, :].rearrange("p (h t) -> p h t", h=2))\
                        .then_inc(hg_out, 1)

            do = {"setup": setup, "lin": linear, "norm": norm, "score": score, "probs": prob, "rope": rope,
                  "gates": gates_, "hvalues": hvalues}
            pos = stream = 0
            for kind, s in steps:
                if kind == "lin":
                    for tile in s["pieces"]:
                        split(pos + LOOK, tile["i"])
                        pos += tile["kind"] == "split"
                        stream = tile["i"] + 1
                else:
                    split(pos + LOOK, stream)
                if kind in do:
                    do[kind](s)

        @block.vector
        def _(dve):
            chained = [0]
            split_done = [0]
            vec = nc.vector

            def chain(ins):
                chained[0] += 1
                ins.then_inc(dve_chain, 1)
                dve.wait_ge(dve_chain, chained[0])

            def split(upto, stream):
                for i in range(split_done[0], min(upto, len(splits))):
                    tile = splits[i]
                    if tile["i"] >= stream + RAW - 1:
                        return
                    landed(dve, tile)
                    dve.wait_ge(w_hi_ready, i + 1)
                    if i >= HL:
                        dve.wait_ge(w_used, i - HL + 1)
                    n = tile["n"] * P
                    vec.tensor_sub(w_lo[:, i % HL, 0:n], raw[:, tile["i"] % RAW, 0:n],
                                   w_hi[:, i % HL, 0:n].bitcast(F32)).then_inc(w_lo_ready, 1)
                    split_done[0] = i + 1

            def setup(s):
                dve.wait_ge(const_in, 96)
                chain(vec.memset(lamt[:, 5:6], EPS))
                chain(vec.tensor_copy(cs1[:, 0, :], rot[:, 0, 0:T].bitcast(I32)))
                chain(vec.tensor_scalar(rot[:, 1, 0:T], cs1[:, 0, :], col("invfreq"), None, ALU.mult))
                for j, shift in ((0, 0.25), (1, 0.0)):
                    ang, turns, dst = rot[:, 1, 0:T], rot[:, 1, T:2 * T], cs1[:, j, :]
                    chain(vec.tensor_scalar(turns, ang, 1 / TWO_PI, shift, ALU.mult, ALU.add))
                    chain(vec.tensor_scalar(turns, turns, ROUND, -ROUND, ALU.add, ALU.add))
                    chain(vec.scalar_tensor_tensor(dst, turns, -PI_A, ang, ALU.mult, ALU.add))
                    chain(vec.scalar_tensor_tensor(dst, turns, -PI_B, dst, ALU.mult, ALU.add))
                    chain(vec.scalar_tensor_tensor(dst, turns, -PI_C, dst, ALU.mult, ALU.add))
                    if j == 0:
                        chain(vec.tensor_scalar(dst, dst, math.pi / 2, None, ALU.add))
                    chain(vec.tensor_scalar(dst, dst, PI_F, -PI_F, ALU.min, ALU.max)) if j == 0 else \
                        vec.tensor_scalar(dst, dst, PI_F, -PI_F, ALU.min, ALU.max).then_inc(tables, 1)
                lam0 = COLS["lam"][0]
                lp = cols[0:64, lam0:lam0 + 4].rearrange("p (a b) -> p a b", b=2)
                vec.tensor_tensor(lamt[0:64, 0:2], lp[:, :, 0], lp[:, :, 1], ALU.mult).then_inc(tables, 1)
                l0 = cols[:, COLS["lb"][0]:COLS["lb"][0] + 8]
                l1 = cols[:, COLS["lb"][0] + 8:COLS["lb"][0] + 16]
                chain(vec.tensor_tensor(lbt[:, 0, :], l0, l1, ALU.max))
                vec.tensor_sub(lbt[:, 1, :], l0, lbt[:, 0, :]).then_inc(tables, 1)
                vec.tensor_sub(lbt[:, 2, :], l1, lbt[:, 0, :]).then_inc(tables, 1)
                dve.wait_ge(tables_act, 4)
                chain(vec.tensor_add(lbt[:, 0, :], lbt[:, 1, :], lbt[:, 2, :]))
                chain(vec.reciprocal(lbt[:, 0, :], lbt[:, 0, :]))
                chain(vec.tensor_mul(lbt[:, 0, :], lbt[:, 0, :], lbt[:, 1, :]))
                chain(vec.tensor_scalar(lbt[:, 3, :], lbt[:, 0, :], -1.0, 1.0, ALU.mult, ALU.add))
                chain(vec.tensor_sub(lamt[:, 4:5], lamt[:, 3:4], lamt[:, 2:3]))
                vec.tensor_scalar(lamt[:, 4:5], lamt[:, 4:5], -LAM_INIT, None, ALU.add).then_inc(tables, 1)

            def two_parts(H, L, src):
                chain(vec.tensor_copy(H, src))
                return vec.tensor_sub(L, src, H.bitcast(F32))

            def linear(s):
                g, ev, t, W = s["g"], s["evac"], s["t"], s["w"]
                bank = lin[g % NLIN]
                free = lin_out[g % NLIN]
                if ev == "ada":
                    dve.wait_ge(ada_used, s["pieces"][0]["a"] + 1)
                    vec.tensor_scalar(ada[:, t, :], bank[:, 0:2], col("ada_b", t), None, ALU.add).then_inc(free, 1)
                    return
                if ev[0] in ("act", "tok", "silu"):
                    return
                if ev[0] == "up":
                    dve.wait_ge(w_used, s["pos"])
                    after_lin(dve, g - 1)
                    r = rot[:, (s["slot"] - 1) % 2, 0:W]
                    chain(vec.tensor_mul(r, r, bank[:, 0:W]))
                    two_parts(FH[:, t, :], FL[:, t, :], r).then_inc(free, 1)
                    return
                if ev[0] == "zgate":
                    O_, H, L = ev[1:]
                    after_lin(dve, g)
                    dve.wait_ge(norm_out, s["norms"])
                    r = rot[:, s["slot"] % 2, 0:W]
                    chain(vec.tensor_mul(r, r, O_[:, t, 0:W]))
                    two_parts(H[:, t, :], L[:, t, :], r).then_inc(gate_used, 1)
                    return
                dve.wait_ge(w_used, s["pos"])
                if ev[0] == "gate_a":
                    dve.wait_ge(gates_ready, 2)
                    vec.tensor_mul(ga[:, t, :], ga[:, t, :], bank[:, 0:W]).then_inc(free, 1)
                elif ev[0] == "gate_b":
                    chain(vec.tensor_mul(gb[:, t, :], gb[:, t, :], bank[:, 0:W]))
                    chain(vec.tensor_add(gb[:, t, :], gb[:, t, :], ga[:, t, :]))
                    two_parts(GH[:, t, :], GL[:, t, :], gb[:, t, :]).then_inc(free, 1)
                elif ev[0] == "add":
                    dve.wait_ge(x_again, 16)
                    vec.tensor_add(ev[1][:, t, :], ev[1][:, t, :], bank[:, 0:W]).then_inc(free, 1)

            def norm(s):
                n, W, ap = s["n"], s["w"], s["apply"]
                dve.wait_ge(rstd_ready, n + 1)
                r = rstd[:, n % 2, 0:W]
                if s["pos"] and ap["kind"] not in ("head", "hgrn"):
                    dve.wait_ge(w_used, s["pos"])
                if ap["kind"] == "head":
                    d = ap["dst"]
                    gain = col(ap["g"], ap.get("gi", 0))
                    if ap["g"] == "subln":
                        chain(vec.tensor_scalar(r, r, 1.0 - LAM_INIT, None, ALU.mult))
                    vec.scalar_tensor_tensor(d, d, gain, r, ALU.mult, ALU.mult).then_inc(norm_out, 1)
                    return
                if ap["kind"] == "hgrn":
                    for j in range(2):
                        h = 2 * ap["pr"] + j
                        chain(vec.scalar_tensor_tensor(qb[:, h, :], qb[:, h, :], col("hgrn", h), r[:, j * T:(j + 1) * T],
                                                       ALU.mult, ALU.mult))
                    two = slice(2 * ap["pr"], 2 * ap["pr"] + 2)
                    chain(vec.tensor_mul(qb[:, two, :], qb[:, two, :], og[:, two, :]))
                    two_parts(HH[:, two, :], HLo[:, two, :], qb[:, two, :]).then_inc(norm_out, 1)
                    return
                tm = ap["tmp"]
                src = s["src"]
                rb = r.unsqueeze(1).broadcast_to([P, DT, W])
                if ap["kind"] in ("ada", "post"):
                    j0 = 24 * ap["layer"]
                    c_ = ap["s"]
                    if ap["kind"] == "ada":
                        after_lin(dve, ap["g_ada"])
                        chain(vec.tensor_scalar(coef[:, 0, :], ada[:, j0 + 8:j0 + 16, c_], 1.0, None, ALU.add))
                        chain(vec.tensor_mul(coef[:, 0, :], coef[:, 0, :], colr(f"pre{ap['layer']}")))
                    else:
                        chain(vec.tensor_mul(coef[:, 0, :], ada[:, j0 + 16:j0 + 24, c_], colr(f"post{ap['layer']}")))
                chain(vec.tensor_tensor(tm[:, :, :], src, rb, ALU.mult))
                if ap["kind"] == "affine":
                    for k in range(DT):
                        ins = vec.tensor_scalar(tm[:, k, :], tm[:, k, :], col(ap["a"], k), None, ALU.mult)
                    chain(ins)
                    two_parts(ap["H"][:, :, :], ap["L"][:, :, :], tm[:, :, :]).then_inc(norm_out, 1)
                elif ap["kind"] == "plain":
                    for k in range(DT):
                        ins = vec.tensor_scalar(ap["dst"][:, k, :], tm[:, k, :], col(ap["a"], k), None, ALU.mult)
                    ins.then_inc(norm_out, 1)
                elif ap["kind"] == "ada":
                    for k in range(DT):
                        ins = vec.tensor_scalar(tm[:, k, :], tm[:, k, :], coef[:, 0, k:k + 1], ada[:, j0 + k, c_:c_ + 1],
                                                ALU.mult, ALU.add)
                    chain(ins)
                    cs = slice(c_ * T, (c_ + 1) * T)
                    two_parts(WH[:, :, cs], WL[:, :, cs], tm[:, :, :]).then_inc(norm_out, 1)
                else:
                    for k in range(DT):
                        ins = vec.scalar_tensor_tensor(ap["res"][:, k, :], tm[:, k, :], coef[:, 0, k:k + 1],
                                                       ap["res"][:, k, :], ALU.mult, ALU.add)
                    ins.then_inc(norm_out, 1)

            def rope(s):
                r = rot[:, s["slot"] % 2, 0:T]
                dve.wait_ge(rot_ready, s["r"] + 1)
                if s["r"] == 0:
                    dve.wait_ge(tables_act, 1)
                if s["r"] >= roped_a:
                    dve.wait_ge(tab_in, 16)
                vec.tensor_mul(s["dst"], s["dst"], s["cos"])
                chain(vec.tensor_mul(r, r, s["sin"]))
                vec.tensor_add(s["dst"], s["dst"], r).then_inc(roped, 1)

            def score(u):
                i = u["u"]
                dve.wait_ge(scored, i + 1)
                if i >= 4:
                    dve.wait_ge(transposed, units[i - 4]["c"] + 1)
                for j, (c0, w, mask) in enumerate(u["segs"]):
                    src = sc_bank[i % 2][:, c0:c0 + w]
                    m = stat[:, 0, i % 4, j:j + 1]
                    if mask is not None:
                        ins = vec.tensor_tensor_reduce(probs[:, i % 4, c0:c0 + w], src, mask, 1.0, NEG,
                                                       ALU.add, ALU.max, m)
                    else:
                        ins = vec.reduce_max(m, src, AX_X)
                chain(ins)
                k = len(u["segs"])
                vec.tensor_scalar(stat[:, 0, i % 4, 0:k], stat[:, 0, i % 4, 0:k], -u["scale"], None, ALU.mult)\
                    .then_inc(maxed, 1)

            def prob(cb):
                us = cb["units"]
                dve.wait_ge(exped, us[-1]["u"] + 1)
                k = len(us[0]["segs"])
                for u in us:
                    i = u["u"] % 4
                    ins = vec.reciprocal(stat[:, 2, i, 0:k], stat[:, 1, i, 0:k])
                chain(ins)
                if len(us) == 2:
                    b = us[1]["u"] % 4
                    chain(vec.tensor_scalar(stat[:, 2, b, 0:k], stat[:, 2, b, 0:k], lamt[:, 4:5], None, ALU.mult))
                a = us[0]["u"] % 4
                for j, (c0, w, _m) in enumerate(us[0]["segs"]):
                    ins = vec.tensor_scalar(probs[:, a, c0:c0 + w], probs[:, a, c0:c0 + w], stat[:, 2, a, j:j + 1], None,
                                            ALU.mult)
                if len(us) == 2:
                    chain(ins)
                    for j, (c0, w, _m) in enumerate(us[0]["segs"]):
                        ins = vec.scalar_tensor_tensor(probs[:, b, c0:c0 + w], probs[:, b, c0:c0 + w],
                                                       stat[:, 2, b, j:j + 1], probs[:, a, c0:c0 + w], ALU.mult, ALU.add)
                ins.then_inc(probs_ready, 1)

            def values(cb):
                if not cb["last"]:
                    return
                dve.wait_ge(pv_done, cb["c"] + 1)
                ev = cb["evac"]
                if ev[0] == "split":
                    for H, L, cs in ev[1]:
                        ins = vec.tensor_copy(H, o_bank[:, cs])
                    chain(ins)
                    for H, L, cs in ev[1]:
                        ins = vec.tensor_sub(L, o_bank[:, cs], H.bitcast(F32))
                    ins.then_inc(heads_out, 1)
                else:
                    vec.tensor_copy(ev[1], o_bank[:, 0:ev[2]]).then_inc(heads_out, 1)

            def hprep(s):
                dve.wait_ge(gates_ready, 2)
                for h in range(B_HEADS):
                    ins = vec.tensor_scalar(fb[:, h, :], fb[:, h, :], lbt[:, 3, h:h + 1], lbt[:, 0, h:h + 1],
                                            ALU.mult, ALU.add)
                chain(ins)
                chain(vec.tensor_scalar(kh[:, :, :], fb[:, :, :], -1.0, 1.0, ALU.mult, ALU.add))

            def hround(s):
                i, r, grp = s["i"], s["r"], s["grp"]
                hs = slice(4 * grp, 4 * grp + 4)
                qd, kd = qk[i % 2][:, 0, :, :], qk[i % 2][:, 1, :, :]
                if i >= 2:
                    dve.wait_ge(hg_scored, i - 1)
                if i == 1:
                    after_lin(dve, g_br_attn)
                sc = P ** -0.5
                if r == 0:
                    if grp == 1:
                        dve.wait_ge(hg_pv, 2)
                    vec.memset(probs[:, 0:2, :], 0.0)
                    vec.tensor_scalar(qd, qb[:, hs, :], sc, None, ALU.mult).then_inc(hg_qk, 1)
                    chain(vec.tensor_copy(decF[:, :, :], fb[:, hs, :]))
                    chain(vec.memset(decB[:, :, :], 1.0))
                elif r == 1:
                    vec.scalar_tensor_tensor(qd, qb[:, hs, :], sc, decF[:, :, :], ALU.mult, ALU.mult).then_inc(hg_qk, 1)
                else:
                    chain(vec.scalar_tensor_tensor(qd, qb[:, hs, :], sc, decF[:, :, :], ALU.mult, ALU.mult))
                    vec.tensor_mul(kd, kh[:, hs, :], decB[:, :, :]).then_inc(hg_qk, 1)
                dve.wait_ge(hg_qk, i + 1)
                if 1 <= r <= LEVELS:
                    half = 1 << (r - 1)
                    Fv = decF[:, :, :].rearrange("p h (b c) -> p (h b) c", c=2 * half)
                    Bv = decB[:, :, :].rearrange("p h (b c) -> p (h b) c", c=2 * half)
                    nb = 4 * T // (2 * half)
                    end1 = Fv[:, :, half - 1:half].broadcast_to([P, nb, half])
                    end2 = Fv[:, :, 2 * half - 1:2 * half].broadcast_to([P, nb, half])
                    chain(vec.tensor_mul(Bv[:, :, 0:half], Bv[:, :, 0:half], end2))
                    chain(vec.tensor_mul(Fv[:, :, half:2 * half], Fv[:, :, half:2 * half], end1))
                dve.wait_ge(hg_scored, i + 1)
                banks = hg_banks[i % 2]
                for j in range(2):
                    if r <= LEVELS:
                        m = hmask[:, r:r + 1, :].broadcast_to([P, 4, P])
                        ins = vec.copy_predicated(probs[:, j, :].rearrange("p (a n) -> p a n", n=P), m,
                                                  banks[j][:, :].rearrange("p (a n) -> p a n", n=P))
                    else:
                        ins = vec.tensor_copy(probs[:, 2, 2 * j * P:(2 * j + 2) * P].rearrange("p (a n) -> p a n", n=P),
                                              banks[j][:, :].rearrange("p (a n) -> p a n", n=2 * P)[:, :, 0:P])
                ins.then_inc(hg_taken, 1)
                dve.wait_ge(hg_taken, i + 1)

            do = {"setup": setup, "lin": linear, "norm": norm, "score": score, "probs": prob, "values": values,
                  "rope": rope, "hprep": hprep, "hround": hround}
            pos = stream = 0
            for kind, s in steps:
                if kind == "lin":
                    for tile in s["pieces"]:
                        split(pos + LOOK, tile["i"])
                        pos += tile["kind"] == "split"
                        stream = tile["i"] + 1
                else:
                    split(pos + LOOK, stream)
                if kind in do:
                    do[kind](s)


def tiled(w):
    k, n = w.shape
    return np.ascontiguousarray(w.reshape(k // P, P, n // P, P).transpose(2, 1, 0, 3).reshape(n // P, P, k))


def feature_major(x):
    return np.ascontiguousarray(x.T.reshape(DT, P, -1).transpose(1, 0, 2))


def constants():
    p = np.arange(P)
    f32 = np.float32
    causal = np.zeros((P, 2 * P), f32)
    causal[:, P:] = np.where(p[None, :] > p[:, None], f32(NEG), f32(0))
    masks = np.zeros((P, 8, P), np.uint32)
    masks[:, 0] = np.eye(P, dtype=np.uint32)
    for r in range(1, LEVELS + 1):
        half = 1 << (r - 1)
        s_, t_ = p[:, None], p[None, :]
        masks[:, r] = (s_ // (2 * half) == t_ // (2 * half)) & (s_ // half % 2 == 0) & (t_ // half % 2 == 1)
    inv = np.power(f32(10000.0), -np.arange(0, A_HD, 2, dtype=f32) / f32(A_HD)).astype(f32)
    tab = np.zeros((P, 4, T), f32)
    tok = np.arange(T)
    for j, hd in ((0, DA_HD), (2, GQ_HD)):
        axis = hd // 2
        fr = np.power(f32(10000.0), -np.arange(0, axis, 2, dtype=f32) / f32(axis)).astype(f32)
        ang = np.concatenate([(tok // 64).astype(f32)[:, None] * fr, (tok % 64).astype(f32)[:, None] * fr], -1)
        ang = ang[:, p % (hd // 2)].T
        tab[:, j], tab[:, j + 1] = np.cos(ang), np.sin(ang)
    return {"causal": causal, "hmask": masks, "tab2": tab, "ident": np.eye(P, dtype=f32), "ones": np.ones((P, P), f32),
            "invfreq": inv[p % 32]}


def kernel(**inputs):
    import concourse.bacc as bacc
    from concourse.bass_utils import run_bass_kernel_spmd

    a = {k: np.asarray(v) for k, v in inputs.items()}
    const = constants()
    vec = np.zeros((P, NCOLS), np.float32)

    def put(name, rows):
        at, n = COLS[name]
        vec[:rows.shape[1], at:at + n] = rows.T

    for name, v in (("norm_mix", a["norm_mix_g"]), ("hgrn", a["hgrn_norm_g"]), ("norm_x", a["norm_x_g"]),
                    ("norm_mem", a["norm_mem_g"]), ("norm_ffn", a["norm_ffn_g"]), ("final", a["final_norm_g"]),
                    ("pre0", a["pre_g_2"][0]), ("pre1", a["pre_g_2"][1]), ("post0", a["post_g_2"][0]),
                    ("post1", a["post_g_2"][1]), ("c", a["c_2"]), ("c_ctx", a["c_ctx_2"]), ("ada_b", a["ada_b_2"]),
                    ("subln", a["a_subln_g_2"]), ("qk_g", a["b_qk_g_2"]), ("lb", a["hgrn_lb_logits"])):
        put(name, v.reshape(-1, P))
    put("lam", a["a_lambda_2"].reshape(4, DA_HD))
    put("invfreq", const.pop("invfreq").reshape(1, P))

    arrays = dict(const)
    arrays["cols"] = vec
    arrays["positions"] = np.ascontiguousarray(np.broadcast_to(a["positions"].reshape(1, T).astype(np.int32), (P, T)))
    arrays["xT"], arrays["memT"] = feature_major(a["x"][0]), feature_major(a["mem"][0])
    arrays["ctxT"] = feature_major(a["ctx_2"][0])
    stages = {"br_attn": a["w_br_attn"][0], "br_hgrn": a["w_br_hgrn"][0], "w_out": a["w_out"][0], "q_x": a["wq_x"][0],
              "wo_x": a["wo_x"][0], "ffn_out": a["w_ffn_out"][0], "w_out0": a["w_out_2"][0], "w_out1": a["w_out_2"][1]}

    def cut(w, names, widths):
        at = 0
        for n, c in zip(names, widths):
            stages[n] = w[:, at:at + c]
            at += c

    cut(a["w_in"][0], ("q_a", "k_a", "v_a", "q_b", "f_b", "i_b", "og_b", "g_a", "g_b"), [D] * 9)
    cut(a["wkv_x"][0], ("k_x", "v_x"), [D] * 2)
    cut(a["w_ffn_in"][0], ("gate", "up"), [FFN] * 2)
    cut(a["a_w_in_2"][0], ("q_2", "k_2", "v_2", "z_2"), [D] * 4)
    cut(a["b_w_in_2"][0], ("q_3", "k_3", "v_3", "z_3"), [D, GQ_KV * GQ_HD, GQ_KV * GQ_HD, D])
    arrays.update({n: tiled(w) for n, w in stages.items()})
    arrays["ada"] = np.concatenate([tiled(a["ada_w_2"][i]) for i in range(2)])

    nc = bacc.Bacc("TRN2", target_bir_lowering=False, num_devices=1)
    dram = {n: nc.dram_tensor(f"in_{n}", v.shape, mybir.dt.from_np(v.dtype), kind="ExternalInput").ap()
            for n, v in arrays.items()}
    out = nc.dram_tensor("out", (P, DT, T), F32, kind="ExternalOutput").ap()
    program(nc, dram, out)
    r = run_bass_kernel_spmd(nc, [{f"in_{n}": v for n, v in arrays.items()}], core_ids=[0])
    got = r.results[0]["out"]
    return np.ascontiguousarray(got.transpose(1, 0, 2).reshape(D, T).T).reshape(1, T, D)
```

```python
import math
from contextlib import ExitStack

import numpy as np

import concourse.bass as bass
from concourse import mybir

F32 = mybir.dt.float32
F32R = mybir.dt.float32r
I32 = mybir.dt.int32
U32 = mybir.dt.uint32
ALU = mybir.AluOpType
ACT = mybir.ActivationFunctionType
AX_X = mybir.AxisListType.X

P = 128
T = 256
D = 1024
DT = D // P
EPS = 1e-6
NEG = -1e30
FFN = 2816
FT = FFN // P
A_HEADS, A_HD = 16, 64
B_HEADS = 8
X_HEADS, X_HD = 4, 256
DA_HEADS, DA_HD = 8, 64
GQ_HEADS, GQ_KV, GQ_HD = 8, 2, 128
LAM_INIT = 0.8 - 0.6 * math.exp(-0.3 * 0)
LEVELS = 7
TWO_PI = 2 * math.pi
PI_A = 6.28125
PI_B = float(np.float32(int((TWO_PI - PI_A) * 2 ** 20) / 2 ** 20))
PI_C = TWO_PI - PI_A - PI_B
ROUND = 1.5 * 2 ** 23
PI_F = 3.1415925

COLS = {}
_at = 0
for _name, _n in [("norm_mix", 8), ("hgrn", 8), ("norm_x", 8), ("norm_mem", 8), ("norm_ffn", 8),
                  ("final", 8), ("pre0", 8), ("pre1", 8), ("post0", 8), ("post1", 8), ("c", 8), ("c_ctx", 8),
                  ("ada_b", 48), ("subln", 1), ("qk_g", 2), ("lb", 16), ("lam", 4), ("invfreq", 1)]:
    COLS[_name] = (_at, _n)
    _at += _n
NCOLS = _at

RAW, HL, LOOK = 7, 4, 3
NLIN = 3


def program(nc, dram, out_dram):
    ctx = ExitStack()
    with ctx:
        base = 16512
        SLAB = DT * T * 4
        at = [base]

        def place(name, shape, dt=F32, offset=None):
            n = int(np.prod(shape[1:])) * 4
            if offset is None:
                offset = at[0]
                at[0] += (n + 31) // 32 * 32
            return nc.alloc_sbuf_tensor_at(name, shape, dt, offset=offset)

        raw = place("w_raw", [P, RAW, DT * P])
        w_hi = place("w_hi", [P, HL, DT * P], F32R)
        w_lo = place("w_lo", [P, HL, DT * P], F32R)
        slab0 = at[0]
        at[0] += 14 * SLAB

        def slab(name, i, shape, dt=F32, extra=0):
            return place(name, [P] + shape, dt, slab0 + i * SLAB + extra)

        probs = place("probs", [P, 4, 512])
        probsT = place("probsT", [P, 2, 512])
        rot = place("rot", [P, 2, 512])
        rstd = place("rstd", [P, 2, 512])
        sqr = place("sqr", [P, 2, 512])
        diag = place("diag", [P, 4, P])
        ms = place("ms", [P, 40, 4])
        rt = ms
        mhalf = place("mhalf", [P, 1])
        ident = place("ident", [P, P])
        ones = place("ones", [P, P])
        causal = place("causal", [P, 2 * P])
        hmask_at = at[0]
        hmask = place("hmask", [P, LEVELS, P], U32)
        tab2 = place("tab2", [P, 4, T], F32, hmask_at)
        cs1 = place("cs1", [P, 2, T])
        cols = place("cols", [P, NCOLS])
        ada = place("ada", [P, 48, 2])
        silu_c = place("silu_c", [P, DT, 2])
        stat = place("stat", [P, 4, 4, 2])
        lbt = place("lbt", [P, 4, 8])
        lamt = place("lamt", [P, 6])
        coef = place("coef", [P, 4, 8])
        assert at[0] <= 229368, at[0]

        xT = slab("xT", 0, [DT, T])
        XH, XL = slab("XH", 1, [DT, T], F32R), slab("XL", 2, [DT, T], F32R)
        Q, K = slab("Q", 3, [DT, T]), slab("K", 4, [DT, T])
        V = slab("V", 5, [2, D])
        qb, fb, og = slab("qb", 6, [DT, T]), slab("fb", 7, [DT, T]), slab("og", 9, [DT, T])
        ib = slab("ib", 8, [2, D])
        ga, gb = slab("ga", 10, [DT, T]), slab("gb", 11, [DT, T])
        AH, AL = slab("AH", 12, [DT, T], F32R), slab("AL", 13, [DT, T], F32R)
        memT = slab("memT", 0, [DT, T])
        MH, ML = slab("MH", 1, [DT, T], F32R), slab("ML", 2, [DT, T], F32R)
        kh = slab("kh", 3, [DT, T])
        decF, decB = slab("decF", 4, [4, T]), slab("decB", 4, [4, T], F32, SLAB // 2)
        qk = [slab("qk0", 5, [2, 4, T]), slab("qk1", 12, [2, 4, T])]
        KX, VX = slab("KX", 13, [DT, T]), slab("VX", 0, [2, D])
        HH, HLo = slab("HH", 7, [DT, T], F32R), slab("HLo", 8, [DT, T], F32R)
        GH, GL = slab("GH", 1, [DT, T], F32R), slab("GL", 2, [DT, T], F32R)
        hres = slab("hres", 3, [DT, T])
        NH, NL = slab("NH", 5, [DT, T], F32R), slab("NL", 6, [DT, T], F32R)
        QX = slab("QX", 7, [DT, T])
        CH, CL = slab("CH", 8, [DT, T], F32R), slab("CL", 9, [DT, T], F32R)
        FH, FL = slab("FH", 7, [FT, T], F32R), slab("FL", 10, [FT, T], F32R)
        X2, XC = slab("X2", 0, [DT, T]), slab("XC", 1, [DT, T])
        WH, WL = slab("WH", 6, [2, DT, T], F32R), slab("WL", 8, [2, DT, T], F32R)
        wideT = slab("wideT", 4, [2, 4, 512])
        Q2, K2 = slab("Q2", 10, [DT, 2 * T]), slab("K2", 12, [DT, 2 * T])
        V2 = slab("V2", 2, [4, D])
        ZH, ZL = slab("ZH", 12, [DT, 2 * T], F32R), slab("ZL", 2, [DT, 2 * T], F32R)
        Y2 = slab("Y2", 6, [DT, 2 * T])
        QB = slab("QB", 10, [DT, T])
        KB = slab("KB", 11, [GQ_KV, 2 * T])
        VB = slab("VB", 11, [4, GQ_KV * GQ_HD], F32, SLAB // 2)
        BH, BL = slab("BH", 12, [DT, T], F32R), slab("BL", 13, [DT, T], F32R)
        YB = slab("YB", 6, [DT, T])
        W3H, W3L = slab("W3H", 2, [2, DT, T], F32R), slab("W3L", 8, [2, DT, T], F32R)

        def psum(name):
            return ctx.enter_context(nc.psum_tensor(name, [P, 512], F32))

        lin = [psum(f"lin{i}") for i in range(NLIN)]
        sc_bank = [psum("score0"), psum("score1")]
        pt_bank, o_bank, sum_bank = psum("pt_bank"), psum("o_bank"), psum("sum_bank")
        hg_banks = [(sc_bank[0], sc_bank[1]), (pt_bank, o_bank)]

        def sem(name):
            return ctx.enter_context(nc.semaphore(name))

        w_landed = [sem(f"w_landed{i}") for i in range(RAW)]
        w_hi_ready, w_lo_ready = sem("w_hi_ready"), sem("w_lo_ready")
        w_used = sem("w_used")
        ada_used = sem("ada_used")
        lin_out = [sem(f"lin_out{i}") for i in range(NLIN)]
        cols_in = sem("cols_in")
        pool_const = sem("pool_const")
        const_in, x_in, mem_in, x_again, ctx_in, tab_in = (sem(n) for n in
                                                            ("const_in", "x_in", "mem_in", "x_again", "ctx_in", "tab_in"))
        tables = sem("tables")
        tables_act = sem("tables_act")
        tables_pe = sem("tables_pe")
        sq_ready, sq_used = sem("sq_ready"), sem("sq_used")
        ms_ready, rt_ready = sem("ms_ready"), sem("rt_ready")
        diag_ready, bc_ready, rstd_ready = sem("diag_ready"), sem("bc_ready"), sem("rstd_ready")
        op_hi, op_ready = sem("op_hi"), sem("op_ready")
        u_ready = sem("u_ready")
        res_ready = sem("res_ready")
        half_done = sem("half_done")
        gate_in, silu_done = sem("gate_in"), sem("silu_done")
        hg_dec, hg_k = sem("hg_dec"), sem("hg_k")
        rot_ready, roped = sem("rot_ready"), sem("roped")
        scored, maxed, exped, probs_ready = (sem(n) for n in ("scored", "maxed", "exped", "probs_ready"))
        transposed, pt_ready, pv_done, heads_out = (sem(n) for n in ("transposed", "pt_ready", "pv_done", "heads_out"))
        gates_ready = sem("gates_ready")
        hg_qk, hg_scored, hg_taken, hg_att, hg_pv, hg_out = (sem(n) for n in
                                                             ("hg_qk", "hg_scored", "hg_taken", "hg_att", "hg_pv", "hg_out"))
        gate_used = sem("gate_used")
        dve_chain, act_chain = sem("dve_chain"), sem("act_chain")
        stored = sem("stored")

        def col(name, i=0):
            return cols[:, COLS[name][0] + i:COLS[name][0] + i + 1]

        def colr(name):
            a, n = COLS[name]
            return cols[:, a:a + n]

        steps = []
        tiles = []
        n_lin = [0]
        n_split = [0]
        n_ada = [0]
        n_z = [0]
        rot_uses = []
        stage_last = {}

        def lin_step(stage, t, kts, feat, op, width, evac, kind="split", part=None):
            pieces = []
            for tt in ([t] if feat else [t, t + 1]):
                k = 0
                while k < kts and part != 1:
                    n = min(DT, kts - k)
                    tile = {"stage": stage, "t": tt, "k": k, "n": n, "kind": kind, "i": len(tiles)}
                    if kind == "split":
                        tile["s"] = n_split[0]
                        n_split[0] += 1
                    else:
                        tile["a"] = n_ada[0]
                        n_ada[0] += 1
                    tiles.append(tile)
                    pieces.append(tile)
                    k += n
            g = n_lin[0]
            n_lin[0] += 1
            stage_last[stage] = g
            slot = len(rot_uses)
            if evac[0] == "silu":
                rot_uses.append(("lin", g + 1))
                n_gate[0] += 1
            elif evac[0] == "zgate":
                n_z[0] += 1
                rot_uses.append(("z", n_z[0]))
            if part == 0:
                n_half[0] += 1
            pos = n_split[0]
            s = {"g": g, "pieces": pieces, "feat": feat, "op": op, "w": width, "evac": evac, "part": part,
                 "t": t, "stage": stage, "pos": pos, "kind": kind, "kts": kts, "half": n_half[0],
                 "slot": slot, "z": n_z[0], "gate": n_gate[0], "first_slot": None if feat or kind != "split" else (pos - 2) % HL}
            assert feat or (pos % 2 == 0)
            if evac[0] == "qk3":
                s["sq"] = new_sq(evac[3], 0, None, width // P, 1)
                lin_sq[0] = s["sq"]
            steps.append(("lin", s))

        def operand(H, L, wide=False, ops=None):
            return {"H": H, "L": L, "wide": wide, "ops": ops}

        def new_norm(n_in, W):
            n = n_norm[0]
            n_norm[0] += 1
            return {"n": n, "inv": 1.0 / n_in, "w": W}

        def new_sq(N, k, src, tts, K):
            m = n_sq[0]
            n_sq[0] += 1
            N["m"] = n_sq[0]
            return {"N": N, "k": k, "src": src, "tts": tts, "K": K, "m": m}

        def sq_step(N, k, src, K=DT, after=None):
            s = new_sq(N, k, src, N["w"] // P, K)
            s["after"] = after
            s["pos"] = n_split[0]
            steps.append(("sq", s))

        def rt_step(N):
            steps.append(("rt", {"N": N, "n": N["n"], "tts": N["w"] // P}))

        def bc_step(N):
            N["r"] = n_bc[0]
            n_bc[0] += 1
            steps.append(("bc", {"N": N, "n": N["n"], "r": N["r"], "tts": N["w"] // P, "w": N["w"]}))

        def bc_with(N):
            lin_s = steps[-1][1]
            bc_step(N)
            lin_s["bc"] = steps.pop()[1]

        def gain_step(k, src, gain, H, L, after=None):
            n_op[0] += 1
            n_hi[0] += 1
            steps.append(("gain", {"k": k, "src": src, "gain": gain, "H": H, "L": L, "after": after, "op": n_op[0],
                                   "hi": n_hi[0], "pos": n_split[0]}))

        def shift_step(N, layer, st, src, H, L):
            first = n_op[0]
            n_op[0] += DT
            n_hi[0] += DT
            steps.append(("shift", {"N": N, "layer": layer, "st": st, "src": src, "H": H, "L": L, "op0": first,
                                    "hi0": n_hi[0] - DT, "u0": n_u[0], "pos": n_split[0]}))
            n_u[0] += DT

        def post_step(N, layer, st, y, res, k):
            n_res[0] += 1
            steps.append(("post", {"N": N, "layer": layer, "st": st, "y": y, "res": res, "k": k, "res_n": n_res[0]}))
            return n_res[0]

        lin_sq = [None]
        n_norm, n_sq, n_bc, n_op, n_hi, n_u, n_res, n_gate, n_half = ([0] for _ in range(9))

        units = []
        combos = []
        groups = []
        n_rope = [0]

        def rope_step(dst, halves, cos, sin, after_g=None, after_res=None):
            steps.append(("rope", {"r": n_rope[0], "dst": dst, "half": halves, "cos": cos, "sin": sin,
                                   "after_g": after_g, "after_res": after_res, "slot": len(rot_uses)}))
            n_rope[0] += 1
            rot_uses.append(("rope", n_rope[0]))

        def ada_some(k):
            for _ in range(k):
                if n_ada[0] < 48:
                    lin_step("ada", n_ada[0], DT, True, None, 2, "ada", "ada")

        def attention(new_units, fill):
            todo = []
            for cb in new_units:
                cb["c"] = len(combos)
                combos.append(cb)
                for u in cb["units"]:
                    u["u"] = len(units)
                    u["c"] = cb["c"]
                    units.append(u)
                cb["pvo"], cb["g0"] = len(pvs), len(groups)
                if cb["pv"]:
                    cb["o"] = len(pvs)
                    pvs.append(cb)
                    if cb["last"]:
                        cb["grp"] = len(groups)
                        groups.append(cb)
                todo.append(cb)
            for u in todo[0]["units"]:
                steps.append(("score_mm", u))
                steps.append(("score_exp", u))
            prev = None
            for j, cb in enumerate(todo):
                steps.append(("pscale", cb))
                nxt = todo[j + 1]["units"] if j + 1 < len(todo) else []
                for u in nxt:
                    steps.append(("score_mm", u))
                if prev is not None and prev["pv"]:
                    steps.append(("values", prev))
                fill()
                steps.append(("transp", cb))
                for u in nxt:
                    steps.append(("score_exp", u))
                if prev is not None and prev["pv"]:
                    steps.append(("values_out", prev))
                prev = cb
            steps.append(("values", prev))
            steps.append(("values_out", prev))

        pvs = []

        NX = new_norm(D, T)
        ops = []
        for k in range(DT):
            gain_step(k, xT[:, k, :], "norm_mix", XH[:, k, :], XL[:, k, :])
            ops.append(n_op[0])
        for k in range(DT):
            sq_step(NX, k, xT[:, k, :])
        XW = operand(XH, XL, ops=ops)

        def feat8(stage, op, evac, width=T, kts=DT, fill=None):
            for t in range(8):
                lin_step(stage, t, kts, True, op, width, evac)
                if fill:
                    fill(t)

        for t in range(8):
            lin_step("q_a", t, DT, True, XW, T, ("act", Q))
            if t == 0:
                rt_step(NX)
                steps.append(("setup", {}))
            elif t == 1:
                bc_step(NX)
            elif t == 2:
                steps.append(("cosr", {}))
                for j in range(3):
                    rope_step(Q[:, j, :], 32, cs1[:, 0, :], cs1[:, 1, :], n_lin[0] - 1)
            else:
                rope_step(Q[:, t, :], 32, cs1[:, 0, :], cs1[:, 1, :], n_lin[0] - 1)
        steps.append(("load_mem", {}))
        for t in range(8):
            lin_step("k_a", t, DT, True, XW, T, ("act", K))
            if t:
                rope_step(K[:, t - 1, :], 32, cs1[:, 0, :], cs1[:, 1, :], n_lin[0] - 2)
        for t in range(0, 8, 2):
            lin_step("v_a", t, DT, False, XW, T, ("tok", V, t, NX))
            if t == 0:
                rope_step(K[:, 7, :], 32, cs1[:, 0, :], cs1[:, 1, :], n_lin[0] - 2)
        roped_a = n_rope[0]

        def head_a(h):
            j, r = h // 2, 64 * (h % 2)
            qh, kk_ = Q[r:r + 64, j, :], K[r:r + 64, j, :]
            u = {"segs": [(0, 128, causal[:, 128:256]), (128, 256, causal[:, :])], "scale": A_HD ** -0.5, "rt": None,
                 "mm": [(0, 128, qh[:, 0:128], kk_[:, 0:128], True, True),
                        (128, 256, qh[:, 128:256], kk_, True, True)],
                 "need_g": stage_last["v_a"], "need_rope": roped_a}
            vh = [V[:, i, h * 64:h * 64 + 64] for i in range(2)]
            return {"units": [u], "blocks": [(0, 0), (128, 128), (256, 256)], "out": (r, 64),
                    "copies": [(slice(0, 384), probsT, slice(0, 384))],
                    "pv": [(0, 256, vh[0], (0, 256), True, False), (128, 128, vh[1], (256, 128), False, True)],
                    "first": h % 2 == 0, "last": h % 2 == 1,
                    "evac": ("split", [(AH[:, j, :], AL[:, j, :], slice(0, T))])}

        todo = [(n, t, ("R", d, NX), True) for n, d in (("q_b", qb), ("f_b", fb)) for t in range(8)]
        todo += [("i_b", t, ("tok", ib, t, NX), False) for t in range(0, 8, 2)]
        todo += [(n, t, ("R", d, NX), True) for n, d in (("og_b", og), ("g_a", ga), ("g_b", gb)) for t in range(8)]

        def fill_w():
            for _ in range(3):
                if todo:
                    n, t, ev, feat = todo.pop(0)
                    lin_step(n, t, DT, feat, XW, T, ev)
                    if n == "og_b" and t == 7:
                        steps.append(("gates", {"g": n_lin[0] - 1, "sig": [fb], "silu": [qb, og]}))

        attention([head_a(h) for h in range(A_HEADS)], fill_w)
        while todo:
            fill_w()
        att_a_groups = len(groups)
        steps.append(("gates", {"g": n_lin[0] - 1, "sig": [ga, gb], "silu": []}))
        steps.append(("hprep", {}))

        NM = new_norm(D, T)
        br_ops = operand(AH, AL)
        for t in range(8):
            lin_step("br_attn", t, DT, True, br_ops, T, ("gate_a", None))
            sq_step(NM, t, memT[:, t, :], after="mem")
        rt_step(NM)
        g_br_attn = stage_last["br_attn"]
        ops = []
        for k in range(DT):
            gain_step(k, memT[:, k, :], "norm_mem", MH[:, k, :], ML[:, k, :])
            ops.append(n_op[0])
        MW = operand(MH, ML, ops=ops)
        kv = [("k_x", t, ("R", KX, NM), True) for t in range(8)] + [("v_x", t, ("tok", VX, t, NM), False) for t in range(0, 8, 2)]
        ROUNDS = LEVELS + 2

        def hform(i):
            steps.append(("hform", {"grp": i // ROUNDS, "r": i % ROUNDS, "i": i}))

        hform(0)
        for i in range(2 * ROUNDS):
            if i + 1 < 2 * ROUNDS:
                hform(i + 1)
            if kv:
                n, t, ev, feat = kv.pop(0)
                lin_step(n, t, DT, feat, MW, T, ev)
                if n == "k_x" and t == 0:
                    bc_with(NM)
            else:
                ada_some(2)
            steps.append(("htake", {"grp": i // ROUNDS, "r": i % ROUNDS, "i": i}))
            if i % ROUNDS == ROUNDS - 1:
                steps.append(("hvalues", {"grp": i // ROUNDS}))
        steps.append(("load_again", {}))
        hg_norms = []
        for pr in range(4):
            N = new_norm(P, 512)
            sq_step(N, 0, qb[:, 2 * pr:2 * pr + 2, :], 1, "hg")
            hg_norms.append(N)
            rt_step(N)
            ada_some(1)
        ops = []
        for pr, N in enumerate(hg_norms):
            bc_step(N)
            n_op[0] += 1
            steps.append(("hgate", {"N": N, "pr": pr}))
            ops += [n_op[0]] * 2
        feat8("br_hgrn", operand(HH, HLo, ops=ops), ("gate_b", None))

        def residual(stage, op, kts, gain, H, L, W2=None):
            N = new_norm(D, T)
            ops = []
            for t in range(8):
                lin_step(stage, t, kts, True, op, T, ("add", hres))
                sq_step(N, t, hres[:, t, :], DT, ("g", n_lin[0] - 1))
                if gain:
                    gain_step(t, hres[:, t, :], gain, H[:, t, :], L[:, t, :], ("g", n_lin[0] - 1))
                    ops.append(n_op[0])
            rt_step(N)
            return N, operand(H, L, ops=ops) if gain else None

        N3, op3 = residual("w_out", operand(GH, GL), DT, "norm_x", NH, NL)

        steps.append(("load_ctx", {}))

        for t in range(8):
            lin_step("q_x", t, DT, True, op3, T, ("R", QX, N3))
            if t == 0:
                bc_with(N3)

        def head_x(h):
            u = {"segs": [(0, 256, None), (256, 256, None)], "scale": X_HD ** -0.5, "rt": None, "need_g": stage_last["q_x"],
                 "mm": [(s * 256, 256, QX[:, 2 * h + k, s * 128:s * 128 + 128], KX[:, 2 * h + k, :], k == 0, k == 1)
                        for s in range(2) for k in range(2)]}
            pv = []
            for dv in range(2):
                for kt in range(2):
                    pv.append((dv * 256, 256, VX[:, kt, h * 256 + dv * 128:h * 256 + dv * 128 + 128],
                               (kt * 256, 256), kt == 0, kt == 1))
            return {"units": [u], "blocks": [(0, 0), (128, 256), (256, 128), (384, 384)], "out": (0, 128), "pv": pv,
                    "copies": [(slice(0, 512), probsT, slice(0, 512))], "first": True, "last": True,
                    "evac": ("split", [(CH[:, 2 * h + dv, :], CL[:, 2 * h + dv, :], slice(dv * 256, dv * 256 + 256))
                                       for dv in range(2)])}

        attention([head_x(h) for h in range(X_HEADS)], lambda: ada_some(3))
        N4, op4 = residual("wo_x", operand(CH, CL), DT, "norm_ffn", NH, NL)

        for t in range(FT):
            lin_step("gate", t, DT, True, op4, T, ("silu", None, N4))
            if t == 0:
                bc_with(N4)
            lin_step("up", t, DT, True, op4, T, ("up", None, N4))
        N5, _ = residual("ffn_out", operand(FH, FL), FT, None, None, None)
        bc_step(N5)
        NP = [new_norm(D, T), new_norm(D, T)]
        for k in range(DT):
            n_res[0] += 1
            steps.append(("final", {"N": N5, "k": k, "res_n": n_res[0]}))
            sq_step(NP[0], k, X2[:, k, :], DT, ("res", n_res[0]))
        rt_step(NP[0])

        ada_some(48)
        g_ada = stage_last["ada"]
        for k in range(DT):
            sq_step(NP[1], k, XC[:, k, :], DT, "ctx")
        rt_step(NP[1])
        ops = []
        for st, src in ((0, X2), (1, XC)):
            bc_step(NP[st])
            shift_step(NP[st], 0, st, src, WH, WL)
        ops2 = [n_op[0] - DT + k + 1 for k in range(DT)]
        W2 = operand(WH, WL, True, ops2)
        for t in range(8):
            lin_step("q_2", t, DT, True, W2, 2 * T, ("act", Q2))
            if t:
                rope_step(Q2[:, t - 1, 0:T], 32, tab2[:, 0, :], tab2[:, 1, :], n_lin[0] - 2)
        for t in range(8):
            lin_step("k_2", t, DT, True, W2, 2 * T, ("act", K2))
            rope_step(K2[:, t - 1, 0:T] if t else Q2[:, 7, 0:T], 32, tab2[:, 0, :], tab2[:, 1, :], n_lin[0] - 2)
        for t in range(0, 8, 2):
            for part in range(2):
                lin_step("v_2", t, DT, False, W2, 2 * T, ("tok", V2, t, None), "split", part)
            if t == 0:
                rope_step(K2[:, 7, 0:T], 32, tab2[:, 0, :], tab2[:, 1, :], n_lin[0] - 3)
        roped_2 = n_rope[0]

        def head_da(h):
            made = []
            vh = [V2[:, i, h * 128:h * 128 + 128] for i in range(4)]
            for part in range(3):
                us = []
                for s in range(2):
                    qq = Q2[64 * s:64 * s + 64, h, :]
                    kk_ = K2[64 * s:64 * s + 64, h, :]
                    if part < 2:
                        segs = [(0, 512, None)]
                        mm = [(0, 512, qq[:, part * 128:part * 128 + 128], kk_, True, True)]
                    else:
                        segs = [(0, 256, None), (256, 256, None)]
                        mm = [(i * 256, 256, qq[:, 256 + i * 128:384 + i * 128], kk_[:, 256:512], True, True)
                              for i in range(2)]
                    us.append({"segs": segs, "scale": DA_HD ** -0.5, "rt": None, "mm": mm, "need_g": stage_last["v_2"],
                               "need_rope": roped_2})
                if part < 2:
                    blocks = [(kt * 128, kt * 128) for kt in range(4)]
                    copies = [(slice(0, 512), wideT[:, h % 2, :, part * 128:part * 128 + 128], None)]
                else:
                    blocks = [(0, 0), (128, 256), (256, 128), (384, 384)]
                    copies = [(slice(0, 512), wideT[:, h % 2, 2:4, 256:512], None)]
                pv = []
                if part == 2:
                    for n, kt in enumerate((2, 3, 0, 1)):
                        w = 512 if kt >= 2 else 256
                        pv.append((0, w, vh[kt], wideT[:, h % 2, kt, 0:w], n == 0, n == 3))
                made.append({"units": us, "blocks": blocks, "out": (0, 128), "pv": pv, "copies": copies, "head": h,
                             "first": True, "last": True, "evac": ("copy", Q2[:, h, :], 512)})
            return made

        attention([c for h in range(DA_HEADS) for c in head_da(h)], lambda: None)
        heads_2 = len(groups)
        sub = []
        for h in range(DA_HEADS):
            N = new_norm(P, 512)
            sub.append(N)
            sq_step(N, 0, Q2[:, h, :], 1, ("heads", heads_2 - DA_HEADS + h + 1))
            rt_step(N)

        def sub_apply(h):
            bc_step(sub[h])
            n_res[0] += 1
            steps.append(("headn", {"N": sub[h], "dst": Q2[:, h, :], "gain": ("subln", 0), "res_n": n_res[0]}))

        for t in range(8):
            sub_apply(t)
            lin_step("z_2", t, DT, True, W2, 2 * T, ("zgate", Q2, ZH, ZL))
        feat8("w_out0", operand(ZH, ZL), ("act", Y2), 2 * T)
        NY = [new_norm(D, T), new_norm(D, T)]
        for st in range(2):
            for k in range(DT):
                sq_step(NY[st], k, Y2[:, k, st * T:(st + 1) * T], DT, ("g", n_lin[0] - 1))
            rt_step(NY[st])

        NQ = [new_norm(D, T), new_norm(D, T)]
        ops3 = []
        for st in range(2):
            res = XC if st else X2
            bc_step(NY[st])
            for k in range(DT):
                r = post_step(NY[st], 0, st, Y2[:, k, st * T:(st + 1) * T], res, k)
                sq_step(NQ[st], k, res[:, k, :], DT, ("res", r))
            rt_step(NQ[st])
            bc_step(NQ[st])
            shift_step(NQ[st], 1, st, res, W3H, W3L)
            ops3.append([n_op[0] - DT + k + 1 for k in range(DT)])
        W3x = operand(W3H, W3L, False, ops3[0])
        W3 = operand(W3H, W3L, True, ops3[1])
        q_norms = [new_norm(P, T) for _ in range(GQ_HEADS)]
        k_norms = [new_norm(P, 2 * T) for _ in range(GQ_KV)]

        def q_tile(t):
            lin_step("q_3", t, DT, True, W3x, T, ("qk3", QB, ("qk_g", 0), q_norms[t]))
            return steps[-1][1]["sq"], q_norms[t], n_lin[0] - 1

        late = None

        def finish(late):
            steps.append(("sqmm", late[0]))
            rt_step(late[1])
            if late[2] is not None:
                rope_step(QB[:, late[0]["t"], :], 64, tab2[:, 2, :], tab2[:, 3, :], late[2])

        for t in range(GQ_HEADS):
            now = q_tile(t)
            now[0]["t"] = t
            if late:
                finish(late)
            late = now
        for t in range(GQ_KV):
            lin_step("k_3", t, DT, True, W3, 2 * T, ("qk3", KB, ("qk_g", 1), k_norms[t]))
            finish(late)
            late = (lin_sq[0], k_norms[t], None)
        for part in range(2):
            lin_step("v_3", 0, DT, False, W3, 2 * T, ("tok", VB, 0, None), "split", part)
            if part == 0:
                finish(late)
        for t in range(GQ_KV):
            bc_step(k_norms[t])
            n_res[0] += 1
            steps.append(("headn", {"N": k_norms[t], "dst": KB[:, t, :], "gain": None, "res_n": n_res[0]}))
            rope_step(KB[:, t, 0:T], 64, tab2[:, 2, :], tab2[:, 3, :], None, n_res[0])
        roped_3 = n_rope[0]

        def head_gq(h):
            kv_ = h // (GQ_HEADS // GQ_KV)
            made = []
            for part in range(2):
                u = {"segs": [(0, 512, None)], "scale": GQ_HD ** -0.5, "need_g": stage_last["v_3"], "need_rope": roped_3,
                     "rt": rt[:, q_norms[h]["n"], part:part + 1],
                     "mm": [(0, 512, QB[:, h, part * 128:part * 128 + 128], KB[:, kv_, :], True, True)]}
                pv = []
                if part == 1:
                    pv = [(0, 256, VB[:, kt, kv_ * 128:kv_ * 128 + 128], wideT[:, h % 2, kt, 0:256], kt == 0, kt == 3)
                          for kt in range(4)]
                made.append({"units": [u], "blocks": [(kt * 128, kt * 128) for kt in range(4)], "out": (0, 128),
                             "pv": pv, "copies": [(slice(0, 512), wideT[:, h % 2, :, part * 128:part * 128 + 128], None)],
                             "head": h, "first": True, "last": True, "evac": ("copy", QB[:, h, :], T)})
            return made

        attention([c for h in range(GQ_HEADS) for c in head_gq(h)], lambda: None)
        heads_3 = len(groups)
        feat8("z_3", W3x, ("zgate", QB, BH, BL))
        NZ = new_norm(D, T)
        for t in range(8):
            lin_step("w_out1", t, DT, True, operand(BH, BL), T, ("act", YB))
            sq_step(NZ, t, YB[:, t, :], DT, ("g", n_lin[0] - 1))
        rt_step(NZ)
        bc_step(NZ)
        for k in range(DT):
            last_res = post_step(NZ, 1, 0, YB[:, k, :], X2, k)
        splits = [t for t in tiles if t["kind"] == "split"]
        assert n_norm[0] <= 40
        done_groups = seen_rt = seen_bc = seen_c = 0
        for kind, s in steps:
            if kind in ("sq", "sqmm", "bc") or "bc" in s:
                (s["bc"] if "bc" in s else s).update(n_rt=seen_rt, n_bc=seen_bc)
            if kind == "rt":
                s["i"] = s["N"]["rti"] = seen_rt
                seen_rt += 1
            seen_bc += kind == "bc" or "bc" in s
            seen_c += kind == "transp"
            s["combos"] = seen_c
            s["groups"] = done_groups
            if kind == "values_out" and s["last"]:
                done_groups += 1
        seen_rt_q = q_norms[-1]["rti"] + 1
        w_out_pos = max(s["pos"] for k, s in steps if k == "lin" and s["stage"] == "w_out")

        def after_lin(eng, g):
            for b in range(NLIN):
                uses = len(range(b, g + 1, NLIN))
                if uses:
                    eng.wait_ge(lin_out[b], uses)

        def lin_done(eng, s):
            if s["kind"] == "ada":
                eng.wait_ge(ada_used, s["pieces"][0]["a"] + 1)
            elif s["part"] == 0:
                eng.wait_ge(half_done, s["half"])
            else:
                eng.wait_ge(w_used, s["pos"])

        def source_ready(eng, after, first):
            if after is None:
                eng.wait_ge(x_in, 16)
            elif after == "mem":
                eng.wait_ge(mem_in, 16)
            elif after == "ctx":
                eng.wait_ge(ctx_in, 16)
            elif after == "hg":
                eng.wait_ge(hg_out, 4)
            elif after[0] == "g":
                after_lin(eng, after[1])
            elif after[0] == "res":
                eng.wait_ge(res_ready, after[1])
            elif after[0] == "heads":
                eng.wait_ge(heads_out, after[1])

        def half_views(i):
            grp, r = divmod(i, ROUNDS)
            half = 1 << (r - 1)
            cutv = lambda a: a.rearrange("p h (b c) -> p (h b) c", c=2 * half)
            hs = slice(4 * grp, 4 * grp + 4)
            return half, cutv(decF[:, :, :]), cutv(decB[:, :, :]), cutv(qb[:, hs, :]), cutv(kh[:, hs, :]), \
                cutv(qk[i % 2][:, 0, :, :]), cutv(qk[i % 2][:, 1, :, :])

        def key_rounds(i):
            return sum(1 for j in range(i) if j % ROUNDS >= 2)

        def landed(eng, tile):
            eng.wait_ge(w_landed[tile["i"] % RAW], 16 * (tile["i"] // RAW + 1))

        def rot_free(eng, slot):
            if slot >= 2:
                kind, n = rot_uses[slot - 2]
                if kind == "rope":
                    eng.wait_ge(roped, n)
                elif kind == "z":
                    eng.wait_ge(gate_used, n)
                else:
                    eng.wait_ge(lin_out[n % NLIN], n // NLIN + 1)

        block = ctx.enter_context(nc.Block())

        @block.sync
        def _(sp):
            sp.dma_start(cols[:, :], dram["cols"]).then_inc(cols_in, 16)
            sp.dma_start(xT[:, :, :], dram["xT"]).then_inc(x_in, 16)
            for name, dst in (("positions", rot[:, 0, 0:T].bitcast(I32)), ("ident", ident[:, :]),
                              ("ones", ones[:, :]), ("causal", causal[:, :]), ("hmask", hmask[:, :, :])):
                sp.dma_start(dst, dram[name]).then_inc(const_in, 16)

            def load(tile):
                i = tile["i"]
                if i >= RAW:
                    old = tiles[i - RAW]
                    if old["kind"] == "split":
                        sp.wait_ge(w_hi_ready, old["s"] + 1)
                        sp.wait_ge(w_lo_ready, old["s"] + 1)
                    else:
                        sp.wait_ge(ada_used, old["a"] + 1)
                n = tile["n"] * P
                sp.dma_start(raw[:, i % RAW, 0:n], dram[tile["stage"]][tile["t"], :, tile["k"] * P:tile["k"] * P + n])\
                    .then_inc(w_landed[i % RAW], 16)

            for tile in tiles:
                load(tile)
            sp.wait_ge(res_ready, last_res)
            sp.dma_start(out_dram, X2[:, :, :]).then_inc(stored, 16)
            sp.wait_ge(stored, 16)

        @block.tensor
        def _(pe):
            seen_op = []

            def setup(s):
                pe.wait_ge(tables, 2)
                pe.wait_ge(ms_ready, 1)
                nc.tensor.matmul(sum_bank[:, 0:2], ones[0:64, :], lamt[0:64, 0:2], start=True, stop=True)\
                    .then_inc(tables_pe, 1)

            def linear(s):
                products(s)
                if "bc" in s:
                    bc(s["bc"])

            def products(s):
                g = s["g"]
                bank = lin[g % NLIN]
                if g >= NLIN:
                    pe.wait_ge(lin_out[g % NLIN], g // NLIN)
                if s["kind"] == "ada":
                    tile = s["pieces"][0]
                    landed(pe, tile)
                    pe.wait_ge(tables_act, 2)
                    for k in range(DT):
                        last = nc.tensor.matmul(bank[:, 0:2], raw[:, tile["i"] % RAW, k * P:(k + 1) * P],
                                                silu_c[:, k, :], start=(k == 0), stop=(k == DT - 1))
                    last.then_inc(ada_used, 1)
                    return
                if s["stage"] in ("br_attn", "wo_x"):
                    pe.wait_ge(heads_out, s["groups"])
                if s["stage"] == "w_out":
                    after_lin(pe, stage_last["br_hgrn"])
                if s["stage"] == "ffn_out":
                    after_lin(pe, stage_last["up"])
                if s["stage"] in ("w_out0", "w_out1"):
                    pe.wait_ge(gate_used, s["z"])
                op, W = s["op"], s["w"]
                H, L, wide = op["H"], op["L"], op["wide"]
                new = op["ops"] is not None and op not in seen_op
                if new:
                    seen_op.append(op)
                two_streams = len(H.shape) == 4

                def moving(X, k):
                    return (X[:, :, k, :] if wide else X[:, 0, k, :]) if two_streams else X[:, k, :]

                def tokens(X, k, tt):
                    if two_streams:
                        return X[:, tt // 2, k, tt % 2 * P:(tt % 2 + 1) * P]
                    return X[:, k, tt * P:(tt + 1) * P]

                for tile in s["pieces"]:
                    pe.wait_ge(w_hi_ready, tile["s"] + 1)
                    pe.wait_ge(w_lo_ready, tile["s"] + 1)
                    slot = tile["s"] % HL
                    if not s["feat"]:
                        continue
                    for k in range(tile["n"]):
                        wh = w_hi[:, slot, k * P:(k + 1) * P]
                        wl = w_lo[:, slot, k * P:(k + 1) * P]
                        kk = tile["k"] + k
                        first, final = kk == 0, kk == s["kts"] - 1
                        if new:
                            pe.wait_ge(op_ready, op["ops"][kk])
                        nc.tensor.matmul(bank[:, 0:W], wh, moving(H, kk), start=first, stop=False)
                        nc.tensor.matmul(bank[:, 0:W], wh, moving(L, kk), start=False, stop=False)
                        last = nc.tensor.matmul(bank[:, 0:W], wl, moving(H, kk), start=False, stop=final)
                    last.then_inc(w_used, 1)
                if s["feat"]:
                    return
                slot = s["first_slot"]
                tts = range(2) if s["part"] is None else range(2 * s["part"], 2 * s["part"] + 2)
                for tt in tts:
                    o = bank[:, tt % 2 * 2 * P:(tt % 2 + 1) * 2 * P]
                    for k in range(DT):
                        wh = w_hi[:, slot:slot + 2, k * P:(k + 1) * P]
                        wl = w_lo[:, slot:slot + 2, k * P:(k + 1) * P]
                        xh, xl = tokens(H, k, tt), tokens(L, k, tt)
                        nc.tensor.matmul(o, xh, wh, start=(k == 0), stop=False)
                        nc.tensor.matmul(o, xh, wl, start=False, stop=False)
                        last = nc.tensor.matmul(o, xl, wh, start=False, stop=(k == DT - 1))
                if s["part"] == 0:
                    last.then_inc(half_done, 1)
                else:
                    last.then_inc(w_used, 2)

            def sq(s):
                pe.wait_ge(sq_ready, s["m"] + 1)
                if s["k"] == 0:
                    pe.wait_ge(const_in, 80)
                    if s["n_rt"]:
                        pe.wait_ge(ms_ready, s["n_rt"])
                    if s["n_bc"]:
                        pe.wait_ge(rstd_ready, s["n_bc"])
                for tt in range(s["tts"]):
                    last = nc.tensor.matmul(sum_bank[:, 2 * tt:2 * tt + 2], sqr[:, s["m"] % 2, tt * P:(tt + 1) * P],
                                            ones[:, 0:2], start=(s["k"] == 0 and tt == 0),
                                            stop=(s["k"] == s["K"] - 1 and tt == s["tts"] - 1))
                last.then_inc(sq_used, 1)

            def bc(s):
                pe.wait_ge(diag_ready, s["r"] + 1)
                pe.wait_ge(ms_ready, s["n_rt"])
                if s["r"] == 0:
                    pe.wait_ge(tables_act, 3)
                if s["n_bc"]:
                    pe.wait_ge(rstd_ready, s["n_bc"])
                nc.tensor.matmul(sum_bank[:, 0:s["w"]], ones[:, :], diag[:, 0:s["tts"], :], start=True, stop=True)\
                    .then_inc(bc_ready, 1)

            def score(u):
                i = u["u"]
                if i >= 2:
                    pe.wait_ge(exped, i - 1)
                if i == A_HEADS:
                    pe.wait_ge(hg_out, 4)
                if "need_rope" in u:
                    pe.wait_ge(roped, u["need_rope"])
                after_lin(pe, u["need_g"])
                for c0, w, q_, k_, st, sp_ in u["mm"]:
                    last = nc.tensor.matmul(sc_bank[i % 2][:, c0:c0 + w], q_, k_, start=st, stop=sp_)
                last.then_inc(scored, 1)

            def transp(cb):
                c = cb["c"]
                pe.wait_ge(probs_ready, c + 1)
                if c:
                    pe.wait_ge(pt_ready, c)
                src = probs[:, cb["units"][-1]["u"] % 4, :]
                for c0, d0 in cb["blocks"]:
                    last = nc.tensor.transpose(pt_bank[:, d0:d0 + P], src[:, c0:c0 + P], ident[:, :])
                last.then_inc(transposed, 1)

            def values(cb):
                pe.wait_ge(pt_ready, cb["c"] + 1)
                if cb["first"] and cb["g0"]:
                    pe.wait_ge(heads_out, cb["g0"])
                r0, m = cb["out"]
                for c0, w, v_, b, st, sp_ in cb["pv"]:
                    moving = probsT[:, cb["c"] % 2, b[0]:b[0] + b[1]] if isinstance(b, tuple) else b
                    last = nc.tensor.matmul(o_bank[r0:r0 + m, c0:c0 + w], v_, moving, start=st, stop=sp_)
                last.then_inc(pv_done, 1)

            def hform(s):
                i, r = s["i"], s["r"]
                pe.wait_ge(hg_qk, i + 1)
                if r >= 2:
                    pe.wait_ge(hg_k, key_rounds(i) + 1)
                if i >= 2:
                    pe.wait_ge(hg_taken, i - 1)
                else:
                    pe.wait_ge(heads_out, att_a_groups)
                if s["grp"] == 1 and r == 1:
                    pe.wait_ge(hg_out, 2)
                banks = hg_banks[i % 2]
                for h in range(4):
                    hh = 4 * s["grp"] + h
                    qv = qk[i % 2][:, 0, h, :]
                    kv_ = kh[:, hh, :] if r < 2 else qk[i % 2][:, 1, h, :]
                    b = banks[h // 2]
                    o = (h % 2) * 256
                    if r <= LEVELS:
                        for tt in range(2):
                            last = nc.tensor.matmul(b[:, o + tt * P:o + (tt + 1) * P], kv_[:, tt * P:(tt + 1) * P],
                                                    qv[:, tt * P:(tt + 1) * P], start=True, stop=True)
                    else:
                        last = nc.tensor.matmul(b[:, o:o + P], kv_[:, 0:P], qv[:, P:2 * P], start=True, stop=True)
                last.then_inc(hg_scored, 1)

            def hvalues(s):
                grp = s["grp"]
                after_lin(pe, stage_last["g_b"])
                pe.wait_ge(hg_taken, (grp + 1) * (LEVELS + 2))
                for h in range(4):
                    hh = 4 * grp + h
                    b = sc_bank[h // 2]
                    o = (h % 2) * 256
                    v_ = [ib[:, i, hh * P:(hh + 1) * P] for i in range(2)]
                    nc.tensor.matmul(b[:, o:o + P], v_[0], probs[:, h // 2, o:o + P], start=True, stop=True)
                    nc.tensor.matmul(b[:, o + P:o + 2 * P], v_[0], probs[:, 2, h * P:(h + 1) * P], start=True, stop=False)
                    last = nc.tensor.matmul(b[:, o + P:o + 2 * P], v_[1], probs[:, h // 2, o + P:o + 2 * P],
                                            start=False, stop=True)
                    if h % 2:
                        last.then_inc(hg_pv, 1)

            do = {"setup": setup, "lin": linear, "sq": sq, "sqmm": sq, "bc": bc, "score_mm": score, "transp": transp,
                  "values": values, "hform": hform, "hvalues": hvalues}
            for kind, s in steps:
                if kind in do:
                    do[kind](s)

        @block.gpsimd
        def _(pool):
            nc.gpsimd.memset(mhalf[:, :], -0.5).then_inc(pool_const, 1)
            pool.wait_ge(pool_const, 1)
            for kind, s in steps:
                if kind == "rt":
                    pool.wait_ge(ms_ready, s["i"] + 1)
                    n, w = s["n"], s["tts"]
                    nc.gpsimd.tensor_tensor(rt[:, n, 0:w], ms[:, n, 0:w], mhalf[:, 0:1].broadcast_to([P, w]), ALU.pow)\
                        .then_inc(rt_ready, 1)
                if kind == "load_mem":
                    pool.wait_ge(sq_ready, DT)
                    pool.wait_ge(op_ready, DT)
                    pool.dma_start(memT[:, :, :], dram["memT"]).then_inc(mem_in, 16)
                if kind == "load_again":
                    pool.wait_ge(hg_out, 4)
                    pool.dma_start(hres[:, :, :], dram["xT"]).then_inc(x_again, 16)
                    pool.dma_start(tab2[:, :, :], dram["tab2"]).then_inc(tab_in, 16)
                if kind == "load_ctx":
                    pool.wait_ge(w_used, w_out_pos)
                    pool.dma_start(XC[:, :, :], dram["ctxT"]).then_inc(ctx_in, 16)
                if kind == "hform" and s["r"] >= 2:
                    i, r = s["i"], s["r"]
                    pool.wait_ge(hg_dec, s["grp"] * LEVELS + r - 1)
                    pool.wait_ge(hg_scored, i - 1)
                    half, _f, Bv, _q, kv_, _qd, kd = half_views(i)
                    w = 2 * half if i < 4 else half
                    nc.gpsimd.tensor_tensor(kd[:, :, 0:w], kv_[:, :, 0:w], Bv[:, :, 0:w], ALU.mult).then_inc(hg_k, 1)

        @block.scalar
        def _(act):
            chained = [0]
            split_done = [0]
            scal = nc.scalar

            def chain(ins):
                chained[0] += 1
                ins.then_inc(act_chain, 1)
                act.wait_ge(act_chain, chained[0])

            def split(upto, stream):
                for i in range(split_done[0], min(upto, len(splits))):
                    tile = splits[i]
                    if tile["i"] >= stream + RAW - 1:
                        return
                    landed(act, tile)
                    if i >= HL:
                        act.wait_ge(w_used, i - HL + 1)
                    n = tile["n"] * P
                    scal.copy(w_hi[:, i % HL, 0:n], raw[:, tile["i"] % RAW, 0:n]).then_inc(w_hi_ready, 1)
                    split_done[0] = i + 1

            def setup(s):
                act.wait_ge(tables, 1)
                scal.activation(cs1[:, :, :], cs1[:, :, :], ACT.Sin).then_inc(tables_act, 1)
                for j, name in enumerate(("c", "c_ctx")):
                    ins = scal.activation(silu_c[:, :, j], colr(name), ACT.Silu)
                ins.then_inc(tables_act, 1)
                act.wait_ge(tables_pe, 1)
                scal.activation(lamt[:, 2:4], sum_bank[:, 0:2], ACT.Exp).then_inc(tables_act, 1)
                act.wait_ge(tables, 4)
                scal.activation(lbt[:, 1:3, :], lbt[:, 1:3, :], ACT.Exp).then_inc(tables_act, 1)

            def square(s, src, W):
                m = s["m"]
                if m >= 2:
                    act.wait_ge(sq_used, m - 1)
                dst = sqr[:, m % 2, 0:W]
                if len(src.shape) == 3:
                    dst = dst.rearrange("p (h t) -> p h t", h=src.shape[1])
                scal.activation(dst, src, ACT.Square).then_inc(sq_ready, 1)

            def sq(s):
                source_ready(act, s["after"], s["k"] == 0)
                square(s, s["src"], s["N"]["w"])

            def linear(s):
                g, ev, t, W = s["g"], s["evac"], s["t"], s["w"]
                bank = lin[g % NLIN]
                free = lin_out[g % NLIN]
                if ev[0] == "act":
                    lin_done(act, s)
                    scal.copy(ev[1][:, t, 0:W], bank[:, 0:W]).then_inc(free, 1)
                elif ev[0] == "tok":
                    lin_done(act, s)
                    cs = slice(t * P, (t + 2) * P)
                    if ev[3] is None:
                        a = 0 if s["part"] is None else 2 * s["part"]
                        scal.copy(ev[1][:, a:a + 2, cs], bank[:, :].rearrange("p (t n) -> p t n", t=2)).then_inc(free, 1)
                    else:
                        n = ev[3]["n"]
                        act.wait_ge(rt_ready, ev[3]["rti"] + 1)
                        for tt in range(2):
                            ins = scal.activation(ev[1][:, tt, cs], bank[:, tt * 2 * P:(tt + 1) * 2 * P], ACT.Copy,
                                                  scale=rt[:, n, tt:tt + 1])
                        ins.then_inc(free, 1)
                elif ev[0] == "silu":
                    after_lin(act, g)
                    r = rot[:, s["slot"] % 2, 0:W]
                    scal.activation(r, r, ACT.Silu).then_inc(silu_done, 1)
                elif ev[0] == "zgate":
                    lin_done(act, s)
                    rot_free(act, s["slot"])
                    scal.activation(rot[:, s["slot"] % 2, 0:W], bank[:, 0:W], ACT.Silu).then_inc(free, 1)
                elif ev[0] == "qk3":
                    lin_done(act, s)
                    square(s["sq"], bank[:, 0:W], W)
                    scal.activation(ev[1][:, t, 0:W], bank[:, 0:W], ACT.Copy, scale=col(*ev[2])).then_inc(free, 1)

            def gates_(s):
                after_lin(act, s["g"])
                for a in s["silu"]:
                    scal.activation(a[:, :, :], a[:, :, :], ACT.Silu).then_inc(gates_ready, 1)
                for a in s["sig"]:
                    scal.activation(a[:, :, :], a[:, :, :], ACT.Sigmoid).then_inc(gates_ready, 1)

            def gain(s):
                act.wait_ge(cols_in, 16)
                source_ready(act, "mem" if s["gain"] == "norm_mem" else s["after"], s["k"] == 0)
                if s["pos"]:
                    act.wait_ge(w_used, s["pos"])
                scal.activation(s["H"], s["src"], ACT.Copy, scale=col(s["gain"], s["k"])).then_inc(op_hi, 1)

            def shift(s):
                if s["pos"]:
                    act.wait_ge(w_used, s["pos"])
                for k in range(DT):
                    act.wait_ge(u_ready, s["u0"] + k + 1)
                    scal.activation(s["H"][:, s["st"], k, :], probs[:, k % 2, 0:T], ACT.Identity,
                                    bias=ada[:, 24 * s["layer"] + k, s["st"]:s["st"] + 1]).then_inc(op_hi, 1)

            def rope(s):
                if s["after_g"] is not None:
                    after_lin(act, s["after_g"])
                if s["after_res"]:
                    act.wait_ge(res_ready, s["after_res"])
                r, hf = s["slot"], s["half"]
                rot_free(act, r)
                for p0 in range(0, P, 2 * hf):
                    scal.mul(rot[p0:p0 + hf, r % 2, 0:T], s["dst"][p0 + hf:p0 + 2 * hf, :], -1.0)
                    ins = scal.copy(rot[p0 + hf:p0 + 2 * hf, r % 2, 0:T], s["dst"][p0:p0 + hf, :])
                ins.then_inc(rot_ready, 1)

            def score(u):
                i = u["u"]
                act.wait_ge(maxed, i + 1)
                if i >= 4:
                    act.wait_ge(transposed, units[i - 4]["c"] + 1)
                for j, (c0, w, mask) in enumerate(u["segs"]):
                    dst = probs[:, i % 4, c0:c0 + w]
                    ins = scal.activation(dst, dst if mask is not None else sc_bank[i % 2][:, c0:c0 + w], ACT.Exp,
                                          bias=stat[:, 0, i % 4, j:j + 1],
                                          scale=u["scale"] if u["rt"] is None else stat[:, 3, i % 4, 0:1],
                                          accum_out=stat[:, 1, i % 4, j:j + 1])
                ins.then_inc(exped, 1)

            def transp(cb):
                act.wait_ge(transposed, cb["c"] + 1)
                if cb["pvo"] >= 2:
                    act.wait_ge(pv_done, cb["pvo"] - 1)
                for src, dst, cs in cb["copies"]:
                    src = pt_bank[:, src]
                    if cs is not None:
                        dst = dst[:, cb["c"] % 2, cs]
                    else:
                        src = src.rearrange("p (a n) -> p a n", a=dst.shape[1])
                    scal.copy(dst, src).then_inc(pt_ready, 1)

            def hvalues(s):
                for j in range(2):
                    act.wait_ge(hg_pv, 2 * s["grp"] + j + 1)
                    a = 4 * s["grp"] + 2 * j
                    scal.copy(qb[:, a:a + 2, :], sc_bank[j][:, :].rearrange("p (h t) -> p h t", h=2))\
                        .then_inc(hg_out, 1)

            do = {"setup": setup, "lin": linear, "sq": sq, "gain": gain, "shift": shift, "score_exp": score,
                  "transp": transp, "rope": rope, "gates": gates_, "hvalues": hvalues}
            pos = stream = 0
            for kind, s in steps:
                if kind == "lin":
                    for tile in s["pieces"]:
                        split(pos + LOOK, tile["i"])
                        pos += tile["kind"] == "split"
                        stream = tile["i"] + 1
                else:
                    split(pos + LOOK, stream)
                if kind in do:
                    do[kind](s)

        @block.vector
        def _(dve):
            chained = [0]
            split_done = [0]
            vec = nc.vector

            def chain(ins):
                chained[0] += 1
                ins.then_inc(dve_chain, 1)
                dve.wait_ge(dve_chain, chained[0])

            def split(upto, stream):
                for i in range(split_done[0], min(upto, len(splits))):
                    tile = splits[i]
                    if tile["i"] >= stream + RAW - 1:
                        return
                    landed(dve, tile)
                    dve.wait_ge(w_hi_ready, i + 1)
                    if i >= HL:
                        dve.wait_ge(w_used, i - HL + 1)
                    n = tile["n"] * P
                    vec.tensor_sub(w_lo[:, i % HL, 0:n], raw[:, tile["i"] % RAW, 0:n],
                                   w_hi[:, i % HL, 0:n].bitcast(F32)).then_inc(w_lo_ready, 1)
                    split_done[0] = i + 1

            def setup(s):
                dve.wait_ge(const_in, 80)
                vec.tensor_scalar(lamt[:, 5:6], col("subln"), 1.0 - LAM_INIT, None, ALU.mult)
                chain(vec.tensor_copy(cs1[:, 0, :], rot[:, 0, 0:T].bitcast(I32)))
                chain(vec.tensor_scalar(rot[:, 1, 0:T], cs1[:, 0, :], col("invfreq"), None, ALU.mult))
                for j, shift in ((0, 0.25), (1, 0.0)):
                    ang, turns, dst = rot[:, 1, 0:T], rot[:, 1, T:2 * T], cs1[:, j, :]
                    chain(vec.tensor_scalar(turns, ang, 1 / TWO_PI, shift, ALU.mult, ALU.add))
                    chain(vec.tensor_scalar(turns, turns, ROUND, -ROUND, ALU.add, ALU.add))
                    chain(vec.scalar_tensor_tensor(dst, turns, -PI_A, ang, ALU.mult, ALU.add))
                    chain(vec.scalar_tensor_tensor(dst, turns, -PI_B, dst, ALU.mult, ALU.add))
                    chain(vec.scalar_tensor_tensor(dst, turns, -PI_C, dst, ALU.mult, ALU.add))
                    if j == 0:
                        chain(vec.tensor_scalar(dst, dst, math.pi / 2, None, ALU.add))
                    chain(vec.tensor_scalar(dst, dst, PI_F, -PI_F, ALU.min, ALU.max)) if j == 0 else \
                        vec.tensor_scalar(dst, dst, PI_F, -PI_F, ALU.min, ALU.max).then_inc(tables, 1)
                lam0 = COLS["lam"][0]
                lp = cols[0:64, lam0:lam0 + 4].rearrange("p (a b) -> p a b", b=2)
                vec.tensor_tensor(lamt[0:64, 0:2], lp[:, :, 0], lp[:, :, 1], ALU.mult).then_inc(tables, 1)
                l0 = cols[:, COLS["lb"][0]:COLS["lb"][0] + 8]
                l1 = cols[:, COLS["lb"][0] + 8:COLS["lb"][0] + 16]
                chain(vec.tensor_tensor(lbt[:, 0, :], l0, l1, ALU.max))
                vec.tensor_sub(lbt[:, 1, :], l0, lbt[:, 0, :]).then_inc(tables, 1)
                vec.tensor_sub(lbt[:, 2, :], l1, lbt[:, 0, :]).then_inc(tables, 1)
                dve.wait_ge(tables_act, 4)
                chain(vec.tensor_add(lbt[:, 0, :], lbt[:, 1, :], lbt[:, 2, :]))
                chain(vec.reciprocal(lbt[:, 0, :], lbt[:, 0, :]))
                chain(vec.tensor_mul(lbt[:, 0, :], lbt[:, 0, :], lbt[:, 1, :]))
                chain(vec.tensor_scalar(lbt[:, 3, :], lbt[:, 0, :], -1.0, 1.0, ALU.mult, ALU.add))
                chain(vec.tensor_sub(lamt[:, 4:5], lamt[:, 3:4], lamt[:, 2:3]))
                vec.tensor_scalar(lamt[:, 4:5], lamt[:, 4:5], -LAM_INIT, None, ALU.add).then_inc(tables, 1)

            def two_parts(H, L, src):
                chain(vec.tensor_copy(H, src))
                return vec.tensor_sub(L, src, H.bitcast(F32))

            def r_of(N, w):
                dve.wait_ge(rstd_ready, N["r"] + 1)
                return rstd[:, N["r"] % 2, 0:w]

            def linear(s):
                if "bc" in s:
                    bc(s["bc"])
                g, ev, t, W = s["g"], s["evac"], s["t"], s["w"]
                bank = lin[g % NLIN]
                free = lin_out[g % NLIN]
                if ev[0] in ("act", "tok", "qk3"):
                    return
                lin_done(dve, s)
                if ev == "ada":
                    vec.tensor_scalar(ada[:, t, :], bank[:, 0:2], col("ada_b", t), None, ALU.add).then_inc(free, 1)
                elif ev[0] == "R":
                    vec.tensor_mul(ev[1][:, t, :], bank[:, 0:W], r_of(ev[2], W)).then_inc(free, 1)
                elif ev[0] == "silu":
                    rot_free(dve, s["slot"])
                    vec.tensor_mul(rot[:, s["slot"] % 2, 0:W], bank[:, 0:W], r_of(ev[2], W)).then_inc(free, 1)
                elif ev[0] == "up":
                    dve.wait_ge(silu_done, s["gate"])
                    r = rot[:, (s["slot"] - 1) % 2, 0:W]
                    chain(vec.tensor_mul(r, r, r_of(ev[2], W)))
                    chain(vec.tensor_mul(r, r, bank[:, 0:W]))
                    two_parts(FH[:, t, :], FL[:, t, :], r).then_inc(free, 1)
                elif ev[0] == "zgate":
                    O_, H, L = ev[1:]
                    after_lin(dve, g)
                    r = rot[:, s["slot"] % 2, 0:W]
                    chain(vec.tensor_mul(r, r, O_[:, t, 0:W]))
                    two_parts(H[:, t, :], L[:, t, :], r).then_inc(gate_used, 1)
                elif ev[0] == "gate_a":
                    dve.wait_ge(gates_ready, 5)
                    vec.tensor_mul(ga[:, t, :], ga[:, t, :], bank[:, 0:W]).then_inc(free, 1)
                elif ev[0] == "gate_b":
                    chain(vec.tensor_mul(gb[:, t, :], gb[:, t, :], bank[:, 0:W]))
                    chain(vec.tensor_add(gb[:, t, :], gb[:, t, :], ga[:, t, :]))
                    two_parts(GH[:, t, :], GL[:, t, :], gb[:, t, :]).then_inc(free, 1)
                elif ev[0] == "add":
                    dve.wait_ge(x_again, 16)
                    vec.tensor_add(ev[1][:, t, :], ev[1][:, t, :], bank[:, 0:W]).then_inc(free, 1)

            def rt_(s):
                w = s["tts"]
                dve.wait_ge(sq_used, s["N"]["m"])
                sums = sum_bank[:, 0:2 * w].rearrange("p (t two) -> p t two", two=2)[:, :, 0]
                vec.tensor_scalar(ms[:, s["n"], 0:w], sums, s["N"]["inv"], EPS, ALU.mult, ALU.add).then_inc(ms_ready, 1)

            def bc(s):
                N, w = s["N"], s["tts"]
                dve.wait_ge(rt_ready, N["rti"] + 1)
                if s["r"]:
                    dve.wait_ge(bc_ready, s["r"])
                dve.wait_ge(const_in, 80)
                r = rt[:, N["n"], 0:w].unsqueeze(2).broadcast_to([P, w, P])
                i_ = ident[:, :].unsqueeze(1).broadcast_to([P, w, P])
                vec.tensor_tensor(diag[:, 0:w, :], i_, r, ALU.mult).then_inc(diag_ready, 1)
                dve.wait_ge(bc_ready, s["r"] + 1)
                vec.tensor_copy(rstd[:, s["r"] % 2, 0:s["w"]], sum_bank[:, 0:s["w"]]).then_inc(rstd_ready, 1)

            def cosr(s):
                dve.wait_ge(tables_act, 1)
                r = rstd[:, 0, 0:T]
                dve.wait_ge(rstd_ready, 1)
                vec.tensor_mul(cs1[:, 0, :], cs1[:, 0, :], r)
                chain(vec.tensor_mul(cs1[:, 1, :], cs1[:, 1, :], r))

            def gain(s):
                dve.wait_ge(op_hi, s["hi"])
                vec.scalar_tensor_tensor(s["L"], s["src"], col(s["gain"], s["k"]), s["H"].bitcast(F32), ALU.mult,
                                         ALU.subtract).then_inc(op_ready, 1)

            def shift(s):
                r = r_of(s["N"], T)
                j0, st = 24 * s["layer"], s["st"]
                if s["pos"]:
                    dve.wait_ge(w_used, s["pos"])
                dve.wait_ge(transposed, s["combos"])
                after_lin(dve, g_ada)
                if s["op0"]:
                    dve.wait_ge(op_ready, s["op0"])
                chain(vec.tensor_scalar(coef[:, 0, :], ada[:, j0 + 8:j0 + 16, st], 1.0, None, ALU.add))
                chain(vec.tensor_mul(coef[:, 0, :], coef[:, 0, :], colr(f"pre{s['layer']}")))
                for k in range(DT + 1):
                    if k < DT:
                        if k >= 2:
                            dve.wait_ge(op_ready, s["op0"] + k - 1)
                        vec.scalar_tensor_tensor(probs[:, k % 2, 0:T], s["src"][:, k, :], coef[:, 0, k:k + 1], r,
                                                 ALU.mult, ALU.mult).then_inc(u_ready, 1)
                    if k:
                        j = k - 1
                        dve.wait_ge(op_hi, s["hi0"] + k)
                        vec.scalar_tensor_tensor(s["L"][:, st, j, :], probs[:, j % 2, 0:T], ada[:, j0 + j, st:st + 1],
                                                 s["H"][:, st, j, :].bitcast(F32), ALU.add, ALU.subtract)\
                            .then_inc(op_ready, 1)

            def post(s):
                k, st = s["k"], s["st"]
                r = r_of(s["N"], T)
                if k == 0:
                    after_lin(dve, stage_last["w_out1" if s["layer"] else "w_out0"])
                    j0 = 24 * s["layer"]
                    if s["res_n"] > 1:
                        dve.wait_ge(res_ready, s["res_n"] - 1)
                    dve.wait_ge(transposed, s["combos"])
                    chain(vec.tensor_mul(coef[:, 1, :], ada[:, j0 + 16:j0 + 24, st], colr(f"post{s['layer']}")))
                u = probs[:, 2 + k % 2, 0:T]
                chain(vec.scalar_tensor_tensor(u, s["y"], coef[:, 1, k:k + 1], r, ALU.mult, ALU.mult))
                vec.tensor_add(s["res"][:, k, :], s["res"][:, k, :], u).then_inc(res_ready, 1)

            def final(s):
                k = s["k"]
                if k == 0:
                    after_lin(dve, stage_last["ffn_out"])
                vec.scalar_tensor_tensor(X2[:, k, :], hres[:, k, :], col("final", k), r_of(s["N"], T), ALU.mult,
                                         ALU.mult).then_inc(res_ready, 1)

            def headn(s):
                w = s["N"]["w"]
                r = r_of(s["N"], w)
                if s["gain"] is None:
                    after_lin(dve, stage_last["k_3"])
                    vec.tensor_mul(s["dst"], s["dst"], r).then_inc(res_ready, 1)
                else:
                    dve.wait_ge(heads_out, heads_2)
                    vec.scalar_tensor_tensor(s["dst"], s["dst"], lamt[:, 5:6], r, ALU.mult, ALU.mult)\
                        .then_inc(res_ready, 1)
                dve.wait_ge(res_ready, s["res_n"])

            def hgate(s):
                pr = s["pr"]
                r = r_of(s["N"], 512)
                dve.wait_ge(hg_out, 4)
                for j in range(2):
                    h = 2 * pr + j
                    ins = vec.scalar_tensor_tensor(qb[:, h, :], qb[:, h, :], col("hgrn", h), r[:, j * T:(j + 1) * T],
                                                   ALU.mult, ALU.mult)
                chain(ins)
                two = slice(2 * pr, 2 * pr + 2)
                chain(vec.tensor_mul(qb[:, two, :], qb[:, two, :], og[:, two, :]))
                two_parts(HH[:, two, :], HLo[:, two, :], qb[:, two, :]).then_inc(op_ready, 1)

            def rope(s):
                r = rot[:, s["slot"] % 2, 0:T]
                dve.wait_ge(rot_ready, s["r"] + 1)
                if s["r"] >= roped_a:
                    dve.wait_ge(tab_in, 16)
                vec.tensor_mul(s["dst"], s["dst"], s["cos"])
                chain(vec.tensor_mul(r, r, s["sin"]))
                vec.tensor_add(s["dst"], s["dst"], r).then_inc(roped, 1)

            def score(u):
                i = u["u"]
                dve.wait_ge(scored, i + 1)
                if i >= 4:
                    dve.wait_ge(transposed, units[i - 4]["c"] + 1)
                for j, (c0, w, mask) in enumerate(u["segs"]):
                    src = sc_bank[i % 2][:, c0:c0 + w]
                    m = stat[:, 0, i % 4, j:j + 1]
                    if mask is not None:
                        ins = vec.tensor_tensor_reduce(probs[:, i % 4, c0:c0 + w], src, mask, 1.0, NEG,
                                                       ALU.add, ALU.max, m)
                    else:
                        ins = vec.reduce_max(m, src, AX_X)
                chain(ins)
                k = len(u["segs"])
                m = stat[:, 0, i % 4, 0:k]
                if u["rt"] is None:
                    vec.tensor_scalar(m, m, -u["scale"], None, ALU.mult).then_inc(maxed, 1)
                else:
                    dve.wait_ge(rt_ready, seen_rt_q)
                    vec.tensor_scalar(stat[:, 3, i % 4, 0:1], u["rt"], u["scale"], None, ALU.mult)
                    vec.tensor_scalar(m, m, -u["scale"], u["rt"], ALU.mult, ALU.mult).then_inc(maxed, 1)

            def prob(cb):
                us = cb["units"]
                dve.wait_ge(exped, us[-1]["u"] + 1)
                k = len(us[0]["segs"])
                for u in us:
                    i = u["u"] % 4
                    ins = vec.reciprocal(stat[:, 2, i, 0:k], stat[:, 1, i, 0:k])
                chain(ins)
                if len(us) == 2:
                    b = us[1]["u"] % 4
                    chain(vec.tensor_scalar(stat[:, 2, b, 0:k], stat[:, 2, b, 0:k], lamt[:, 4:5], None, ALU.mult))
                a = us[0]["u"] % 4
                for j, (c0, w, _m) in enumerate(us[0]["segs"]):
                    ins = vec.tensor_scalar(probs[:, a, c0:c0 + w], probs[:, a, c0:c0 + w], stat[:, 2, a, j:j + 1], None,
                                            ALU.mult)
                if len(us) == 2:
                    chain(ins)
                    for j, (c0, w, _m) in enumerate(us[0]["segs"]):
                        ins = vec.scalar_tensor_tensor(probs[:, b, c0:c0 + w], probs[:, b, c0:c0 + w],
                                                       stat[:, 2, b, j:j + 1], probs[:, a, c0:c0 + w], ALU.mult, ALU.add)
                ins.then_inc(probs_ready, 1)

            def values(cb):
                if not cb["last"]:
                    return
                dve.wait_ge(pv_done, cb["o"] + 1)
                ev = cb["evac"]
                if ev[0] == "split":
                    for H, L, cs in ev[1]:
                        ins = vec.tensor_copy(H, o_bank[:, cs])
                    chain(ins)
                    for H, L, cs in ev[1]:
                        ins = vec.tensor_sub(L, o_bank[:, cs], H.bitcast(F32))
                    ins.then_inc(heads_out, 1)
                else:
                    vec.tensor_copy(ev[1], o_bank[:, 0:ev[2]]).then_inc(heads_out, 1)

            def hprep(s):
                dve.wait_ge(gates_ready, 3)
                for h in range(B_HEADS):
                    ins = vec.tensor_scalar(fb[:, h, :], fb[:, h, :], lbt[:, 3, h:h + 1], lbt[:, 0, h:h + 1],
                                            ALU.mult, ALU.add)
                chain(ins)
                chain(vec.tensor_scalar(kh[:, :, :], fb[:, :, :], -1.0, 1.0, ALU.mult, ALU.add))

            def hform(s):
                i, r, grp = s["i"], s["r"], s["grp"]
                hs = slice(4 * grp, 4 * grp + 4)
                if i >= 2:
                    dve.wait_ge(hg_scored, i - 1)
                if i == 1:
                    after_lin(dve, g_br_attn)
                sc = P ** -0.5
                if r == 0:
                    vec.tensor_scalar(qk[i % 2][:, 0, :, :], qb[:, hs, :], sc, None, ALU.mult).then_inc(hg_qk, 1)
                    if i:
                        dve.wait_ge(hg_k, key_rounds(i))
                    chain(vec.tensor_copy(decF[:, :, :], fb[:, hs, :]))
                    chain(vec.memset(decB[:, :, :], 1.0))
                    return
                half, Fv, Bv, qv, kv_, qd, _kd = half_views(i)
                lo = 0 if i < 4 or r == 1 else half
                vec.scalar_tensor_tensor(qd[:, :, lo:2 * half], qv[:, :, lo:2 * half], sc, Fv[:, :, lo:2 * half],
                                         ALU.mult, ALU.mult).then_inc(hg_qk, 1)
                if r > LEVELS:
                    return
                nb = 4 * T // (2 * half)
                end1 = Fv[:, :, half - 1:half].broadcast_to([P, nb, half])
                end2 = Fv[:, :, 2 * half - 1:2 * half].broadcast_to([P, nb, half])
                if r >= 2:
                    dve.wait_ge(hg_k, key_rounds(i) + 1)
                chain(vec.tensor_mul(Bv[:, :, 0:half], Bv[:, :, 0:half], end2))
                dve.wait_ge(hg_qk, i + 1)
                vec.tensor_mul(Fv[:, :, half:2 * half], Fv[:, :, half:2 * half], end1).then_inc(hg_dec, 1)
                dve.wait_ge(hg_dec, grp * LEVELS + r)

            def htake(s):
                i, r, grp = s["i"], s["r"], s["grp"]
                if r == 0:
                    if grp == 1:
                        dve.wait_ge(hg_pv, 2)
                    else:
                        dve.wait_ge(transposed, s["combos"])
                    chain(vec.memset(probs[:, 0:2, :], 0.0))
                if i:
                    dve.wait_ge(hg_taken, i)
                dve.wait_ge(hg_scored, i + 1)
                banks = hg_banks[i % 2]
                for j in range(2):
                    if r <= LEVELS:
                        m = hmask[:, r - 1:r, :] if r else ident[:, :].bitcast(U32).rearrange("p (a n) -> p a n", a=1)
                        m = m.broadcast_to([P, 4, P])
                        ins = vec.copy_predicated(probs[:, j, :].rearrange("p (a n) -> p a n", n=P), m,
                                                  banks[j][:, :].rearrange("p (a n) -> p a n", n=P))
                    else:
                        ins = vec.tensor_copy(probs[:, 2, 2 * j * P:(2 * j + 2) * P].rearrange("p (a n) -> p a n", n=P),
                                              banks[j][:, :].rearrange("p (a n) -> p a n", n=2 * P)[:, :, 0:P])
                ins.then_inc(hg_taken, 1)

            do = {"setup": setup, "lin": linear, "rt": rt_, "bc": bc, "cosr": cosr, "gain": gain, "shift": shift,
                  "post": post, "final": final, "headn": headn, "hgate": hgate, "score_exp": score, "pscale": prob,
                  "values_out": values, "rope": rope, "hprep": hprep, "hform": hform, "htake": htake}
            pos = stream = 0
            for kind, s in steps:
                if kind == "lin":
                    for tile in s["pieces"]:
                        split(pos + LOOK, tile["i"])
                        pos += tile["kind"] == "split"
                        stream = tile["i"] + 1
                else:
                    split(pos + LOOK, stream)
                if kind in do:
                    do[kind](s)


def tiled(w):
    k, n = w.shape
    return np.ascontiguousarray(w.reshape(k // P, P, n // P, P).transpose(2, 1, 0, 3).reshape(n // P, P, k))


def feature_major(x):
    return np.ascontiguousarray(x.T.reshape(DT, P, -1).transpose(1, 0, 2))


def constants():
    p = np.arange(P)
    f32 = np.float32
    causal = np.zeros((P, 2 * P), f32)
    causal[:, P:] = np.where(p[None, :] > p[:, None], f32(NEG), f32(0))
    masks = np.zeros((P, LEVELS, P), np.uint32)
    for r in range(1, LEVELS + 1):
        half = 1 << (r - 1)
        s_, t_ = p[:, None], p[None, :]
        masks[:, r - 1] = (s_ // (2 * half) == t_ // (2 * half)) & (s_ // half % 2 == 0) & (t_ // half % 2 == 1)
    inv = np.power(f32(10000.0), -np.arange(0, A_HD, 2, dtype=f32) / f32(A_HD)).astype(f32)
    tab = np.zeros((P, 4, T), f32)
    tok = np.arange(T)
    for j, hd in ((0, DA_HD), (2, GQ_HD)):
        axis = hd // 2
        fr = np.power(f32(10000.0), -np.arange(0, axis, 2, dtype=f32) / f32(axis)).astype(f32)
        ang = np.concatenate([(tok // 64).astype(f32)[:, None] * fr, (tok % 64).astype(f32)[:, None] * fr], -1)
        ang = ang[:, p % (hd // 2)].T
        tab[:, j], tab[:, j + 1] = np.cos(ang), np.sin(ang)
    return {"causal": causal, "hmask": masks, "tab2": tab, "ident": np.eye(P, dtype=f32), "ones": np.ones((P, P), f32),
            "invfreq": inv[p % 32]}


def kernel(**inputs):
    import concourse.bacc as bacc
    from concourse.bass_utils import run_bass_kernel_spmd

    a = {k: np.asarray(v) for k, v in inputs.items()}
    const = constants()
    vec = np.zeros((P, NCOLS), np.float32)

    def put(name, rows):
        at, n = COLS[name]
        vec[:rows.shape[1], at:at + n] = rows.T

    for name, v in (("norm_mix", a["norm_mix_g"]), ("hgrn", a["hgrn_norm_g"]), ("norm_x", a["norm_x_g"]),
                    ("norm_mem", a["norm_mem_g"]), ("norm_ffn", a["norm_ffn_g"]), ("final", a["final_norm_g"]),
                    ("pre0", a["pre_g_2"][0]), ("pre1", a["pre_g_2"][1]), ("post0", a["post_g_2"][0]),
                    ("post1", a["post_g_2"][1]), ("c", a["c_2"]), ("c_ctx", a["c_ctx_2"]), ("ada_b", a["ada_b_2"]),
                    ("subln", a["a_subln_g_2"]), ("qk_g", a["b_qk_g_2"]), ("lb", a["hgrn_lb_logits"])):
        put(name, v.reshape(-1, P))
    put("lam", a["a_lambda_2"].reshape(4, DA_HD))
    put("invfreq", const.pop("invfreq").reshape(1, P))

    arrays = dict(const)
    arrays["cols"] = vec
    arrays["positions"] = np.ascontiguousarray(np.broadcast_to(a["positions"].reshape(1, T).astype(np.int32), (P, T)))
    arrays["xT"], arrays["memT"] = feature_major(a["x"][0]), feature_major(a["mem"][0])
    arrays["ctxT"] = feature_major(a["ctx_2"][0])
    stages = {"br_attn": a["w_br_attn"][0], "br_hgrn": a["w_br_hgrn"][0], "w_out": a["w_out"][0], "q_x": a["wq_x"][0],
              "wo_x": a["wo_x"][0], "ffn_out": a["w_ffn_out"][0], "w_out0": a["w_out_2"][0], "w_out1": a["w_out_2"][1]}

    def cut(w, names, widths):
        at = 0
        for n, c in zip(names, widths):
            stages[n] = w[:, at:at + c]
            at += c

    cut(a["w_in"][0], ("q_a", "k_a", "v_a", "q_b", "f_b", "i_b", "og_b", "g_a", "g_b"), [D] * 9)
    cut(a["wkv_x"][0], ("k_x", "v_x"), [D] * 2)
    cut(a["w_ffn_in"][0], ("gate", "up"), [FFN] * 2)
    cut(a["a_w_in_2"][0], ("q_2", "k_2", "v_2", "z_2"), [D] * 4)
    cut(a["b_w_in_2"][0], ("q_3", "k_3", "v_3", "z_3"), [D, GQ_KV * GQ_HD, GQ_KV * GQ_HD, D])
    arrays.update({n: tiled(w) for n, w in stages.items()})
    arrays["ada"] = np.concatenate([tiled(a["ada_w_2"][i]) for i in range(2)])

    nc = bacc.Bacc("TRN2", target_bir_lowering=False, num_devices=1)
    dram = {n: nc.dram_tensor(f"in_{n}", v.shape, mybir.dt.from_np(v.dtype), kind="ExternalInput").ap()
            for n, v in arrays.items()}
    out = nc.dram_tensor("out", (P, DT, T), F32, kind="ExternalOutput").ap()
    program(nc, dram, out)
    r = run_bass_kernel_spmd(nc, [{f"in_{n}": v for n, v in arrays.items()}], core_ids=[0])
    got = r.results[0]["out"]
    return np.ascontiguousarray(got.transpose(1, 0, 2).reshape(D, T).T).reshape(1, T, D)
```

```python
import math
from contextlib import ExitStack

import numpy as np

import concourse.bass as bass
from concourse import mybir

F32 = mybir.dt.float32
F32R = mybir.dt.float32r
I32 = mybir.dt.int32
U32 = mybir.dt.uint32
ALU = mybir.AluOpType
ACT = mybir.ActivationFunctionType
AX_X = mybir.AxisListType.X

P = 128
T = 256
D = 1024
DT = D // P
EPS = 1e-6
NEG = -1e30
FFN = 2816
FT = FFN // P
A_HEADS, A_HD = 16, 64
B_HEADS = 8
X_HEADS, X_HD = 4, 256
DA_HEADS, DA_HD = 8, 64
GQ_HEADS, GQ_KV, GQ_HD = 8, 2, 128
LAM_INIT = 0.8 - 0.6 * math.exp(-0.3 * 0)
ADA_TILES = 48
LEVELS = 7
TWO_PI = 2 * math.pi
PI_A = 6.28125
PI_B = float(np.float32(int((TWO_PI - PI_A) * 2 ** 20) / 2 ** 20))
PI_C = TWO_PI - PI_A - PI_B
ROUND = 1.5 * 2 ** 23
PI_F = 3.1415925

COLS = {}
_at = 0
for _name, _n in [("norm_mix", 8), ("hgrn", 8), ("norm_x", 8), ("norm_mem", 8), ("norm_ffn", 8),
                  ("final", 8), ("pre0", 8), ("pre1", 8), ("post0", 8), ("post1", 8), 
                  ("ada_b", 48), ("subln", 1), ("qk_g", 2), ("lb", 16), ("lam", 4), ("invfreq", 1)]:
    COLS[_name] = (_at, _n)
    _at += _n
NCOLS = _at

RAW, HL, LOOK = 7, 4, 3
NLIN = 3


def program(nc, dram, out_dram):
    ctx = ExitStack()
    with ctx:
        base = 16512
        SLAB = DT * T * 4
        at = [base]

        def place(name, shape, dt=F32, offset=None):
            n = int(np.prod(shape[1:])) * 4
            if offset is None:
                offset = at[0]
                at[0] += (n + 31) // 32 * 32
            return nc.alloc_sbuf_tensor_at(name, shape, dt, offset=offset)

        raw = place("w_raw", [P, RAW, DT * P])
        w_hi = place("w_hi", [P, HL, DT * P], F32R)
        w_lo = place("w_lo", [P, HL, DT * P], F32R)
        slab0 = at[0]
        at[0] += 14 * SLAB

        def slab(name, i, shape, dt=F32, extra=0):
            return place(name, [P] + shape, dt, slab0 + i * SLAB + extra)

        probs = place("probs", [P, 4, 512])
        probsT = place("probsT", [P, 2, 512])
        rot = place("rot", [P, 2, 512])
        rstd = place("rstd", [P, 2, 512])
        sqr = place("sqr", [P, 2, 512])
        diag = place("diag", [P, 4, P])
        ms = place("ms", [P, 40, 4])
        rt = ms
        mhalf = place("mhalf", [P, 1])
        ident = place("ident", [P, P])
        ones = place("ones", [P, P])
        causal = place("causal", [P, 2 * P])
        hmask_at = at[0]
        hmask = place("hmask", [P, LEVELS, P], U32)
        tab2 = place("tab2", [P, 4, T], F32, hmask_at)
        cs1 = place("cs1", [P, 2, T])
        cols = place("cols", [P, NCOLS])
        ada = place("ada", [P, 48, 2])
        stat = place("stat", [P, 4, 4, 2])
        lbt = place("lbt", [P, 4, 8])
        lamt = place("lamt", [P, 6])
        coef = place("coef", [P, 4, 8])
        assert at[0] <= 229368, at[0]

        xT = slab("xT", 0, [DT, T])
        XH, XL = slab("XH", 1, [DT, T], F32R), slab("XL", 2, [DT, T], F32R)
        Q, K = slab("Q", 3, [DT, T]), slab("K", 4, [DT, T])
        V = slab("V", 5, [2, D])
        qb, fb, og = slab("qb", 6, [DT, T]), slab("fb", 7, [DT, T]), slab("og", 9, [DT, T])
        ib = slab("ib", 8, [2, D])
        ga, gb = slab("ga", 10, [DT, T]), slab("gb", 11, [DT, T])
        AH, AL = slab("AH", 12, [DT, T], F32R), slab("AL", 13, [DT, T], F32R)
        memT = slab("memT", 0, [DT, T])
        MH, ML = slab("MH", 1, [DT, T], F32R), slab("ML", 2, [DT, T], F32R)
        kh = slab("kh", 3, [DT, T])
        decF, decB = slab("decF", 4, [4, T]), slab("decB", 4, [4, T], F32, SLAB // 2)
        qk = [slab("qk0", 5, [2, 4, T]), slab("qk1", 12, [2, 4, T])]
        KX, VX = slab("KX", 13, [DT, T]), slab("VX", 0, [2, D])
        HH, HLo = slab("HH", 7, [DT, T], F32R), slab("HLo", 8, [DT, T], F32R)
        GH, GL = slab("GH", 1, [DT, T], F32R), slab("GL", 2, [DT, T], F32R)
        hres = slab("hres", 3, [DT, T])
        NH, NL = slab("NH", 5, [DT, T], F32R), slab("NL", 6, [DT, T], F32R)
        QX = slab("QX", 7, [DT, T])
        CH, CL = slab("CH", 8, [DT, T], F32R), slab("CL", 9, [DT, T], F32R)
        FH, FL = slab("FH", 7, [FT, T], F32R), slab("FL", 10, [FT, T], F32R)
        X2, XC = slab("X2", 0, [DT, T]), slab("XC", 1, [DT, T])
        WH, WL = slab("WH", 12, [2, DT, T], F32R), slab("WL", 3, [2, DT, T], F32R)
        silu_c = slab("silu_c", 2, [2, D])
        prods = [slab("prod0", 4, [2, D]), slab("prod1", 5, [2, D])]
        wideT = [slab("wideT0", 2, [4, 512]), slab("wideT1", 5, [4, 512])]
        Q2, K2 = slab("Q2", 10, [DT, 2 * T]), slab("K2", 8, [DT, 2 * T])
        V2 = slab("V2", 6, [4, D])
        ZH, ZL = slab("ZH", 8, [DT, 2 * T], F32R), slab("ZL", 6, [DT, 2 * T], F32R)
        Y2 = slab("Y2", 12, [DT, 2 * T])
        QB = slab("QB", 10, [DT, T])
        KB = slab("KB", 11, [GQ_KV, 2 * T])
        VB = slab("VB", 11, [4, GQ_KV * GQ_HD], F32, SLAB // 2)
        BH, BL = slab("BH", 8, [DT, T], F32R), slab("BL", 9, [DT, T], F32R)
        YB = slab("YB", 12, [DT, T])
        W3H, W3L = slab("W3H", 6, [2, DT, T], F32R), slab("W3L", 3, [2, DT, T], F32R)

        def psum(name):
            return ctx.enter_context(nc.psum_tensor(name, [P, 512], F32))

        lin = [psum(f"lin{i}") for i in range(NLIN)]
        sc_bank = [psum("score0"), psum("score1")]
        pt_bank, o_bank, sum_bank = psum("pt_bank"), psum("o_bank"), psum("sum_bank")
        da_banks = [sc_bank[0], sc_bank[1], lin[1], lin[2]]
        hg_banks = [(sc_bank[0], sc_bank[1]), (pt_bank, o_bank)]

        def sem(name):
            return ctx.enter_context(nc.semaphore(name))

        w_landed = [sem(f"w_landed{i}") for i in range(RAW)]
        w_hi_ready, w_lo_ready = sem("w_hi_ready"), sem("w_lo_ready")
        w_used = sem("w_used")
        c_in, c_ready = sem("c_in"), sem("c_ready")
        ada_mul, ada_sum = sem("ada_mul"), sem("ada_sum")
        lin_out = [sem(f"lin_out{i}") for i in range(NLIN)]
        cols_in = sem("cols_in")
        pool_const = sem("pool_const")
        const_in, x_in, mem_in, x_again, ctx_in, tab_in = (sem(n) for n in
                                                            ("const_in", "x_in", "mem_in", "x_again", "ctx_in", "tab_in"))
        tables = sem("tables")
        tables_act = sem("tables_act")
        tables_pe = sem("tables_pe")
        sq_ready, sq_used = sem("sq_ready"), sem("sq_used")
        ms_ready, rt_ready = sem("ms_ready"), sem("rt_ready")
        diag_ready, bc_ready, rstd_ready = sem("diag_ready"), sem("bc_ready"), sem("rstd_ready")
        op_hi, op_ready = sem("op_hi"), sem("op_ready")
        u_ready = sem("u_ready")
        res_ready = sem("res_ready")
        half_done = sem("half_done")
        silu_done = sem("silu_done")
        hg_dec, hg_k = sem("hg_dec"), sem("hg_k")
        rot_ready, roped = sem("rot_ready"), sem("roped")
        scored, maxed, exped, probs_ready = (sem(n) for n in ("scored", "maxed", "exped", "probs_ready"))
        transposed, pt_ready, pv_done, heads_out = (sem(n) for n in ("transposed", "pt_ready", "pv_done", "heads_out"))
        gates_ready = sem("gates_ready")
        hg_qk, hg_scored, hg_taken, hg_att, hg_pv, hg_out = (sem(n) for n in
                                                             ("hg_qk", "hg_scored", "hg_taken", "hg_att", "hg_pv", "hg_out"))
        gate_used = sem("gate_used")
        dve_chain, act_chain = sem("dve_chain"), sem("act_chain")
        stored = sem("stored")

        def col(name, i=0):
            return cols[:, COLS[name][0] + i:COLS[name][0] + i + 1]

        def colr(name):
            a, n = COLS[name]
            return cols[:, a:a + n]

        steps = []
        tiles = []
        n_lin = [0]
        n_split = [0]
        n_z = [0]
        rot_uses = []
        stage_last = {}

        lin_of = {}
        pending = []
        defer = [False]

        def evac_pending():
            while pending:
                steps.append(("evac", pending.pop(0)))

        def lin_step(stage, t, kts, feat, op, width, evac, kind="split", part=None):
            pieces = []
            for tt in ([t] if feat else [t, t + 1]):
                k = 0
                while k < kts and part != 1:
                    n = min(DT, kts - k)
                    tile = {"stage": stage, "t": tt, "k": k, "n": n, "kind": kind, "i": len(tiles)}
                    tile["s"] = n_split[0]
                    n_split[0] += 1
                    tiles.append(tile)
                    pieces.append(tile)
                    k += n
            g = n_lin[0]
            n_lin[0] += 1
            stage_last[stage] = g
            slot = len(rot_uses)
            if evac[0] == "silu":
                rot_uses.append(("lin", g + 1))
                n_gate[0] += 1
            elif evac[0] == "zgate":
                n_z[0] += 1
                rot_uses.append(("z", n_z[0]))
            if part == 0:
                n_half[0] += 1
            pos = n_split[0]
            s = {"g": g, "pieces": pieces, "feat": feat, "op": op, "w": width, "evac": evac, "part": part,
                 "t": t, "stage": stage, "pos": pos, "kind": kind, "kts": kts, "half": n_half[0],
                 "slot": slot, "z": n_z[0], "gate": n_gate[0], "first_slot": None if feat or kind != "split" else (pos - 2) % HL}
            assert feat or (pos % 2 == 0)
            if evac[0] == "qk3":
                s["sq"] = new_sq(evac[3], 0, None, width // P, 1)
                lin_sq[0] = s["sq"]
            s["later"] = defer[0]
            steps.append(("lin", s))
            lin_of[stage, t] = g
            if defer[0]:
                pending.append(s)

        def operand(H, L, wide=False, ops=None):
            return {"H": H, "L": L, "wide": wide, "ops": ops}

        def new_norm(n_in, W):
            n = n_norm[0]
            n_norm[0] += 1
            return {"n": n, "inv": 1.0 / n_in, "w": W}

        def new_sq(N, k, src, tts, K):
            m = n_sq[0]
            n_sq[0] += 1
            N["m"] = n_sq[0]
            return {"N": N, "k": k, "src": src, "tts": tts, "K": K, "m": m}

        def sq_step(N, k, src, K=DT, after=None, kind="sq"):
            s = new_sq(N, k, src, N["w"] // P, K)
            s["after"] = after
            s["pos"] = n_split[0]
            if kind == "sq":
                steps.append(("sq", s))
                return
            if k:
                steps.append(("sqmm", N["late"]))
            N["late"] = s
            steps.append(("sqa", s))

        def rt_step(N):
            if "late" in N:
                steps.append(("sqmm", N["late"]))
            steps.append(("rt", {"N": N, "n": N["n"], "tts": N["w"] // P}))

        def bc_step(N):
            N["r"] = n_bc[0]
            n_bc[0] += 1
            steps.append(("bc", {"N": N, "n": N["n"], "r": N["r"], "tts": N["w"] // P, "w": N["w"]}))

        def bc_with(N):
            lin_s = steps[-1][1]
            bc_step(N)
            lin_s["bc"] = steps.pop()[1]

        def gain_step(k, src, gain, H, L, after=None):
            n_op[0] += 1
            n_hi[0] += 1
            steps.append(("gain", {"k": k, "src": src, "gain": gain, "H": H, "L": L, "after": after, "op": n_op[0],
                                   "hi": n_hi[0], "pos": n_split[0]}))

        biased = []

        def shift_step(N, layer, st, src, H, L):
            first = n_op[0]
            n_op[0] += DT
            n_hi[0] += DT
            steps.append(("shift", {"bias": layer not in biased, "ada_sums": 2 * ada_first[-1], "N": N, "layer": layer, "st": st, "src": src, "H": H, "L": L, "op0": first,
                                    "hi0": n_hi[0] - DT, "u0": n_u[0], "pos": n_split[0]}))
            n_u[0] += DT
            biased.append(layer)

        def post_step(N, layer, st, y, res, k):
            n_res[0] += 1
            steps.append(("post", {"N": N, "layer": layer, "st": st, "y": y, "res": res, "k": k, "res_n": n_res[0]}))
            return n_res[0]

        lin_sq = [None]
        n_norm, n_sq, n_bc, n_op, n_hi, n_u, n_res, n_gate, n_half = ([0] for _ in range(9))

        units = []
        combos = []
        groups = []
        n_rope = [0]

        def rope_step(dst, halves, cos, sin, after_g=None, after_res=None):
            steps.append(("rope", {"r": n_rope[0], "dst": dst, "half": halves, "cos": cos, "sin": sin,
                                   "after_g": after_g, "after_res": after_res, "slot": len(rot_uses)}))
            n_rope[0] += 1
            rot_uses.append(("rope", n_rope[0]))

        ada_tiles = []
        ada_summed = [0]

        def ada_flush():
            if ada_summed[0] < len(ada_tiles):
                steps.append(("adasum", ada_tiles[-1]))
                ada_summed[0] += 1

        def ada_some(k):
            for _ in range(k):
                n = len(ada_tiles)
                if n < ADA_TILES:
                    tile = {"stage": "ada", "t": n, "k": 0, "n": DT, "kind": "ada", "i": len(tiles), "a": n,
                            "prod": prods[ada_slab[0]], "first": n in ada_first, "pos": n_split[0]}
                    ada_flush()
                    tiles.append(tile)
                    ada_tiles.append(tile)
                    steps.append(("adamul", tile))
                    if n == ADA_TILES - 1:
                        ada_flush()

        ada_slab, ada_first = [0], [0]

        def attention(new_units, fill):
            todo = []
            for cb in new_units:
                cb["c"] = len(combos)
                combos.append(cb)
                for u in cb["units"]:
                    u["u"] = len(units)
                    u["c"] = cb["c"]
                    ring = da_banks if len(cb["units"]) == 2 else sc_bank
                    u["ring"], u["bank"] = len(ring), ring[u["u"] % len(ring)]
                    units.append(u)
                cb["pvo"], cb["g0"] = len(pvs), len(groups)
                if cb["pv"]:
                    cb["o"] = len(pvs)
                    pvs.append(cb)
                    if cb["last"]:
                        cb["grp"] = len(groups)
                        groups.append(cb)
                todo.append(cb)
            for u in todo[0]["units"]:
                steps.append(("score_mm", u))
                steps.append(("score_exp", u))
            prev = None
            for j, cb in enumerate(todo):
                steps.append(("pscale", cb))
                nxt = todo[j + 1]["units"] if j + 1 < len(todo) else []
                for u in nxt:
                    steps.append(("score_mm", u))
                for u in nxt:
                    steps.append(("score_exp", u))
                if prev is not None and prev["pv"]:
                    steps.append(("values", prev))
                fill()
                steps.append(("transp", cb))
                if prev is not None and prev["pv"]:
                    steps.append(("values_out", prev))
                prev = cb
            steps.append(("values", prev))
            steps.append(("values_out", prev))

        pvs = []

        NX = new_norm(D, T)
        ops = []
        for k in range(DT):
            gain_step(k, xT[:, k, :], "norm_mix", XH[:, k, :], XL[:, k, :])
            ops.append(n_op[0])
        for k in range(DT):
            sq_step(NX, k, xT[:, k, :])
        XW = operand(XH, XL, ops=ops)

        def feat8(stage, op, evac, width=T, kts=DT, fill=None):
            for t in range(8):
                lin_step(stage, t, kts, True, op, width, evac)
                if fill:
                    fill(t)

        for t in range(8):
            lin_step("q_a", t, DT, True, XW, T, ("act", Q))
            if t == 0:
                rt_step(NX)
                steps.append(("setup", {}))
            elif t == 1:
                bc_step(NX)
            elif t == 2:
                steps.append(("cosr", {}))
                for j in range(3):
                    rope_step(Q[:, j, :], 32, cs1[:, 0, :], cs1[:, 1, :], n_lin[0] - 1)
            else:
                rope_step(Q[:, t, :], 32, cs1[:, 0, :], cs1[:, 1, :], n_lin[0] - 1)
        steps.append(("load_mem", {}))
        for t in range(8):
            lin_step("k_a", t, DT, True, XW, T, ("act", K))
            if t:
                rope_step(K[:, t - 1, :], 32, cs1[:, 0, :], cs1[:, 1, :], n_lin[0] - 2)
        for t in range(0, 8, 2):
            lin_step("v_a", t, DT, False, XW, T, ("tok", V, t, NX))
            if t == 0:
                rope_step(K[:, 7, :], 32, cs1[:, 0, :], cs1[:, 1, :], n_lin[0] - 2)
        roped_a = n_rope[0]

        def head_a(h):
            j, r = h // 2, 64 * (h % 2)
            qh, kk_ = Q[r:r + 64, j, :], K[r:r + 64, j, :]
            u = {"segs": [(0, 128, causal[:, 128:256]), (128, 256, causal[:, :])], "scale": A_HD ** -0.5, "rt": None,
                 "mm": [(0, 128, qh[:, 0:128], kk_[:, 0:128], True, True),
                        (128, 256, qh[:, 128:256], kk_, True, True)],
                 "need_g": stage_last["v_a"], "need_rope": roped_a}
            vh = [V[:, i, h * 64:h * 64 + 64] for i in range(2)]
            return {"units": [u], "blocks": [(0, 0), (128, 128), (256, 256)], "out": (r, 64),
                    "copies": [(slice(0, 384), probsT, slice(0, 384))],
                    "pv": [(0, 256, vh[0], (0, 256), True, False), (128, 128, vh[1], (256, 128), False, True)],
                    "first": h % 2 == 0, "last": h % 2 == 1,
                    "evac": ("split", [(AH[:, j, :], AL[:, j, :], slice(0, T))])}

        todo = [(n, t, ("R", d, NX), True) for n, d in (("q_b", qb), ("f_b", fb)) for t in range(8)]
        todo += [("i_b", t, ("tok", ib, t, NX), False) for t in range(0, 8, 2)]
        todo += [(n, t, ("R", d, NX), True) for n, d in (("og_b", og), ("g_a", ga), ("g_b", gb)) for t in range(8)]

        def fill_w():
            for _ in range(3):
                if todo:
                    n, t, ev, feat = todo.pop(0)
                    lin_step(n, t, DT, feat, XW, T, ev)
                    if n == "og_b" and t == 7:
                        steps.append(("gates", {"g": n_lin[0] - 1, "sig": [fb], "silu": [qb, og]}))

        attention([head_a(h) for h in range(A_HEADS)], fill_w)
        while todo:
            fill_w()
        att_a_groups = len(groups)
        steps.append(("gates", {"g": n_lin[0] - 1, "sig": [ga, gb], "silu": []}))
        steps.append(("hprep", {}))

        NM = new_norm(D, T)
        br_ops = operand(AH, AL)
        for t in range(8):
            lin_step("br_attn", t, DT, True, br_ops, T, ("gate_a", None))
            sq_step(NM, t, memT[:, t, :], after="mem")
        rt_step(NM)
        g_br_attn = stage_last["br_attn"]
        ops = []
        for k in range(DT):
            gain_step(k, memT[:, k, :], "norm_mem", MH[:, k, :], ML[:, k, :])
            ops.append(n_op[0])
        MW = operand(MH, ML, ops=ops)
        kv = [("k_x", t, ("R", KX, NM), True) for t in range(8)] + [("v_x", t, ("tok", VX, t, NM), False) for t in range(0, 8, 2)]
        ROUNDS = LEVELS + 2

        def hform(i):
            steps.append(("hform", {"grp": i // ROUNDS, "r": i % ROUNDS, "i": i}))

        def hg_norm(pr):
            N = new_norm(P, 512)
            sq_step(N, 0, qb[:, 2 * pr:2 * pr + 2, :], 1, ("hg", 2 * (pr // 2) + 2))
            hg_norms.append(N)
            rt_step(N)

        hg_norms = []
        defer[0] = True
        hform(0)
        for i in range(2 * ROUNDS):
            if i + 1 < 2 * ROUNDS:
                hform(i + 1)
            steps.append(("htake", {"grp": i // ROUNDS, "r": i % ROUNDS, "i": i}))
            evac_pending()
            if kv:
                n, t, ev, feat = kv.pop(0)
                lin_step(n, t, DT, feat, MW, T, ev)
                if n == "k_x" and t == 0:
                    bc_with(NM)
            if i % ROUNDS == ROUNDS - 1:
                steps.append(("hvalues", {"grp": i // ROUNDS}))
            if i in (ROUNDS, ROUNDS + 1):
                hg_norm(i - ROUNDS)
            if i in (ROUNDS + 4, ROUNDS + 5):
                bc_step(hg_norms[i - ROUNDS - 4])
        evac_pending()
        defer[0] = False
        steps.append(("load_again", {}))
        hg_norm(2)
        hg_norm(3)
        ops = []
        for pr, N in enumerate(hg_norms):
            n_op[0] += 1
            steps.append(("hgate", {"N": N, "pr": pr}))
            ops += [n_op[0]] * 2
            if pr < 2:
                bc_step(hg_norms[pr + 2])
        feat8("br_hgrn", operand(HH, HLo, ops=ops), ("gate_b", None))

        def residual(stage, op, kts, gain, H, L, beside=None, ada_each=0):
            N = new_norm(D, T)
            ops = []
            for t in range(8):
                ada_some(ada_each * (t % 2))
                lin_step(stage, t, kts, True, op, T, ("add", hres))
                if t == 0 and beside:
                    beside()
                sq_step(N, t, hres[:, t, :], DT, ("g", lin_of[stage, t]), "late")
                if gain:
                    gain_step(t, hres[:, t, :], gain, H[:, t, :], L[:, t, :], ("g", n_lin[0] - 1))
                    ops.append(n_op[0])
            rt_step(N)
            return N, operand(H, L, ops=ops) if gain else None

        N3, op3 = residual("w_out", operand(GH, GL), DT, "norm_x", NH, NL)

        steps.append(("load_ctx", {}))

        q_todo = list(range(8))

        def q_x():
            lin_step("q_x", q_todo.pop(0), DT, True, op3, T, ("R", QX, N3))

        q_x()
        bc_with(N3)
        for _ in range(3):
            q_x()
        steps.append(("silu_c", {}))

        def head_x(h):
            u = {"segs": [(0, 256, None), (256, 256, None)], "scale": X_HD ** -0.5, "rt": None, "need_q": 2 * h + 1,
                 "mm": [(s * 256, 256, QX[:, 2 * h + k, s * 128:s * 128 + 128], KX[:, 2 * h + k, :], k == 0, k == 1)
                        for s in range(2) for k in range(2)]}
            pv = []
            for dv in range(2):
                for kt in range(2):
                    pv.append((dv * 256, 256, VX[:, kt, h * 256 + dv * 128:h * 256 + dv * 128 + 128],
                               (kt * 256, 256), kt == 0, kt == 1))
            return {"units": [u], "blocks": [(0, 0), (128, 256), (256, 128), (384, 384)], "out": (0, 128), "pv": pv,
                    "copies": [(slice(0, 512), probsT, slice(0, 512))], "first": True, "last": True,
                    "evac": ("split", [(CH[:, 2 * h + dv, :], CL[:, 2 * h + dv, :], slice(dv * 256, dv * 256 + 256))
                                       for dv in range(2)])}

        def fill_x():
            ada_some(1)
            if q_todo:
                q_x()
                q_x()

        attention([head_x(h) for h in range(X_HEADS)], fill_x)
        N4, op4 = residual("wo_x", operand(CH, CL), DT, "norm_ffn", NH, NL, ada_each=1)

        NP = [new_norm(D, T), new_norm(D, T)]
        for t in range(FT):
            ada_some(min(1, t % 4))
            lin_step("gate", t, DT, True, op4, T, ("silu", None, N4))
            if t == 0:
                bc_with(N4)
            lin_step("up", t, DT, True, op4, T, ("up", None, N4))
            if 4 <= t < 4 + DT:
                sq_step(NP[1], t - 4, XC[:, t - 4, :], DT, "ctx", "late")
            elif t == 4 + DT:
                rt_step(NP[1])
        ada_flush()
        ada_slab[0] = 1
        ada_first.append(len(ada_tiles))
        ops_c = []

        def ctx_norm():
            bc_step(NP[1])
            shift_step(NP[1], 0, 1, XC, WH, WL)
            ops_c.extend(n_op[0] - DT + k + 1 for k in range(DT))

        N5, _ = residual("ffn_out", operand(FH, FL), FT, None, None, None, ctx_norm)
        bc_step(N5)
        for k in range(DT):
            n_res[0] += 1
            steps.append(("final", {"N": N5, "k": k, "res_n": n_res[0]}))
            sq_step(NP[0], k, X2[:, k, :], DT, ("res", n_res[0]))
        rt_step(NP[0])

        bc_step(NP[0])
        shift_step(NP[0], 0, 0, X2, WH, WL)
        ops2 = [n_op[0] - DT + k + 1 for k in range(DT)]
        W2 = operand(WH, WL, True, ops2)
        for t in range(8):
            ada_some(1)
            lin_step("q_2", t, DT, True, W2, 2 * T, ("act", Q2))
            if t:
                rope_step(Q2[:, t - 1, 0:T], 32, tab2[:, 0, :], tab2[:, 1, :], n_lin[0] - 2)
        for t in range(8):
            ada_some(1)
            lin_step("k_2", t, DT, True, W2, 2 * T, ("act", K2))
            rope_step(K2[:, t - 1, 0:T] if t else Q2[:, 7, 0:T], 32, tab2[:, 0, :], tab2[:, 1, :], n_lin[0] - 2)
        for t in range(0, 8, 2):
            for part in range(2):
                ada_some(1)
                lin_step("v_2", t, DT, False, W2, 2 * T, ("tok", V2, t, None), "split", part)
            if t == 0:
                rope_step(K2[:, 7, 0:T], 32, tab2[:, 0, :], tab2[:, 1, :], n_lin[0] - 3)
        roped_2 = n_rope[0]
        ada_some(ADA_TILES)
        combo_da, unit_da = len(combos), len(units)

        def head_da(h):
            made = []
            vh = [V2[:, i, h * 128:h * 128 + 128] for i in range(4)]
            for part in range(3):
                us = []
                for s in range(2):
                    qq = Q2[64 * s:64 * s + 64, h, :]
                    kk_ = K2[64 * s:64 * s + 64, h, :]
                    if part < 2:
                        segs = [(0, 512, None)]
                        mm = [(0, 512, qq[:, part * 128:part * 128 + 128], kk_, True, True)]
                    else:
                        segs = [(0, 256, None), (256, 256, None)]
                        mm = [(i * 256, 256, qq[:, 256 + i * 128:384 + i * 128], kk_[:, 256:512], True, True)
                              for i in range(2)]
                    us.append({"segs": segs, "scale": DA_HD ** -0.5, "rt": None, "mm": mm, "need_g": stage_last["v_2"],
                               "need_rope": roped_2})
                if part < 2:
                    blocks = [(kt * 128, kt * 128) for kt in range(4)]
                    copies = [(slice(0, 512), wideT[h % 2][:, :, part * 128:part * 128 + 128], None)]
                else:
                    blocks = [(0, 0), (128, 256), (256, 128), (384, 384)]
                    copies = [(slice(0, 512), wideT[h % 2][:, 2:4, 256:512], None)]
                pv = []
                if part == 2:
                    for n, kt in enumerate((2, 3, 0, 1)):
                        w = 512 if kt >= 2 else 256
                        pv.append((0, w, vh[kt], wideT[h % 2][:, kt, 0:w], n == 0, n == 3))
                made.append({"units": us, "blocks": blocks, "out": (0, 128), "pv": pv, "copies": copies, "head": h,
                             "first": True, "last": True, "evac": ("copy", Q2[:, h, :], 512)})
            return made

        heads_before = len(groups)
        sub = []
        fills = [0]

        def sub_norm(h):
            N = new_norm(P, 512)
            sub.append(N)
            sq_step(N, 0, Q2[:, h, :], 1, ("heads", heads_before + h + 1), "late")

        def sub_apply(h):
            bc_step(sub[h])
            n_res[0] += 1
            steps.append(("headn", {"N": sub[h], "dst": Q2[:, h, :], "gain": ("subln", 0), "res_n": n_res[0],
                                    "heads": heads_before + h + 1}))

        def fill_da():
            h, part = divmod(fills[0], 3)
            fills[0] += 1
            if part == 0 and h >= 2:
                sub_apply(h - 2)
            elif part == 1 and h >= 1:
                sub_norm(h - 1)
            elif part == 2 and h >= 1:
                rt_step(sub[h - 1])

        attention([c for h in range(DA_HEADS) for c in head_da(h)], fill_da)
        sub_norm(DA_HEADS - 1)
        rt_step(sub[DA_HEADS - 1])
        sub_apply(DA_HEADS - 2)
        for t in range(8):
            lin_step("z_2", t, DT, True, W2, 2 * T, ("zgate", Q2, ZH, ZL))
            if t == 0:
                sub_apply(DA_HEADS - 1)
        NY = new_norm(D, 2 * T)
        for t in range(8):
            lin_step("w_out0", t, DT, True, operand(ZH, ZL), 2 * T, ("act", Y2))
            sq_step(NY, t, Y2[:, t, :], DT, ("g", n_lin[0] - 1), "late")
        rt_step(NY)

        NQ = [new_norm(D, T), new_norm(D, T)]
        ops3 = []

        def add_y(st, ks):
            res = XC if st else X2
            for k in ks:
                r = post_step(NY, 0, st, Y2[:, k, st * T:(st + 1) * T], res, k)
                sq_step(NQ[st], k, res[:, k, :], DT, ("res", r))
            if ks[-1] == DT - 1:
                rt_step(NQ[st])

        def norm_q(st):
            bc_step(NQ[st])
            shift_step(NQ[st], 1, st, XC if st else X2, W3H, W3L)
            ops3.append([n_op[0] - DT + k + 1 for k in range(DT)])

        bc_step(NY)
        add_y(0, range(DT))
        norm_q(0)
        W3x = operand(W3H, W3L, False, ops3[0])
        q_norms = [new_norm(P, T) for _ in range(GQ_HEADS)]
        k_norms = [new_norm(P, 2 * T) for _ in range(GQ_KV)]
        late = None

        def finish(late):
            if late is None:
                return
            steps.append(("sqmm", late["sq"]))
            rt_step(late["N"])
            if late["t"] is not None:
                rope_step(QB[:, late["t"], :], 64, tab2[:, 2, :], tab2[:, 3, :], late["g"])

        def q_tile(t):
            lin_step("q_3", t, DT, True, W3x, T, ("qk3", QB, ("qk_g", 0), q_norms[t]))
            finish(late)
            return {"sq": lin_sq[0], "N": q_norms[t], "g": n_lin[0] - 1, "t": t}

        for t in range(2):
            late = q_tile(t)
        finish(late)
        late = None
        add_y(1, range(DT))
        norm_q(1)
        W3 = operand(W3H, W3L, True, ops3[1])
        for t in range(2, 6):
            late = q_tile(t)
        for t in range(GQ_KV):
            lin_step("k_3", t, DT, True, W3, 2 * T, ("qk3", KB, ("qk_g", 1), k_norms[t]))
            finish(late)
            late = {"sq": lin_sq[0], "N": k_norms[t], "t": None}
        for t in range(6, 8):
            late = q_tile(t)
        finish(late)
        for t in range(GQ_KV):
            bc_step(k_norms[t])
            n_res[0] += 1
            steps.append(("headn", {"N": k_norms[t], "dst": KB[:, t, :], "gain": None, "res_n": n_res[0]}))
            rope_step(KB[:, t, 0:T], 64, tab2[:, 2, :], tab2[:, 3, :], None, n_res[0])
        for part in range(2):
            lin_step("v_3", 0, DT, False, W3, 2 * T, ("tok", VB, 0, None), "split", part)
        roped_3 = n_rope[0]

        def head_gq(h):
            kv_ = h // (GQ_HEADS // GQ_KV)
            made = []
            for part in range(2):
                u = {"segs": [(0, 512, None)], "scale": GQ_HD ** -0.5, "need_g": stage_last["v_3"], "need_rope": roped_3,
                     "rt": rt[:, q_norms[h]["n"], part:part + 1],
                     "mm": [(0, 512, QB[:, h, part * 128:part * 128 + 128], KB[:, kv_, :], True, True)]}
                pv = []
                if part == 1:
                    pv = [(0, 256, VB[:, kt, kv_ * 128:kv_ * 128 + 128], wideT[h % 2][:, kt, 0:256], kt == 0, kt == 3)
                          for kt in range(4)]
                made.append({"units": [u], "blocks": [(kt * 128, kt * 128) for kt in range(4)], "out": (0, 128),
                             "pv": pv, "copies": [(slice(0, 512), wideT[h % 2][:, :, part * 128:part * 128 + 128], None)],
                             "head": h, "first": True, "last": True, "evac": ("copy", QB[:, h, :], T)})
            return made

        attention([c for h in range(GQ_HEADS) for c in head_gq(h)], lambda: None)
        heads_3 = len(groups)
        feat8("z_3", W3x, ("zgate", QB, BH, BL))
        NZ = new_norm(D, T)
        for t in range(8):
            lin_step("w_out1", t, DT, True, operand(BH, BL), T, ("act", YB))
            sq_step(NZ, t, YB[:, t, :], DT, ("g", n_lin[0] - 1), "late")
        rt_step(NZ)
        bc_step(NZ)
        for k in range(DT):
            last_res = post_step(NZ, 1, 0, YB[:, k, :], X2, k)
        splits = [t for t in tiles if t["kind"] == "split"]
        assert n_norm[0] <= 40
        done_groups = seen_rt = seen_bc = seen_c = 0
        for kind, s in steps:
            if kind == "evac":
                continue
            if kind in ("sq", "sqmm", "bc") or "bc" in s:
                (s["bc"] if "bc" in s else s).update(n_rt=seen_rt, n_bc=seen_bc)
            if kind == "rt":
                s["i"] = s["N"]["rti"] = seen_rt
                seen_rt += 1
            seen_bc += kind == "bc" or "bc" in s
            seen_c += kind == "transp"
            s["combos"] = seen_c
            s["groups"] = done_groups
            if kind == "values_out" and s["last"]:
                done_groups += 1
        seen_rt_q = max(n["rti"] for n in q_norms + k_norms) + 1
        w_out_pos = max(s["pos"] for k, s in steps if k == "lin" and s["stage"] == "w_out")

        def after_lin(eng, g):
            for b in range(NLIN):
                uses = len(range(b, g + 1, NLIN))
                if uses:
                    eng.wait_ge(lin_out[b], uses)

        def lin_done(eng, s):
            if s["part"] == 0:
                eng.wait_ge(half_done, s["half"])
            else:
                eng.wait_ge(w_used, s["pos"])

        def source_ready(eng, after, first):
            if after is None:
                eng.wait_ge(x_in, 16)
            elif after == "mem":
                eng.wait_ge(mem_in, 16)
            elif after == "ctx":
                eng.wait_ge(ctx_in, 16)
            elif after[0] == "hg":
                eng.wait_ge(hg_out, after[1])
            elif after[0] == "g":
                after_lin(eng, after[1])
            elif after[0] == "res":
                eng.wait_ge(res_ready, after[1])
            elif after[0] == "heads":
                eng.wait_ge(heads_out, after[1])

        def half_views(i):
            grp, r = divmod(i, ROUNDS)
            half = 1 << (r - 1)
            cutv = lambda a: a.rearrange("p h (b c) -> p (h b) c", c=2 * half)
            hs = slice(4 * grp, 4 * grp + 4)
            return half, cutv(decF[:, :, :]), cutv(decB[:, :, :]), cutv(qb[:, hs, :]), cutv(kh[:, hs, :]), \
                cutv(qk[i % 2][:, 0, :, :]), cutv(qk[i % 2][:, 1, :, :])

        def key_rounds(i):
            return sum(1 for j in range(i) if j % ROUNDS >= 2)

        def landed(eng, tile):
            eng.wait_ge(w_landed[tile["i"] % RAW], 16 * (tile["i"] // RAW + 1))

        def rot_free(eng, slot):
            if slot >= 2:
                kind, n = rot_uses[slot - 2]
                if kind == "rope":
                    eng.wait_ge(roped, n)
                elif kind == "z":
                    eng.wait_ge(gate_used, n)
                else:
                    eng.wait_ge(lin_out[n % NLIN], n // NLIN + 1)

        block = ctx.enter_context(nc.Block())

        @block.sync
        def _(sp):
            sp.dma_start(cols[:, :], dram["cols"]).then_inc(cols_in, 16)
            sp.dma_start(xT[:, :, :], dram["xT"]).then_inc(x_in, 16)
            for name, dst in (("positions", rot[:, 0, 0:T].bitcast(I32)), ("ident", ident[:, :]),
                              ("ones", ones[:, :]), ("causal", causal[:, :]), ("hmask", hmask[:, :, :])):
                sp.dma_start(dst, dram[name]).then_inc(const_in, 16)

            def load(tile):
                i = tile["i"]
                if i >= RAW:
                    old = tiles[i - RAW]
                    if old["kind"] == "split":
                        sp.wait_ge(w_hi_ready, old["s"] + 1)
                        sp.wait_ge(w_lo_ready, old["s"] + 1)
                    else:
                        sp.wait_ge(ada_mul, 2 * old["a"] + 2)
                n = tile["n"] * P
                sp.dma_start(raw[:, i % RAW, 0:n], dram[tile["stage"]][tile["t"], :, tile["k"] * P:tile["k"] * P + n])\
                    .then_inc(w_landed[i % RAW], 16)

            for tile in tiles:
                load(tile)
            sp.wait_ge(res_ready, last_res)
            sp.dma_start(out_dram, X2[:, :, :]).then_inc(stored, 16)
            sp.wait_ge(stored, 16)

        @block.tensor
        def _(pe):
            seen_op = []

            def setup(s):
                pe.wait_ge(tables, 2)
                pe.wait_ge(ms_ready, 1)
                nc.tensor.matmul(sum_bank[:, 0:2], ones[0:64, :], lamt[0:64, 0:2], start=True, stop=True)\
                    .then_inc(tables_pe, 1)

            def linear(s):
                products(s)
                if "bc" in s:
                    bc(s["bc"])

            def products(s):
                g = s["g"]
                bank = lin[g % NLIN]
                if g >= NLIN:
                    pe.wait_ge(lin_out[g % NLIN], g // NLIN)
                if s["stage"] in ("br_attn", "wo_x"):
                    pe.wait_ge(heads_out, s["groups"])
                if s["stage"] == "z_2":
                    pe.wait_ge(exped, unit_da + 6 * DA_HEADS)
                if s["stage"] == "w_out":
                    after_lin(pe, stage_last["br_hgrn"])
                if s["stage"] == "ffn_out":
                    after_lin(pe, stage_last["up"])
                if s["stage"] in ("w_out0", "w_out1"):
                    pe.wait_ge(gate_used, s["z"])
                op, W = s["op"], s["w"]
                H, L, wide = op["H"], op["L"], op["wide"]
                new = op["ops"] is not None and op not in seen_op
                if new:
                    seen_op.append(op)
                two_streams = len(H.shape) == 4

                def moving(X, k):
                    return (X[:, :, k, :] if wide else X[:, 0, k, :]) if two_streams else X[:, k, :]

                def tokens(X, k, tt):
                    if two_streams:
                        return X[:, tt // 2, k, tt % 2 * P:(tt % 2 + 1) * P]
                    return X[:, k, tt * P:(tt + 1) * P]

                for tile in s["pieces"]:
                    pe.wait_ge(w_hi_ready, tile["s"] + 1)
                    pe.wait_ge(w_lo_ready, tile["s"] + 1)
                    slot = tile["s"] % HL
                    if not s["feat"]:
                        continue
                    for k in range(tile["n"]):
                        wh = w_hi[:, slot, k * P:(k + 1) * P]
                        wl = w_lo[:, slot, k * P:(k + 1) * P]
                        kk = tile["k"] + k
                        first, final = kk == 0, kk == s["kts"] - 1
                        if new:
                            pe.wait_ge(op_ready, op["ops"][kk])
                        nc.tensor.matmul(bank[:, 0:W], wh, moving(H, kk), start=first, stop=False)
                        nc.tensor.matmul(bank[:, 0:W], wh, moving(L, kk), start=False, stop=False)
                        last = nc.tensor.matmul(bank[:, 0:W], wl, moving(H, kk), start=False, stop=final)
                    last.then_inc(w_used, 1)
                if s["feat"]:
                    return
                slot = s["first_slot"]
                tts = range(2) if s["part"] is None else range(2 * s["part"], 2 * s["part"] + 2)
                for tt in tts:
                    o = bank[:, tt % 2 * 2 * P:(tt % 2 + 1) * 2 * P]
                    for k in range(DT):
                        wh = w_hi[:, slot:slot + 2, k * P:(k + 1) * P]
                        wl = w_lo[:, slot:slot + 2, k * P:(k + 1) * P]
                        xh, xl = tokens(H, k, tt), tokens(L, k, tt)
                        nc.tensor.matmul(o, xh, wh, start=(k == 0), stop=False)
                        nc.tensor.matmul(o, xh, wl, start=False, stop=False)
                        last = nc.tensor.matmul(o, xl, wh, start=False, stop=(k == DT - 1))
                if s["part"] == 0:
                    last.then_inc(half_done, 1)
                else:
                    last.then_inc(w_used, 2)

            def sq(s):
                pe.wait_ge(sq_ready, s["m"] + 1)
                if s["k"] == 0:
                    pe.wait_ge(const_in, 80)
                    if s["n_rt"]:
                        pe.wait_ge(ms_ready, s["n_rt"])
                    if s["n_bc"]:
                        pe.wait_ge(rstd_ready, s["n_bc"])
                for tt in range(s["tts"]):
                    last = nc.tensor.matmul(sum_bank[:, 2 * tt:2 * tt + 2], sqr[:, s["m"] % 2, tt * P:(tt + 1) * P],
                                            ones[:, 0:2], start=(s["k"] == 0 and tt == 0),
                                            stop=(s["k"] == s["K"] - 1 and tt == s["tts"] - 1))
                last.then_inc(sq_used, 1)

            def bc(s):
                pe.wait_ge(diag_ready, s["r"] + 1)
                pe.wait_ge(ms_ready, s["n_rt"])
                if s["r"] == 0:
                    pe.wait_ge(tables_act, 2)
                if s["n_bc"]:
                    pe.wait_ge(rstd_ready, s["n_bc"])
                nc.tensor.matmul(sum_bank[:, 0:s["w"]], ones[:, :], diag[:, 0:s["tts"], :], start=True, stop=True)\
                    .then_inc(bc_ready, 1)

            def score(u):
                i = u["u"]
                if i >= 2:
                    pe.wait_ge(exped, i - 1 if i < unit_da + 4 else i + 1 - u["ring"])
                if i == A_HEADS:
                    pe.wait_ge(hg_out, 4)
                if "need_rope" in u:
                    pe.wait_ge(roped, u["need_rope"])
                after_lin(pe, lin_of["q_x", u["need_q"]] if "need_q" in u else u["need_g"])
                for c0, w, q_, k_, st, sp_ in u["mm"]:
                    last = nc.tensor.matmul(u["bank"][:, c0:c0 + w], q_, k_, start=st, stop=sp_)
                last.then_inc(scored, 1)

            def transp(cb):
                c = cb["c"]
                pe.wait_ge(probs_ready, c + 1)
                if c:
                    pe.wait_ge(pt_ready, c)
                src = probs[:, cb["units"][-1]["u"] % 4, :]
                for c0, d0 in cb["blocks"]:
                    last = nc.tensor.transpose(pt_bank[:, d0:d0 + P], src[:, c0:c0 + P], ident[:, :])
                last.then_inc(transposed, 1)

            def values(cb):
                pe.wait_ge(pt_ready, cb["c"] + 1)
                if cb["first"] and cb["g0"]:
                    pe.wait_ge(heads_out, cb["g0"])
                r0, m = cb["out"]
                for c0, w, v_, b, st, sp_ in cb["pv"]:
                    moving = probsT[:, cb["c"] % 2, b[0]:b[0] + b[1]] if isinstance(b, tuple) else b
                    last = nc.tensor.matmul(o_bank[r0:r0 + m, c0:c0 + w], v_, moving, start=st, stop=sp_)
                last.then_inc(pv_done, 1)

            def hform(s):
                i, r = s["i"], s["r"]
                pe.wait_ge(hg_qk, i + 1)
                if r >= 2:
                    pe.wait_ge(hg_k, key_rounds(i) + 1)
                if i >= 2:
                    pe.wait_ge(hg_taken, i - 1)
                else:
                    pe.wait_ge(heads_out, att_a_groups)
                if s["grp"] == 1 and r == 1:
                    pe.wait_ge(hg_out, 2)
                banks = hg_banks[i % 2]
                for h in range(4):
                    hh = 4 * s["grp"] + h
                    qv = qk[i % 2][:, 0, h, :]
                    kv_ = kh[:, hh, :] if r < 2 else qk[i % 2][:, 1, h, :]
                    b = banks[h // 2]
                    o = (h % 2) * 256
                    if r <= LEVELS:
                        for tt in range(2):
                            last = nc.tensor.matmul(b[:, o + tt * P:o + (tt + 1) * P], kv_[:, tt * P:(tt + 1) * P],
                                                    qv[:, tt * P:(tt + 1) * P], start=True, stop=True)
                    else:
                        last = nc.tensor.matmul(b[:, o:o + P], kv_[:, 0:P], qv[:, P:2 * P], start=True, stop=True)
                last.then_inc(hg_scored, 1)

            def hvalues(s):
                grp = s["grp"]
                after_lin(pe, stage_last["g_b"])
                pe.wait_ge(hg_taken, (grp + 1) * (LEVELS + 2))
                for h in range(4):
                    hh = 4 * grp + h
                    b = sc_bank[h // 2]
                    o = (h % 2) * 256
                    v_ = [ib[:, i, hh * P:(hh + 1) * P] for i in range(2)]
                    nc.tensor.matmul(b[:, o:o + P], v_[0], probs[:, h // 2, o:o + P], start=True, stop=True)
                    nc.tensor.matmul(b[:, o + P:o + 2 * P], v_[0], probs[:, 2, h * P:(h + 1) * P], start=True, stop=False)
                    last = nc.tensor.matmul(b[:, o + P:o + 2 * P], v_[1], probs[:, h // 2, o + P:o + 2 * P],
                                            start=False, stop=True)
                    if h % 2:
                        last.then_inc(hg_pv, 1)

            do = {"setup": setup, "lin": linear, "sq": sq, "sqmm": sq, "bc": bc, "score_mm": score, "transp": transp,
                  "values": values, "hform": hform, "hvalues": hvalues}
            for kind, s in steps:
                if kind in do:
                    do[kind](s)

        @block.gpsimd
        def _(pool):
            nc.gpsimd.memset(mhalf[:, :], -0.5).then_inc(pool_const, 1)
            pool.wait_ge(pool_const, 1)
            for kind, s in steps:
                if kind == "rt":
                    pool.wait_ge(ms_ready, s["i"] + 1)
                    n, w = s["n"], s["tts"]
                    nc.gpsimd.tensor_tensor(rt[:, n, 0:w], ms[:, n, 0:w], mhalf[:, 0:1].broadcast_to([P, w]), ALU.pow)\
                        .then_inc(rt_ready, 1)
                if kind == "load_mem":
                    pool.wait_ge(sq_ready, DT)
                    pool.wait_ge(op_ready, DT)
                    pool.dma_start(memT[:, :, :], dram["memT"]).then_inc(mem_in, 16)
                if kind == "load_again":
                    pool.wait_ge(hg_out, 4)
                    pool.dma_start(hres[:, :, :], dram["xT"]).then_inc(x_again, 16)
                    pool.dma_start(tab2[:, :, :], dram["tab2"]).then_inc(tab_in, 16)
                if kind == "adamul":
                    a = s["a"]
                    landed(pool, s)
                    pool.wait_ge(c_ready, 1)
                    if s["first"]:
                        pool.wait_ge(w_used, s["pos"])
                    for st in range(2):
                        if a:
                            pool.wait_ge(ada_sum, 2 * a - 1 + st)
                        nc.gpsimd.tensor_tensor(s["prod"][:, st, :], raw[:, s["i"] % RAW, :], silu_c[:, st, :],
                                                ALU.mult).then_inc(ada_mul, 1)
                if kind == "load_ctx":
                    pool.wait_ge(w_used, w_out_pos)
                    pool.dma_start(silu_c[:, :, :], dram["c_rows"]).then_inc(c_in, 16)
                    pool.dma_start(XC[:, :, :], dram["ctxT"]).then_inc(ctx_in, 16)
                if kind == "hform" and s["r"] >= 2:
                    i, r = s["i"], s["r"]
                    pool.wait_ge(hg_dec, s["grp"] * LEVELS + r - 1)
                    pool.wait_ge(hg_scored, i - 1)
                    half, _f, Bv, _q, kv_, _qd, kd = half_views(i)
                    w = 2 * half if i < 4 else half
                    nc.gpsimd.tensor_tensor(kd[:, :, 0:w], kv_[:, :, 0:w], Bv[:, :, 0:w], ALU.mult).then_inc(hg_k, 1)

        @block.scalar
        def _(act):
            chained = [0]
            split_done = [0]
            scal = nc.scalar

            def chain(ins):
                chained[0] += 1
                ins.then_inc(act_chain, 1)
                act.wait_ge(act_chain, chained[0])

            def split(upto, stream):
                for i in range(split_done[0], min(upto, len(splits))):
                    tile = splits[i]
                    if tile["i"] >= stream + RAW - 3:
                        return
                    landed(act, tile)
                    if i >= HL:
                        act.wait_ge(w_used, i - HL + 1)
                    n = tile["n"] * P
                    scal.copy(w_hi[:, i % HL, 0:n], raw[:, tile["i"] % RAW, 0:n]).then_inc(w_hi_ready, 1)
                    split_done[0] = i + 1

            def setup(s):
                act.wait_ge(tables, 1)
                scal.activation(cs1[:, :, :], cs1[:, :, :], ACT.Sin).then_inc(tables_act, 1)
                act.wait_ge(tables_pe, 1)
                scal.activation(lamt[:, 2:4], sum_bank[:, 0:2], ACT.Exp).then_inc(tables_act, 1)
                act.wait_ge(tables, 4)
                scal.activation(lbt[:, 1:3, :], lbt[:, 1:3, :], ACT.Exp).then_inc(tables_act, 1)

            def silu_c_(s):
                act.wait_ge(c_in, 16)
                scal.activation(silu_c[:, :, :], silu_c[:, :, :], ACT.Silu).then_inc(c_ready, 1)

            def adasum(s):
                for st in range(2):
                    act.wait_ge(ada_mul, 2 * s["a"] + st + 1)
                    pr = s["prod"][:, st, :]
                    scal.activation(pr, pr, ACT.Copy, accum_out=ada[:, s["a"], st:st + 1]).then_inc(ada_sum, 1)

            def square(s, src, W):
                m = s["m"]
                if m >= 2:
                    act.wait_ge(sq_used, m - 1)
                dst = sqr[:, m % 2, 0:W]
                if len(src.shape) == 3:
                    dst = dst.rearrange("p (h t) -> p h t", h=src.shape[1])
                scal.activation(dst, src, ACT.Square).then_inc(sq_ready, 1)

            def sq(s):
                source_ready(act, s["after"], s["k"] == 0)
                square(s, s["src"], s["N"]["w"])

            def linear(s):
                g, ev, t, W = s["g"], s["evac"], s["t"], s["w"]
                bank = lin[g % NLIN]
                free = lin_out[g % NLIN]
                if ev[0] == "act":
                    lin_done(act, s)
                    scal.copy(ev[1][:, t, 0:W], bank[:, 0:W]).then_inc(free, 1)
                elif ev[0] == "tok":
                    lin_done(act, s)
                    cs = slice(t * P, (t + 2) * P)
                    if ev[3] is None:
                        a = 0 if s["part"] is None else 2 * s["part"]
                        scal.copy(ev[1][:, a:a + 2, cs], bank[:, :].rearrange("p (t n) -> p t n", t=2)).then_inc(free, 1)
                    else:
                        n = ev[3]["n"]
                        act.wait_ge(rt_ready, ev[3]["rti"] + 1)
                        for tt in range(2):
                            ins = scal.activation(ev[1][:, tt, cs], bank[:, tt * 2 * P:(tt + 1) * 2 * P], ACT.Copy,
                                                  scale=rt[:, n, tt:tt + 1])
                        ins.then_inc(free, 1)
                elif ev[0] == "silu":
                    after_lin(act, g)
                    r = rot[:, s["slot"] % 2, 0:W]
                    scal.activation(r, r, ACT.Silu).then_inc(silu_done, 1)
                elif ev[0] == "zgate":
                    lin_done(act, s)
                    rot_free(act, s["slot"])
                    scal.activation(rot[:, s["slot"] % 2, 0:W], bank[:, 0:W], ACT.Silu).then_inc(free, 1)
                elif ev[0] == "qk3":
                    lin_done(act, s)
                    square(s["sq"], bank[:, 0:W], W)
                    scal.activation(ev[1][:, t, 0:W], bank[:, 0:W], ACT.Copy, scale=col(*ev[2])).then_inc(free, 1)

            def gates_(s):
                after_lin(act, s["g"])
                for a in s["silu"]:
                    scal.activation(a[:, :, :], a[:, :, :], ACT.Silu).then_inc(gates_ready, 1)
                for a in s["sig"]:
                    scal.activation(a[:, :, :], a[:, :, :], ACT.Sigmoid).then_inc(gates_ready, 1)

            def gain(s):
                act.wait_ge(cols_in, 16)
                source_ready(act, "mem" if s["gain"] == "norm_mem" else s["after"], s["k"] == 0)
                if s["pos"]:
                    act.wait_ge(w_used, s["pos"])
                scal.activation(s["H"], s["src"], ACT.Copy, scale=col(s["gain"], s["k"])).then_inc(op_hi, 1)

            def shift(s):
                if s["pos"]:
                    act.wait_ge(w_used, s["pos"])
                for k in range(DT):
                    act.wait_ge(u_ready, s["u0"] + k + 1)
                    scal.activation(s["H"][:, s["st"], k, :], probs[:, k % 2, 0:T], ACT.Identity,
                                    bias=ada[:, 24 * s["layer"] + k, s["st"]:s["st"] + 1]).then_inc(op_hi, 1)

            def rope(s):
                if s["after_g"] is not None:
                    after_lin(act, s["after_g"])
                if s["after_res"]:
                    act.wait_ge(res_ready, s["after_res"])
                r, hf = s["slot"], s["half"]
                rot_free(act, r)
                for p0 in range(0, P, 2 * hf):
                    scal.mul(rot[p0:p0 + hf, r % 2, 0:T], s["dst"][p0 + hf:p0 + 2 * hf, :], -1.0)
                    ins = scal.copy(rot[p0 + hf:p0 + 2 * hf, r % 2, 0:T], s["dst"][p0:p0 + hf, :])
                ins.then_inc(rot_ready, 1)

            def score(u):
                i = u["u"]
                act.wait_ge(maxed, i + 1)
                if i >= 4:
                    act.wait_ge(transposed, units[i - 4]["c"] + 1)
                for j, (c0, w, mask) in enumerate(u["segs"]):
                    dst = probs[:, i % 4, c0:c0 + w]
                    ins = scal.activation(dst, dst if mask is not None else u["bank"][:, c0:c0 + w], ACT.Exp,
                                          bias=stat[:, 0, i % 4, j:j + 1],
                                          scale=u["scale"] if u["rt"] is None else stat[:, 3, i % 4, 0:1],
                                          accum_out=stat[:, 1, i % 4, j:j + 1])
                ins.then_inc(exped, 1)

            def transp(cb):
                act.wait_ge(transposed, cb["c"] + 1)
                if cb["pvo"] >= 2:
                    act.wait_ge(pv_done, cb["pvo"] - 1)
                if cb["c"] == combo_da:
                    act.wait_ge(ada_mul, 2 * ADA_TILES)
                    act.wait_ge(ada_sum, 2 * ADA_TILES)
                for src, dst, cs in cb["copies"]:
                    src = pt_bank[:, src]
                    if cs is not None:
                        dst = dst[:, cb["c"] % 2, cs]
                    else:
                        src = src.rearrange("p (a n) -> p a n", a=dst.shape[1])
                    scal.copy(dst, src).then_inc(pt_ready, 1)

            def hvalues(s):
                for j in range(2):
                    act.wait_ge(hg_pv, 2 * s["grp"] + j + 1)
                    a = 4 * s["grp"] + 2 * j
                    scal.copy(qb[:, a:a + 2, :], sc_bank[j][:, :].rearrange("p (h t) -> p h t", h=2))\
                        .then_inc(hg_out, 1)

            do = {"setup": setup, "lin": linear, "sq": sq, "sqa": sq, "gain": gain, "shift": shift, "score_exp": score,
                  "transp": transp, "rope": rope, "gates": gates_, "hvalues": hvalues,
                  "silu_c": silu_c_, "adasum": adasum}
            pos = stream = 0
            for kind, s in steps:
                if kind == "lin":
                    for tile in s["pieces"]:
                        split(pos + LOOK, tile["i"])
                        pos += tile["kind"] == "split"
                        stream = tile["i"] + 1
                else:
                    split(pos + LOOK, stream)
                    if kind == "adamul":
                        stream = s["i"] + 1
                if kind in do:
                    do[kind](s)

        @block.vector
        def _(dve):
            chained = [0]
            split_done = [0]
            vec = nc.vector

            def chain(ins):
                chained[0] += 1
                ins.then_inc(dve_chain, 1)
                dve.wait_ge(dve_chain, chained[0])

            def split(upto, stream):
                for i in range(split_done[0], min(upto, len(splits))):
                    tile = splits[i]
                    if tile["i"] >= stream + RAW - 3:
                        return
                    landed(dve, tile)
                    dve.wait_ge(w_hi_ready, i + 1)
                    if i >= HL:
                        dve.wait_ge(w_used, i - HL + 1)
                    n = tile["n"] * P
                    vec.tensor_sub(w_lo[:, i % HL, 0:n], raw[:, tile["i"] % RAW, 0:n],
                                   w_hi[:, i % HL, 0:n].bitcast(F32)).then_inc(w_lo_ready, 1)
                    split_done[0] = i + 1

            def setup(s):
                dve.wait_ge(const_in, 80)
                vec.tensor_scalar(lamt[:, 5:6], col("subln"), 1.0 - LAM_INIT, None, ALU.mult)
                chain(vec.tensor_copy(cs1[:, 0, :], rot[:, 0, 0:T].bitcast(I32)))
                chain(vec.tensor_scalar(rot[:, 1, 0:T], cs1[:, 0, :], col("invfreq"), None, ALU.mult))
                for j, shift in ((0, 0.25), (1, 0.0)):
                    ang, turns, dst = rot[:, 1, 0:T], rot[:, 1, T:2 * T], cs1[:, j, :]
                    chain(vec.tensor_scalar(turns, ang, 1 / TWO_PI, shift, ALU.mult, ALU.add))
                    chain(vec.tensor_scalar(turns, turns, ROUND, -ROUND, ALU.add, ALU.add))
                    chain(vec.scalar_tensor_tensor(dst, turns, -PI_A, ang, ALU.mult, ALU.add))
                    chain(vec.scalar_tensor_tensor(dst, turns, -PI_B, dst, ALU.mult, ALU.add))
                    chain(vec.scalar_tensor_tensor(dst, turns, -PI_C, dst, ALU.mult, ALU.add))
                    if j == 0:
                        chain(vec.tensor_scalar(dst, dst, math.pi / 2, None, ALU.add))
                    chain(vec.tensor_scalar(dst, dst, PI_F, -PI_F, ALU.min, ALU.max)) if j == 0 else \
                        vec.tensor_scalar(dst, dst, PI_F, -PI_F, ALU.min, ALU.max).then_inc(tables, 1)
                lam0 = COLS["lam"][0]
                lp = cols[0:64, lam0:lam0 + 4].rearrange("p (a b) -> p a b", b=2)
                vec.tensor_tensor(lamt[0:64, 0:2], lp[:, :, 0], lp[:, :, 1], ALU.mult).then_inc(tables, 1)
                l0 = cols[:, COLS["lb"][0]:COLS["lb"][0] + 8]
                l1 = cols[:, COLS["lb"][0] + 8:COLS["lb"][0] + 16]
                chain(vec.tensor_tensor(lbt[:, 0, :], l0, l1, ALU.max))
                vec.tensor_sub(lbt[:, 1, :], l0, lbt[:, 0, :]).then_inc(tables, 1)
                vec.tensor_sub(lbt[:, 2, :], l1, lbt[:, 0, :]).then_inc(tables, 1)
                dve.wait_ge(tables_act, 3)
                chain(vec.tensor_add(lbt[:, 0, :], lbt[:, 1, :], lbt[:, 2, :]))
                chain(vec.reciprocal(lbt[:, 0, :], lbt[:, 0, :]))
                chain(vec.tensor_mul(lbt[:, 0, :], lbt[:, 0, :], lbt[:, 1, :]))
                chain(vec.tensor_scalar(lbt[:, 3, :], lbt[:, 0, :], -1.0, 1.0, ALU.mult, ALU.add))
                chain(vec.tensor_sub(lamt[:, 4:5], lamt[:, 3:4], lamt[:, 2:3]))
                vec.tensor_scalar(lamt[:, 4:5], lamt[:, 4:5], -LAM_INIT, None, ALU.add).then_inc(tables, 1)

            def two_parts(H, L, src):
                chain(vec.tensor_copy(H, src))
                return vec.tensor_sub(L, src, H.bitcast(F32))

            def r_of(N, w):
                dve.wait_ge(rstd_ready, N["r"] + 1)
                return rstd[:, N["r"] % 2, 0:w]

            def linear(s):
                if not s["later"]:
                    evacuate(s)

            def evacuate(s):
                if "bc" in s:
                    bc(s["bc"])
                g, ev, t, W = s["g"], s["evac"], s["t"], s["w"]
                bank = lin[g % NLIN]
                free = lin_out[g % NLIN]
                if ev[0] in ("act", "tok", "qk3"):
                    return
                lin_done(dve, s)
                if ev[0] == "R":
                    vec.tensor_mul(ev[1][:, t, :], bank[:, 0:W], r_of(ev[2], W)).then_inc(free, 1)
                elif ev[0] == "silu":
                    rot_free(dve, s["slot"])
                    vec.tensor_mul(rot[:, s["slot"] % 2, 0:W], bank[:, 0:W], r_of(ev[2], W)).then_inc(free, 1)
                elif ev[0] == "up":
                    dve.wait_ge(silu_done, s["gate"])
                    r = rot[:, (s["slot"] - 1) % 2, 0:W]
                    chain(vec.tensor_mul(r, r, r_of(ev[2], W)))
                    chain(vec.tensor_mul(r, r, bank[:, 0:W]))
                    two_parts(FH[:, t, :], FL[:, t, :], r).then_inc(free, 1)
                elif ev[0] == "zgate":
                    O_, H, L = ev[1:]
                    after_lin(dve, g)
                    r = rot[:, s["slot"] % 2, 0:W]
                    chain(vec.tensor_mul(r, r, O_[:, t, 0:W]))
                    two_parts(H[:, t, :], L[:, t, :], r).then_inc(gate_used, 1)
                elif ev[0] == "gate_a":
                    dve.wait_ge(gates_ready, 5)
                    vec.tensor_mul(ga[:, t, :], ga[:, t, :], bank[:, 0:W]).then_inc(free, 1)
                elif ev[0] == "gate_b":
                    chain(vec.tensor_mul(gb[:, t, :], gb[:, t, :], bank[:, 0:W]))
                    chain(vec.tensor_add(gb[:, t, :], gb[:, t, :], ga[:, t, :]))
                    two_parts(GH[:, t, :], GL[:, t, :], gb[:, t, :]).then_inc(free, 1)
                elif ev[0] == "add":
                    dve.wait_ge(x_again, 16)
                    vec.tensor_add(ev[1][:, t, :], ev[1][:, t, :], bank[:, 0:W]).then_inc(free, 1)

            def rt_(s):
                w = s["tts"]
                dve.wait_ge(sq_used, s["N"]["m"])
                sums = sum_bank[:, 0:2 * w].rearrange("p (t two) -> p t two", two=2)[:, :, 0]
                vec.tensor_scalar(ms[:, s["n"], 0:w], sums, s["N"]["inv"], EPS, ALU.mult, ALU.add).then_inc(ms_ready, 1)

            def bc(s):
                N, w = s["N"], s["tts"]
                dve.wait_ge(rt_ready, N["rti"] + 1)
                if s["r"]:
                    dve.wait_ge(bc_ready, s["r"])
                dve.wait_ge(const_in, 80)
                r = rt[:, N["n"], 0:w].unsqueeze(2).broadcast_to([P, w, P])
                i_ = ident[:, :].unsqueeze(1).broadcast_to([P, w, P])
                vec.tensor_tensor(diag[:, 0:w, :], i_, r, ALU.mult).then_inc(diag_ready, 1)
                dve.wait_ge(bc_ready, s["r"] + 1)
                vec.tensor_copy(rstd[:, s["r"] % 2, 0:s["w"]], sum_bank[:, 0:s["w"]]).then_inc(rstd_ready, 1)

            def cosr(s):
                dve.wait_ge(tables_act, 1)
                r = rstd[:, 0, 0:T]
                dve.wait_ge(rstd_ready, 1)
                vec.tensor_mul(cs1[:, 0, :], cs1[:, 0, :], r)
                chain(vec.tensor_mul(cs1[:, 1, :], cs1[:, 1, :], r))

            def gain(s):
                dve.wait_ge(op_hi, s["hi"])
                vec.scalar_tensor_tensor(s["L"], s["src"], col(s["gain"], s["k"]), s["H"].bitcast(F32), ALU.mult,
                                         ALU.subtract).then_inc(op_ready, 1)

            def shift(s):
                r = r_of(s["N"], T)
                j0, st = 24 * s["layer"], s["st"]
                if s["pos"]:
                    dve.wait_ge(w_used, s["pos"])
                dve.wait_ge(transposed, s["combos"])
                if s["op0"]:
                    dve.wait_ge(op_ready, s["op0"])
                if s["bias"]:
                    dve.wait_ge(ada_sum, 2 * (j0 + 24))
                    b_ = colr("ada_b")[:, j0:j0 + 24].unsqueeze(2).broadcast_to([P, 24, 2])
                    chain(vec.tensor_tensor(ada[:, j0:j0 + 24, :], ada[:, j0:j0 + 24, :], b_, ALU.add))
                    dve.wait_ge(ada_sum, s["ada_sums"])
                chain(vec.tensor_scalar(coef[:, 0, :], ada[:, j0 + 8:j0 + 16, st], 1.0, None, ALU.add))
                chain(vec.tensor_mul(coef[:, 0, :], coef[:, 0, :], colr(f"pre{s['layer']}")))
                for k in range(DT + 1):
                    if k < DT:
                        if k >= 2:
                            dve.wait_ge(op_ready, s["op0"] + k - 1)
                        vec.scalar_tensor_tensor(probs[:, k % 2, 0:T], s["src"][:, k, :], coef[:, 0, k:k + 1], r,
                                                 ALU.mult, ALU.mult).then_inc(u_ready, 1)
                    if k:
                        j = k - 1
                        dve.wait_ge(op_hi, s["hi0"] + k)
                        vec.scalar_tensor_tensor(s["L"][:, st, j, :], probs[:, j % 2, 0:T], ada[:, j0 + j, st:st + 1],
                                                 s["H"][:, st, j, :].bitcast(F32), ALU.add, ALU.subtract)\
                            .then_inc(op_ready, 1)

            def post(s):
                k, st = s["k"], s["st"]
                r = r_of(s["N"], s["N"]["w"])[:, st * T:(st + 1) * T]
                if k == 0:
                    after_lin(dve, stage_last["w_out1" if s["layer"] else "w_out0"])
                    j0 = 24 * s["layer"]
                    if s["res_n"] > 1:
                        dve.wait_ge(res_ready, s["res_n"] - 1)
                    dve.wait_ge(transposed, s["combos"])
                    chain(vec.tensor_mul(coef[:, 1, :], ada[:, j0 + 16:j0 + 24, st], colr(f"post{s['layer']}")))
                u = probs[:, 2 + k % 2, 0:T]
                chain(vec.scalar_tensor_tensor(u, s["y"], coef[:, 1, k:k + 1], r, ALU.mult, ALU.mult))
                vec.tensor_add(s["res"][:, k, :], s["res"][:, k, :], u).then_inc(res_ready, 1)

            def final(s):
                k = s["k"]
                if k == 0:
                    after_lin(dve, stage_last["ffn_out"])
                vec.scalar_tensor_tensor(X2[:, k, :], hres[:, k, :], col("final", k), r_of(s["N"], T), ALU.mult,
                                         ALU.mult).then_inc(res_ready, 1)

            def headn(s):
                w = s["N"]["w"]
                r = r_of(s["N"], w)
                if s["gain"] is None:
                    after_lin(dve, stage_last["k_3"])
                    vec.tensor_mul(s["dst"], s["dst"], r).then_inc(res_ready, 1)
                else:
                    dve.wait_ge(heads_out, s["heads"])
                    vec.scalar_tensor_tensor(s["dst"], s["dst"], lamt[:, 5:6], r, ALU.mult, ALU.mult)\
                        .then_inc(res_ready, 1)
                dve.wait_ge(res_ready, s["res_n"])

            def hgate(s):
                pr = s["pr"]
                r = r_of(s["N"], 512)
                dve.wait_ge(hg_out, 4)
                for j in range(2):
                    h = 2 * pr + j
                    ins = vec.scalar_tensor_tensor(qb[:, h, :], qb[:, h, :], col("hgrn", h), r[:, j * T:(j + 1) * T],
                                                   ALU.mult, ALU.mult)
                chain(ins)
                two = slice(2 * pr, 2 * pr + 2)
                chain(vec.tensor_mul(qb[:, two, :], qb[:, two, :], og[:, two, :]))
                two_parts(HH[:, two, :], HLo[:, two, :], qb[:, two, :]).then_inc(op_ready, 1)

            def rope(s):
                r = rot[:, s["slot"] % 2, 0:T]
                dve.wait_ge(rot_ready, s["r"] + 1)
                if s["r"] >= roped_a:
                    dve.wait_ge(tab_in, 16)
                vec.tensor_mul(s["dst"], s["dst"], s["cos"])
                chain(vec.tensor_mul(r, r, s["sin"]))
                vec.tensor_add(s["dst"], s["dst"], r).then_inc(roped, 1)

            def score(u):
                i = u["u"]
                dve.wait_ge(scored, i + 1)
                if i >= 4:
                    dve.wait_ge(transposed, units[i - 4]["c"] + 1)
                for j, (c0, w, mask) in enumerate(u["segs"]):
                    src = u["bank"][:, c0:c0 + w]
                    m = stat[:, 0, i % 4, j:j + 1]
                    if mask is not None:
                        ins = vec.tensor_tensor_reduce(probs[:, i % 4, c0:c0 + w], src, mask, 1.0, NEG,
                                                       ALU.add, ALU.max, m)
                    else:
                        ins = vec.reduce_max(m, src, AX_X)
                chain(ins)
                k = len(u["segs"])
                m = stat[:, 0, i % 4, 0:k]
                if u["rt"] is None:
                    vec.tensor_scalar(m, m, -u["scale"], None, ALU.mult).then_inc(maxed, 1)
                else:
                    dve.wait_ge(rt_ready, seen_rt_q)
                    vec.tensor_scalar(stat[:, 3, i % 4, 0:1], u["rt"], u["scale"], None, ALU.mult)
                    vec.tensor_scalar(m, m, -u["scale"], u["rt"], ALU.mult, ALU.mult).then_inc(maxed, 1)

            def prob(cb):
                us = cb["units"]
                dve.wait_ge(exped, us[-1]["u"] + 1)
                k = len(us[0]["segs"])
                for u in us:
                    i = u["u"] % 4
                    ins = vec.reciprocal(stat[:, 2, i, 0:k], stat[:, 1, i, 0:k])
                chain(ins)
                if len(us) == 2:
                    b = us[1]["u"] % 4
                    chain(vec.tensor_scalar(stat[:, 2, b, 0:k], stat[:, 2, b, 0:k], lamt[:, 4:5], None, ALU.mult))
                a = us[0]["u"] % 4
                for j, (c0, w, _m) in enumerate(us[0]["segs"]):
                    ins = vec.tensor_scalar(probs[:, a, c0:c0 + w], probs[:, a, c0:c0 + w], stat[:, 2, a, j:j + 1], None,
                                            ALU.mult)
                if len(us) == 2:
                    chain(ins)
                    for j, (c0, w, _m) in enumerate(us[0]["segs"]):
                        ins = vec.scalar_tensor_tensor(probs[:, b, c0:c0 + w], probs[:, b, c0:c0 + w],
                                                       stat[:, 2, b, j:j + 1], probs[:, a, c0:c0 + w], ALU.mult, ALU.add)
                ins.then_inc(probs_ready, 1)

            def values(cb):
                if not cb["last"]:
                    return
                dve.wait_ge(pv_done, cb["o"] + 1)
                ev = cb["evac"]
                if ev[0] == "split":
                    for H, L, cs in ev[1]:
                        ins = vec.tensor_copy(H, o_bank[:, cs])
                    chain(ins)
                    for H, L, cs in ev[1]:
                        ins = vec.tensor_sub(L, o_bank[:, cs], H.bitcast(F32))
                    ins.then_inc(heads_out, 1)
                else:
                    vec.tensor_copy(ev[1], o_bank[:, 0:ev[2]]).then_inc(heads_out, 1)

            def hprep(s):
                dve.wait_ge(gates_ready, 3)
                for h in range(B_HEADS):
                    ins = vec.tensor_scalar(fb[:, h, :], fb[:, h, :], lbt[:, 3, h:h + 1], lbt[:, 0, h:h + 1],
                                            ALU.mult, ALU.add)
                chain(ins)
                chain(vec.tensor_scalar(kh[:, :, :], fb[:, :, :], -1.0, 1.0, ALU.mult, ALU.add))

            def hform(s):
                i, r, grp = s["i"], s["r"], s["grp"]
                hs = slice(4 * grp, 4 * grp + 4)
                if i >= 2:
                    dve.wait_ge(hg_scored, i - 1)
                if i == 1:
                    after_lin(dve, g_br_attn)
                sc = P ** -0.5
                if r == 0:
                    vec.tensor_scalar(qk[i % 2][:, 0, :, :], qb[:, hs, :], sc, None, ALU.mult).then_inc(hg_qk, 1)
                    if i:
                        dve.wait_ge(hg_k, key_rounds(i))
                        dve.wait_ge(hg_qk, i)
                    chain(vec.tensor_copy(decF[:, :, :], fb[:, hs, :]))
                    chain(vec.memset(decB[:, :, :], 1.0))
                    return
                half, Fv, Bv, qv, kv_, qd, _kd = half_views(i)
                lo = 0 if i < 4 or r == 1 else half
                vec.scalar_tensor_tensor(qd[:, :, lo:2 * half], qv[:, :, lo:2 * half], sc, Fv[:, :, lo:2 * half],
                                         ALU.mult, ALU.mult).then_inc(hg_qk, 1)
                if r > LEVELS:
                    return
                nb = 4 * T // (2 * half)
                end1 = Fv[:, :, half - 1:half].broadcast_to([P, nb, half])
                end2 = Fv[:, :, 2 * half - 1:2 * half].broadcast_to([P, nb, half])
                if r >= 2:
                    dve.wait_ge(hg_k, key_rounds(i) + 1)
                chain(vec.tensor_mul(Bv[:, :, 0:half], Bv[:, :, 0:half], end2))
                dve.wait_ge(hg_qk, i + 1)
                vec.tensor_mul(Fv[:, :, half:2 * half], Fv[:, :, half:2 * half], end1).then_inc(hg_dec, 1)
                dve.wait_ge(hg_dec, grp * LEVELS + r)

            def htake(s):
                i, r, grp = s["i"], s["r"], s["grp"]
                if r == 0:
                    if grp == 1:
                        dve.wait_ge(hg_pv, 2)
                    else:
                        dve.wait_ge(transposed, s["combos"])
                    chain(vec.memset(probs[:, 0:2, :], 0.0))
                if i:
                    dve.wait_ge(hg_taken, i)
                dve.wait_ge(hg_scored, i + 1)
                banks = hg_banks[i % 2]
                for j in range(2):
                    if r <= LEVELS:
                        m = hmask[:, r - 1:r, :] if r else ident[:, :].bitcast(U32).rearrange("p (a n) -> p a n", a=1)
                        m = m.broadcast_to([P, 4, P])
                        ins = vec.copy_predicated(probs[:, j, :].rearrange("p (a n) -> p a n", n=P), m,
                                                  banks[j][:, :].rearrange("p (a n) -> p a n", n=P))
                    else:
                        ins = vec.tensor_copy(probs[:, 2, 2 * j * P:(2 * j + 2) * P].rearrange("p (a n) -> p a n", n=P),
                                              banks[j][:, :].rearrange("p (a n) -> p a n", n=2 * P)[:, :, 0:P])
                ins.then_inc(hg_taken, 1)

            do = {"setup": setup, "lin": linear, "rt": rt_, "bc": bc, "cosr": cosr, "gain": gain, "shift": shift,
                  "post": post, "final": final, "headn": headn, "hgate": hgate, "score_exp": score, "pscale": prob,
                  "values_out": values, "rope": rope, "hprep": hprep, "hform": hform, "htake": htake, "evac": evacuate}
            pos = stream = 0
            for kind, s in steps:
                if kind == "lin":
                    for tile in s["pieces"]:
                        split(pos + LOOK, tile["i"])
                        pos += tile["kind"] == "split"
                        stream = tile["i"] + 1
                else:
                    split(pos + LOOK, stream)
                    if kind == "adamul":
                        stream = s["i"] + 1
                if kind in do:
                    do[kind](s)


def tiled(w):
    k, n = w.shape
    return np.ascontiguousarray(w.reshape(k // P, P, n // P, P).transpose(2, 1, 0, 3).reshape(n // P, P, k))


def feature_major(x):
    return np.ascontiguousarray(x.T.reshape(DT, P, -1).transpose(1, 0, 2))


def constants():
    p = np.arange(P)
    f32 = np.float32
    causal = np.zeros((P, 2 * P), f32)
    causal[:, P:] = np.where(p[None, :] > p[:, None], f32(NEG), f32(0))
    masks = np.zeros((P, LEVELS, P), np.uint32)
    for r in range(1, LEVELS + 1):
        half = 1 << (r - 1)
        s_, t_ = p[:, None], p[None, :]
        masks[:, r - 1] = (s_ // (2 * half) == t_ // (2 * half)) & (s_ // half % 2 == 0) & (t_ // half % 2 == 1)
    inv = np.power(f32(10000.0), -np.arange(0, A_HD, 2, dtype=f32) / f32(A_HD)).astype(f32)
    tab = np.zeros((P, 4, T), f32)
    tok = np.arange(T)
    for j, hd in ((0, DA_HD), (2, GQ_HD)):
        axis = hd // 2
        fr = np.power(f32(10000.0), -np.arange(0, axis, 2, dtype=f32) / f32(axis)).astype(f32)
        ang = np.concatenate([(tok // 64).astype(f32)[:, None] * fr, (tok % 64).astype(f32)[:, None] * fr], -1)
        ang = ang[:, p % (hd // 2)].T
        tab[:, j], tab[:, j + 1] = np.cos(ang), np.sin(ang)
    return {"causal": causal, "hmask": masks, "tab2": tab, "ident": np.eye(P, dtype=f32), "ones": np.ones((P, P), f32),
            "invfreq": inv[p % 32]}


def kernel(**inputs):
    import concourse.bacc as bacc
    from concourse.bass_utils import run_bass_kernel_spmd

    a = {k: np.asarray(v) for k, v in inputs.items()}
    const = constants()
    vec = np.zeros((P, NCOLS), np.float32)

    def put(name, rows):
        at, n = COLS[name]
        vec[:rows.shape[1], at:at + n] = rows.T

    for name, v in (("norm_mix", a["norm_mix_g"]), ("hgrn", a["hgrn_norm_g"]), ("norm_x", a["norm_x_g"]),
                    ("norm_mem", a["norm_mem_g"]), ("norm_ffn", a["norm_ffn_g"]), ("final", a["final_norm_g"]),
                    ("pre0", a["pre_g_2"][0]), ("pre1", a["pre_g_2"][1]), ("post0", a["post_g_2"][0]),
                    ("post1", a["post_g_2"][1]), ("ada_b", a["ada_b_2"]),
                    ("subln", a["a_subln_g_2"]), ("qk_g", a["b_qk_g_2"]), ("lb", a["hgrn_lb_logits"])):
        put(name, v.reshape(-1, P))
    put("lam", a["a_lambda_2"].reshape(4, DA_HD))
    put("invfreq", const.pop("invfreq").reshape(1, P))

    arrays = dict(const)
    arrays["cols"] = vec
    arrays["positions"] = np.ascontiguousarray(np.broadcast_to(a["positions"].reshape(1, T), (P, T)))
    arrays["xT"], arrays["memT"] = feature_major(a["x"][0]), feature_major(a["mem"][0])
    arrays["ctxT"] = feature_major(a["ctx_2"][0])
    stages = {"br_attn": a["w_br_attn"][0], "br_hgrn": a["w_br_hgrn"][0], "w_out": a["w_out"][0], "q_x": a["wq_x"][0],
              "wo_x": a["wo_x"][0], "ffn_out": a["w_ffn_out"][0], "w_out0": a["w_out_2"][0], "w_out1": a["w_out_2"][1]}

    def cut(w, names, widths):
        at = 0
        for n, c in zip(names, widths):
            stages[n] = w[:, at:at + c]
            at += c

    cut(a["w_in"][0], ("q_a", "k_a", "v_a", "q_b", "f_b", "i_b", "og_b", "g_a", "g_b"), [D] * 9)
    cut(a["wkv_x"][0], ("k_x", "v_x"), [D] * 2)
    cut(a["w_ffn_in"][0], ("gate", "up"), [FFN] * 2)
    cut(a["a_w_in_2"][0], ("q_2", "k_2", "v_2", "z_2"), [D] * 4)
    cut(a["b_w_in_2"][0], ("q_3", "k_3", "v_3", "z_3"), [D, GQ_KV * GQ_HD, GQ_KV * GQ_HD, D])
    arrays.update({n: tiled(w) for n, w in stages.items()})
    arrays["ada"] = np.ascontiguousarray(a["ada_w_2"].transpose(0, 2, 1)).reshape(ADA_TILES, P, D)
    c_rows = np.stack([a["c_2"].reshape(D), a["c_ctx_2"].reshape(D)])
    arrays["c_rows"] = np.ascontiguousarray(np.broadcast_to(c_rows, (P, 2, D)))

    nc = bacc.Bacc("TRN2", target_bir_lowering=False, num_devices=1)
    dram = {n: nc.dram_tensor(f"in_{n}", v.shape, mybir.dt.from_np(v.dtype), kind="ExternalInput").ap()
            for n, v in arrays.items()}
    out = nc.dram_tensor("out", (P, DT, T), F32, kind="ExternalOutput").ap()
    program(nc, dram, out)
    r = run_bass_kernel_spmd(nc, [{f"in_{n}": v for n, v in arrays.items()}], core_ids=[0])
    got = r.results[0]["out"]
    return np.ascontiguousarray(got.transpose(1, 0, 2).reshape(D, T).T).reshape(1, T, D)
```
